# Optimizing a Trainium2 kernel written in Bass

```python
import jax, jax.numpy as jnp
from jax import lax
import numpy as np

D_MODEL = 1024
BATCH = 1
SEQ = 2048
DEPTH = 1

CTX_LEN = 256
GRID_W = 64
D_INNER = 2 * D_MODEL
W_POOL = D_INNER // 2
W_SSD = D_INNER - W_POOL
POOL_WINDOWS = (2, 4, 8, 16)
N_POOL_GROUPS = len(POOL_WINDOWS)
POOL_GROUP_W = W_POOL // N_POOL_GROUPS
SSD_HEADDIM = 64
SSD_HEADS = W_SSD // SSD_HEADDIM
SSD_GROUPS = 4
SSD_HEADS_PER_GROUP = SSD_HEADS // SSD_GROUPS
D_STATE = 128
D_CONV = 4
CONV_LEFT = D_CONV // 2
CHUNK = 128
N_DIR = 2
GN = SSD_GROUPS * D_STATE
CONV_DIM = W_SSD + 2 * GN
OFF_POOL_Z = W_POOL
OFF_SSD_Z = 2 * W_POOL
OFF_XBC = 2 * W_POOL + W_SSD
OFF_DT = OFF_XBC + CONV_DIM
PROJ_DIM = OFF_DT + N_DIR * SSD_HEADS
EPS = 1e-6


def rmsnorm(x, w):
    xf = x.astype(jnp.float32)
    y = xf * lax.rsqrt(jnp.mean(xf * xf, axis=-1, keepdims=True) + EPS)
    return (y * w.astype(jnp.float32)).astype(x.dtype)

def box_mean(x, window, axis):
    n = x.shape[axis]
    s = jnp.cumsum(x.astype(jnp.float32), axis=axis)
    pad = [(0, 0)] * x.ndim
    pad[axis] = (1, 0)
    s = jnp.pad(s, pad)
    t = jnp.arange(n)
    lo = jnp.clip(t - window // 2, 0, n)
    hi = jnp.clip(t + window - window // 2, 0, n)
    total = jnp.take(s, hi, axis=axis) - jnp.take(s, lo, axis=axis)
    shape = [1] * x.ndim
    shape[axis] = n
    count = (hi - lo).astype(jnp.float32).reshape(shape)
    return (total / count).astype(x.dtype)

def pool_mixer(u, w_lin, scale, grid):
    b, n, _ = u.shape
    groups = u.reshape(b, n, N_POOL_GROUPS, POOL_GROUP_W)
    outs = []
    for g, w in enumerate(POOL_WINDOWS):
        ug = groups[:, :, g]
        if grid:
            rows = n // GRID_W
            img = ug.reshape(b, rows, GRID_W, POOL_GROUP_W)
            m = box_mean(box_mean(img, w, 1), w, 2).reshape(b, n, POOL_GROUP_W)
        else:
            m = box_mean(ug, w, 1)
        outs.append(m - ug)
    d = jnp.stack(outs, axis=2)
    y = jnp.einsum('bngc,gcd->bngd', d, w_lin).reshape(b, n, W_POOL)
    return y * scale

def centred_dwconv(u, w, bias):
    n = u.shape[1]
    up = jnp.pad(u, ((0, 0), (CONV_LEFT, D_CONV - 1 - CONV_LEFT), (0, 0)))
    y = sum(up[:, k:k + n] * w[k] for k in range(D_CONV))
    return jax.nn.silu(y + bias)

def ssd_scan(x, dt, a, b_in, c_in, h0):
    bsz, n = x.shape[:2]
    nc = n // CHUNK
    G, R = SSD_GROUPS, SSD_HEADS_PER_GROUP
    xd = (x * dt[..., None]).reshape(bsz, nc, CHUNK, G, R, SSD_HEADDIM)
    adt = (dt * a).reshape(bsz, nc, CHUNK, G, R)
    bc = b_in.reshape(bsz, nc, CHUNK, G, D_STATE)
    cc = c_in.reshape(bsz, nc, CHUNK, G, D_STATE)
    acum = jnp.cumsum(adt, axis=2)
    seg = acum[:, :, :, None] - acum[:, :, None, :]
    lower = jnp.tril(jnp.ones((CHUNK, CHUNK), dtype=bool))[:, :, None, None]
    decay = jnp.exp(jnp.where(lower, seg, -jnp.inf))
    cb = jnp.einsum('bclgn,bcsgn->bclsg', cc, bc)
    y_diag = jnp.einsum('bclsg,bclsgr,bcsgrp->bclgrp', cb, decay, xd)
    decay_to_end = jnp.exp(acum[:, :, -1:] - acum)
    chunk_states = jnp.einsum('bclgn,bclgr,bclgrp->bcgrpn', bc, decay_to_end, xd)
    chunk_decay = jnp.exp(acum[:, :, -1])

    def step(h, inp):
        s_c, d_c = inp
        return h * d_c[..., None, None] + s_c, h

    h_final, h_starts = lax.scan(
        step, h0, (jnp.moveaxis(chunk_states, 1, 0), jnp.moveaxis(chunk_decay, 1, 0)))
    h_starts = jnp.moveaxis(h_starts, 0, 1)
    y_off = jnp.einsum('bclgn,bcgrpn,bclgr->bclgrp', cc, h_starts, jnp.exp(acum))
    y = (y_diag + y_off).reshape(bsz, n, SSD_HEADS, SSD_HEADDIM)
    return y, h_final

def ssd_bidir(xbc_raw, dt_raw, conv_w, conv_b, a_log, dt_bias, d_skip, h0):
    bsz, n, _ = xbc_raw.shape
    xbc = centred_dwconv(xbc_raw, conv_w, conv_b)
    xs = xbc[..., :W_SSD].reshape(bsz, n, SSD_HEADS, SSD_HEADDIM)
    bs = xbc[..., W_SSD:W_SSD + GN].reshape(bsz, n, SSD_GROUPS, D_STATE)
    cs = xbc[..., W_SSD + GN:].reshape(bsz, n, SSD_GROUPS, D_STATE)
    dt = jax.nn.softplus(dt_raw.reshape(bsz, n, N_DIR, SSD_HEADS).astype(jnp.float32)
                         + dt_bias.astype(jnp.float32))
    a = -jnp.exp(a_log.astype(jnp.float32))
    flip = lambda t: jnp.flip(t, axis=1)
    y_f, h_f = ssd_scan(xs, dt[:, :, 0], a[0], bs, cs, h0[0])
    y_b, h_b = ssd_scan(flip(xs), flip(dt[:, :, 1]), a[1], flip(bs), flip(cs), h0[1])
    y = y_f + flip(y_b) + d_skip[:, None] * xs
    return y.reshape(bsz, n, W_SSD).astype(xbc_raw.dtype), jnp.stack([h_f, h_b])

def modulated_projection(h, norm_w, shift, scale, w_in):
    hm = rmsnorm(h, norm_w) * (1.0 + scale) + shift
    return hm @ w_in

def mixer_output(p, y_ssd, grid, pool_w, pool_scale, ssd_norm_w, w_out):
    bsz, n, _ = p.shape
    u_pool = p[..., :W_POOL]
    z_pool = p[..., OFF_POOL_Z:OFF_SSD_Z]
    z_ssd = p[..., OFF_SSD_Z:OFF_XBC]
    y_pool = pool_mixer(u_pool, pool_w, pool_scale, grid) * jax.nn.silu(z_pool)
    gated = (y_ssd * jax.nn.silu(z_ssd)).reshape(bsz, n, SSD_GROUPS, W_SSD // SSD_GROUPS)
    y_s = rmsnorm(gated, ssd_norm_w.reshape(SSD_GROUPS, W_SSD // SSD_GROUPS)).reshape(bsz, n, W_SSD)
    return jnp.concatenate([y_pool, y_s], axis=-1) @ w_out

def first_inputs(seed: int = 0) -> dict:
    key = jax.random.key(seed)
    ks = jax.random.split(key, 20)
    nrm = jax.random.normal
    x = nrm(ks[0], (BATCH, SEQ, D_MODEL), jnp.float32)
    c = nrm(ks[1], (BATCH, D_MODEL), jnp.float32)
    ctx = nrm(ks[2], (BATCH, CTX_LEN, D_MODEL), jnp.float32)
    c_ctx = nrm(ks[3], (D_MODEL,), jnp.float32)
    norm_w = 1.0 + 0.02 * nrm(ks[4], (DEPTH, D_MODEL), jnp.float32)
    w_ada = 0.5 * D_MODEL ** -0.5 * nrm(ks[5], (DEPTH, D_MODEL, 3 * D_MODEL), jnp.float32)
    b_ada = 0.02 * nrm(ks[6], (DEPTH, 3 * D_MODEL), jnp.float32)
    w_in = D_MODEL ** -0.5 * nrm(ks[7], (DEPTH, D_MODEL, PROJ_DIM), jnp.float32)
    conv_w = D_CONV ** -0.5 * nrm(ks[8], (DEPTH, D_CONV, CONV_DIM), jnp.float32)
    conv_b = 0.02 * nrm(ks[9], (DEPTH, CONV_DIM), jnp.float32)
    a_log = jnp.log(jax.random.uniform(ks[10], (DEPTH, N_DIR, SSD_HEADS), jnp.float32, 1.0, 16.0))
    dt0 = jnp.exp(jax.random.uniform(ks[11], (DEPTH, N_DIR, SSD_HEADS), jnp.float32,
                                     float(np.log(1e-3)), float(np.log(1e-1))))
    dt_bias = dt0 + jnp.log(-jnp.expm1(-dt0))
    d_skip = 1.0 + 0.02 * nrm(ks[12], (DEPTH, SSD_HEADS), jnp.float32)
    ssd_norm_w = 1.0 + 0.02 * nrm(ks[13], (DEPTH, W_SSD), jnp.float32)
    pool_w = POOL_GROUP_W ** -0.5 * nrm(ks[14], (DEPTH, N_POOL_GROUPS, POOL_GROUP_W, POOL_GROUP_W), jnp.float32)
    pool_scale = 1.0 + 0.02 * nrm(ks[15], (DEPTH, W_POOL), jnp.float32)
    w_out = D_INNER ** -0.5 * nrm(ks[16], (DEPTH, D_INNER, D_MODEL), jnp.float32)
    final_norm_w = 1.0 + 0.02 * nrm(ks[17], (D_MODEL,), jnp.float32)
    return {"x": x, "c": c, "ctx": ctx, "c_ctx": c_ctx, "norm_w": norm_w,
            "w_ada": w_ada, "b_ada": b_ada, "w_in": w_in, "conv_w": conv_w,
            "conv_b": conv_b, "a_log": a_log, "dt_bias": dt_bias, "d_skip": d_skip,
            "ssd_norm_w": ssd_norm_w, "pool_w": pool_w, "pool_scale": pool_scale,
            "w_out": w_out, "final_norm_w": final_norm_w}

def first_block(x, c, ctx, c_ctx, norm_w, w_ada, b_ada, w_in, conv_w, conv_b, a_log,
              dt_bias, d_skip, ssd_norm_w, pool_w, pool_scale, w_out, final_norm_w):
    bsz = x.shape[0]
    h_lat, h_ctx = x, ctx
    for i in range(DEPTH):
        mod_lat = jax.nn.silu(c) @ w_ada[i] + b_ada[i]
        mod_ctx = jax.nn.silu(c_ctx) @ w_ada[i] + b_ada[i]
        sh_l, sc_l, g_l = jnp.split(mod_lat[:, None, :], 3, axis=-1)
        sh_c, sc_c, g_c = jnp.split(mod_ctx, 3, axis=-1)

        p_ctx = modulated_projection(h_ctx, norm_w[i], sh_c, sc_c, w_in[i])
        h0 = jnp.zeros((N_DIR, bsz, SSD_GROUPS, SSD_HEADS_PER_GROUP, SSD_HEADDIM, D_STATE), jnp.float32)
        y_ssd_ctx, h_ctx_end = ssd_bidir(p_ctx[..., OFF_XBC:OFF_DT], p_ctx[..., OFF_DT:],
                                         conv_w[i], conv_b[i], a_log[i], dt_bias[i], d_skip[i], h0)

        p_lat = modulated_projection(h_lat, norm_w[i], sh_l, sc_l, w_in[i])
        y_ssd_lat, _ = ssd_bidir(p_lat[..., OFF_XBC:OFF_DT], p_lat[..., OFF_DT:],
                                 conv_w[i], conv_b[i], a_log[i], dt_bias[i], d_skip[i], h_ctx_end)
        h_lat = h_lat + g_l * mixer_output(p_lat, y_ssd_lat, True, pool_w[i], pool_scale[i],
                                           ssd_norm_w[i], w_out[i])
        if i < DEPTH - 1:
            h_ctx = h_ctx + g_c * mixer_output(p_ctx, y_ssd_ctx, False, pool_w[i], pool_scale[i],
                                               ssd_norm_w[i], w_out[i])
    return rmsnorm(h_lat, final_norm_w)


_first_inputs = first_inputs


def first_inputs(seed=0):
    import zlib

    import numpy as np

    out = dict(_first_inputs(seed))
    spreads = {}
    factors = {'ctx': 64.0,
     'c_ctx': 64.0,
     'norm_w': 8.0,
     'b_ada': 2.937,
     'conv_b': 64.0,
     'd_skip': 64.0,
     'ssd_norm_w': 64.0,
     'pool_scale': 23.018,
     'final_norm_w': 8.352,
     'conv_w': 3.286,
     'a_log': 8.0,
     'dt_bias': 8.0}
    for name, (base, spread) in spreads.items():
        noise = np.random.default_rng([zlib.crc32(name.encode()), seed]).standard_normal(out[name].shape)
        drawn = base * np.exp(spread * noise) if base else spread * noise
        out[name] = __import__('jax').numpy.asarray(drawn.astype(out[name].dtype))
    for name, factor in factors.items():
        out[name] = (out[name] * factor).astype(out[name].dtype)
    return out


_narrow_inputs = first_inputs


def first_inputs(seed=0):

    out = dict(_narrow_inputs(seed))
    wider = {'conv_b': 12.0,
     'd_skip': 12.0,
     'ssd_norm_w': 12.0,
     'pool_scale': 3.24,
     'final_norm_w': 3.27}
    for name, times in wider.items():
        mean = out[name].mean()
        out[name] = (mean + times * (out[name] - mean)).astype(out[name].dtype)
    return out


CHUNK_2 = 64
D_MIX = D_MODEL
D_LRU = D_MIX // 2
D_ATTN = D_MIX - D_LRU
HEAD_DIM = 64
N_ATTN_HEADS = D_ATTN // HEAD_DIM
LRU_BLOCKS = 8
LRU_BLOCK_W = D_LRU // LRU_BLOCKS
CONV_W = 4
LRU_C = 8.0
Q_BLOCK = 128
N_IN = 2 * D_LRU + 4 * D_ATTN + N_ATTN_HEADS
DEEPNORM_ALPHA = (2.0 * DEPTH) ** 0.25
DEEPNORM_BETA = (8.0 * DEPTH) ** -0.25
LN_EPS = 1e-5
NEG_INF = -1e30


def _layer_norm(x):
    x32 = x.astype(jnp.float32)
    mu = jnp.mean(x32, axis=-1, keepdims=True)
    var = jnp.mean(jnp.square(x32 - mu), axis=-1, keepdims=True)
    return (x32 - mu) * lax.rsqrt(var + LN_EPS)

def _rms_norm(y, g):
    y32 = y.astype(jnp.float32)
    return y32 * lax.rsqrt(jnp.mean(jnp.square(y32), axis=-1, keepdims=True) + LN_EPS) * g.astype(jnp.float32)

def _causal_depthwise_conv(x, w, b):
    K = w.shape[0]
    S = x.shape[1]
    xp = jnp.pad(x, ((0, 0), (K - 1, 0), (0, 0)))
    out = b
    for k in range(K):
        out = out + xp[:, k:k + S, :] * w[k]
    return out

def _rg_lru(x, w_a, b_a, w_x, b_x, lam):
    B, S, C = x.shape
    xb = x.reshape(B, S, LRU_BLOCKS, LRU_BLOCK_W)
    r = jax.nn.sigmoid((jnp.einsum('bsnd,nde->bsne', xb, w_a).reshape(B, S, C) + b_a).astype(jnp.float32))
    i = jax.nn.sigmoid((jnp.einsum('bsnd,nde->bsne', xb, w_x).reshape(B, S, C) + b_x).astype(jnp.float32))
    log_a = -LRU_C * r * jax.nn.softplus(-lam.astype(jnp.float32))
    a = jnp.exp(log_a)
    mult = jnp.sqrt(-jnp.expm1(2.0 * log_a))
    u = mult * (i * x.astype(jnp.float32))

    def combine(left, right):
        a1, b1 = left
        a2, b2 = right
        return a2 * a1, a2 * b1 + b2

    _, h = lax.associative_scan(combine, (a, u), axis=1)
    return h

def _forgetting_attention(q, k, v, log_f):
    B, S, _ = q.shape
    H, dh = N_ATTN_HEADS, HEAD_DIM
    q = q.reshape(B, S, H, dh).transpose(0, 2, 1, 3)
    k = k.reshape(B, S, H, dh).transpose(0, 2, 1, 3)
    v = v.reshape(B, S, H, dh).transpose(0, 2, 1, 3)
    d_cum = jnp.cumsum(log_f.astype(jnp.float32), axis=1).transpose(0, 2, 1)
    scale = dh ** -0.5
    kpos = jnp.arange(S)
    n_blocks = S // Q_BLOCK

    def block(bi):
        qs = bi * Q_BLOCK
        qb = lax.dynamic_slice_in_dim(q, qs, Q_BLOCK, axis=2)
        dq = lax.dynamic_slice_in_dim(d_cum, qs, Q_BLOCK, axis=2)
        s = jnp.einsum('bhqd,bhkd->bhqk', qb, k).astype(jnp.float32) * scale
        s = s + (dq[..., :, None] - d_cum[:, :, None, :])
        qpos = qs + jnp.arange(Q_BLOCK)
        mask = kpos[None, :] <= qpos[:, None]
        s = jnp.where(mask, s, NEG_INF)
        p = jax.nn.softmax(s, axis=-1)
        return jnp.einsum('bhqk,bhkd->bhqd', p.astype(v.dtype), v)

    out = lax.map(block, jnp.arange(n_blocks))
    return out.transpose(1, 0, 3, 2, 4).reshape(B, S, H * dh)

def second_inputs(seed: int = 0) -> dict:
    key = jax.random.key(seed)
    ks = jax.random.split(key, 18)
    f32 = jnp.float32
    x = jax.random.normal(ks[0], (BATCH, SEQ, D_MODEL), f32)
    c = jax.random.normal(ks[1], (BATCH, D_MODEL), f32)
    w_ada = jax.random.normal(ks[2], (DEPTH, D_MODEL, 3 * D_MODEL), f32) * (0.5 * D_MODEL ** -0.5)
    b_ada = 0.01 * jax.random.normal(ks[3], (DEPTH, 3 * D_MODEL), f32)
    w_in = jax.random.normal(ks[4], (DEPTH, D_MODEL, N_IN), f32) * D_MODEL ** -0.5
    b_fgate = jax.random.uniform(ks[5], (DEPTH, N_ATTN_HEADS), f32, minval=1.0, maxval=5.0)
    conv_w = jax.random.normal(ks[6], (DEPTH, CONV_W, D_LRU), f32) * CONV_W ** -0.5
    conv_b = 0.01 * jax.random.normal(ks[7], (DEPTH, D_LRU), f32)
    w_gate_a = jax.random.normal(ks[8], (DEPTH, LRU_BLOCKS, LRU_BLOCK_W, LRU_BLOCK_W), f32) * LRU_BLOCK_W ** -0.5
    b_gate_a = 0.01 * jax.random.normal(ks[9], (DEPTH, D_LRU), f32)
    w_gate_x = jax.random.normal(ks[10], (DEPTH, LRU_BLOCKS, LRU_BLOCK_W, LRU_BLOCK_W), f32) * LRU_BLOCK_W ** -0.5
    b_gate_x = 0.01 * jax.random.normal(ks[11], (DEPTH, D_LRU), f32)
    u = jax.random.uniform(ks[12], (DEPTH, D_LRU), f32, minval=0.9, maxval=0.999)
    a0 = u ** (1.0 / LRU_C)
    lru_lambda = jnp.log(a0) - jnp.log1p(-a0)
    norm_lru = 1.0 + 0.01 * jax.random.normal(ks[13], (DEPTH, D_LRU), f32)
    norm_attn = 1.0 + 0.01 * jax.random.normal(ks[14], (DEPTH, D_ATTN), f32)
    w_out = jax.random.normal(ks[15], (DEPTH, D_MIX, D_MODEL), f32) * (D_MIX ** -0.5 * DEEPNORM_BETA)
    ln_gain = 1.0 + 0.01 * jax.random.normal(ks[16], (DEPTH, D_MODEL), f32)
    ln_bias = 0.01 * jax.random.normal(ks[17], (DEPTH, D_MODEL), f32)
    return {"x": x, "c": c, "w_ada": w_ada, "b_ada": b_ada, "w_in": w_in, "b_fgate": b_fgate,
            "conv_w": conv_w, "conv_b": conv_b, "w_gate_a": w_gate_a, "b_gate_a": b_gate_a,
            "w_gate_x": w_gate_x, "b_gate_x": b_gate_x, "lru_lambda": lru_lambda,
            "norm_lru": norm_lru, "norm_attn": norm_attn, "w_out": w_out,
            "ln_gain": ln_gain, "ln_bias": ln_bias}

def second_block(x, c, w_ada, b_ada, w_in, b_fgate, conv_w, conv_b, w_gate_a, b_gate_a,
              w_gate_x, b_gate_x, lru_lambda, norm_lru, norm_attn, w_out, ln_gain, ln_bias):
    dtype = x.dtype
    split_idx = [D_LRU, 2 * D_LRU, 2 * D_LRU + D_ATTN, 2 * D_LRU + 2 * D_ATTN,
                 2 * D_LRU + 3 * D_ATTN, 2 * D_LRU + 4 * D_ATTN]
    c_act = jax.nn.silu(c)
    for l in range(DEPTH):
        mod = c_act @ w_ada[l] + b_ada[l]
        shift, scale, gate = jnp.split(mod, 3, axis=-1)
        h = (_layer_norm(x) * (1.0 + scale[:, None, :].astype(jnp.float32))
             + shift[:, None, :].astype(jnp.float32)).astype(dtype)
        proj = h @ w_in[l]
        xr, zr, q, k, v, za, fl = jnp.split(proj, split_idx, axis=-1)
        xc = _causal_depthwise_conv(xr, conv_w[l], conv_b[l])
        y_r = _rg_lru(xc, w_gate_a[l], b_gate_a[l], w_gate_x[l], b_gate_x[l], lru_lambda[l])
        y_r = (_rms_norm(y_r, norm_lru[l]) * jax.nn.silu(zr.astype(jnp.float32))).astype(dtype)
        log_f = jax.nn.log_sigmoid((fl + b_fgate[l]).astype(jnp.float32))
        y_a = _forgetting_attention(q, k, v, log_f)
        y_a = (_rms_norm(y_a, norm_attn[l]) * jax.nn.silu(za.astype(jnp.float32))).astype(dtype)
        y = jnp.concatenate([y_r, y_a], axis=-1) @ w_out[l]
        res = DEEPNORM_ALPHA * x.astype(jnp.float32) + gate[:, None, :].astype(jnp.float32) * y.astype(jnp.float32)
        x = (_layer_norm(res) * ln_gain[l].astype(jnp.float32) + ln_bias[l].astype(jnp.float32)).astype(dtype)
    return x


_first_inputs_2 = second_inputs


def second_inputs(seed=0):
    import zlib

    import numpy as np

    out = dict(_first_inputs_2(seed))
    spreads = {}
    factors = {'b_ada': 8.0,
     'conv_b': 8.0,
     'w_gate_a': 5.115,
     'b_gate_a': 64.0,
     'w_gate_x': 2.875,
     'b_gate_x': 47.139,
     'norm_lru': 64.0,
     'norm_attn': 64.0,
     'ln_gain': 33.596,
     'ln_bias': 32.874}
    for name, (base, spread) in spreads.items():
        noise = np.random.default_rng([zlib.crc32(name.encode()), seed]).standard_normal(out[name].shape)
        drawn = base * np.exp(spread * noise) if base else spread * noise
        out[name] = __import__('jax').numpy.asarray(drawn.astype(out[name].dtype))
    for name, factor in factors.items():
        out[name] = (out[name] * factor).astype(out[name].dtype)
    return out


_narrow_inputs_2 = second_inputs


def second_inputs(seed=0):

    out = dict(_narrow_inputs_2(seed))
    wider = {'norm_lru': 9.52, 'norm_attn': 9.99, 'ln_gain': 6.86, 'ln_bias': 6.6}
    for name, times in wider.items():
        mean = out[name].mean()
        out[name] = (mean + times * (out[name] - mean)).astype(out[name].dtype)
    return out


def setup_inputs(seed=0):
    out = dict(first_inputs(seed))
    for name, value in second_inputs(seed + 1).items():
        if name != "x":
            out[name + "_2"] = value
    return out


def reference(
    x, c, ctx, c_ctx, norm_w, w_ada, b_ada, w_in, conv_w, conv_b, a_log, dt_bias, d_skip,
    ssd_norm_w, pool_w, pool_scale, w_out, final_norm_w, c_2, w_ada_2, b_ada_2, w_in_2,
    b_fgate_2, conv_w_2, conv_b_2, w_gate_a_2, b_gate_a_2, w_gate_x_2, b_gate_x_2, lru_lambda_2,
    norm_lru_2, norm_attn_2, w_out_2, ln_gain_2, ln_bias_2,
):
    x = first_block(
        x, c, ctx, c_ctx, norm_w, w_ada, b_ada, w_in, conv_w, conv_b, a_log, dt_bias, d_skip,
        ssd_norm_w, pool_w, pool_scale, w_out, final_norm_w,
    )
    return second_block(
        x, c_2, w_ada_2, b_ada_2, w_in_2, b_fgate_2, conv_w_2, conv_b_2, w_gate_a_2, b_gate_a_2,
        w_gate_x_2, b_gate_x_2, lru_lambda_2, norm_lru_2, norm_attn_2, w_out_2, ln_gain_2,
        ln_bias_2,
    )


_drawn_inputs = setup_inputs


def setup_inputs(seed=0):
    import zlib

    import numpy as np

    out = dict(_drawn_inputs(seed))
    spreads = {}
    factors = {'conv_b': 8.0, 'd_skip': 8.0, 'ssd_norm_w': 2.71, 'b_gate_a_2': 3.339}
    for name, (base, spread) in spreads.items():
        noise = np.random.default_rng([zlib.crc32(name.encode()), seed]).standard_normal(out[name].shape)
        drawn = base * np.exp(spread * noise) if base else spread * noise
        out[name] = __import__('jax').numpy.asarray(drawn.astype(out[name].dtype))
    for name, factor in factors.items():
        out[name] = (out[name] * factor).astype(out[name].dtype)
    return out
```

```python
from contextlib import ExitStack, contextmanager

import numpy as np

import concourse.bass as bass
from concourse import mybir

ALU = mybir.AluOpType
ACT = mybir.ActivationFunctionType
AX_X = mybir.AxisListType.X
F32 = mybir.dt.float32
F32R = mybir.dt.float32r

P = 128
D = 1024
KT = D // P
SEQ, CTX = 2048, 256
TOK = SEQ + CTX
LT, CT = SEQ // P, CTX // P
TT = LT + CT
CH = 512
NCH = SEQ // CH
EPS = 1e-6

W_HALF = 1024
HEADS, GROUPS, HPG, HD, NS = 16, 4, 4, 64, 128
NDH = 2 * HEADS
WINDOWS = (2, 4, 8, 16)
GRID_R, GRID_C = 32, 64
XS0, B0, C0, DT0, ZS0, ZP0, U0, NBLK = 0, 8, 12, 16, 17, 25, 33, 41

V_BADA, V_NORM, V_CONVB, V_CONVW, V_PSCALE, V_SNORM = 0, 24, 32, 48, 112, 120
V2_BADA, V2_CONVW, V2_CONVB, V2_BA, V2_BX, V2_LAM, V2_NLRU, V2_NATT = 0, 24, 40, 44, 48, 52, 56, 60

XR0, ZR0, QK0, VZ0, FL0, NBLK2 = 0, 4, 8, 16, 24, 25
NH2, HD2 = 8, 64
W2 = NH2 * HD2
LRU_C = 8.0
ALPHA = 2.0 ** 0.25
LN_EPS = 1e-5


class Tally:

    def __init__(self, sem):
        self.sem, self.base, self.local = sem, 0, 0

    @property
    def value(self):
        return self.base + self.local

    def mark(self, ins):
        ins.then_inc(self.sem, 1)
        self.local += 1
        return ins

    @contextmanager
    def turn(self, i, per, turns):
        before = self.base + self.local
        self.base, self.local = before + i * per, 0
        yield
        assert self.local == per, (self.local, per)
        self.base, self.local = before + per * turns, 0


class Names:
    pass


class Kit:

    def __init__(self, nc):
        self.nc, self.in_use = nc, []

    def sbuf(self, ctx, name, shape, dt=F32):
        return ctx.enter_context(self.nc.sbuf_tensor(name, shape, dt))

    def psum(self, ctx, name, shape):
        return ctx.enter_context(self.nc.psum_tensor(name, shape, F32))

    def sem(self, name):
        self.in_use.append(self.nc.alloc_semaphore(name))
        return self.in_use[-1]

    def end_phase(self):
        self.nc.all_engine_barrier()
        self.nc.clear_and_free_semaphores(self.in_use)
        self.in_use = []
        self.nc.all_engine_barrier()

    def sems(self, prefix, names):
        return {n: self.sem(prefix + n) for n in names}


def modulation(nc, kit, a, s, hmT):
    hm_hi, hm_lo = hmT
    with ExitStack() as ctx:
        sb = lambda *args: kit.sbuf(ctx, *args)
        ps = lambda *args: kit.psum(ctx, *args)
        WC = 256
        wada = [sb(f"wada{n}", [P, KT, WC]) for n in range(2)]
        c3 = sb("c3", [P, KT, 3])
        sc3 = sb("silu_c3", [P, KT, 3])
        cbc = sb("c_bcast", [P, 2, KT, P])
        xt = [sb(f"xt{n}", [P, D]) for n in range(2)]
        xn = [sb(f"xn{n}", [P, D]) for n in range(2)]
        full = [sb(f"hm_full{n}", [P, KT, P]) for n in range(2)]
        stat = sb("hm_stat", [P, 4, 2])
        mA = sb("mod_scale", [P, 2, KT])
        mS = sb("mod_shift", [P, 2, KT])
        brow = [sb(f"b_gate_row{n}", [P, WC]) for n in range(2)]
        grow = [sb(f"gate_row{n}", [P, WC]) for n in range(2)]
        psC = ps("ps_modcols", [P, 32, 4])
        psT = [ps(f"ps_hmT{n}", [P, KT, P]) for n in range(2)]
        psJ = ps("ps_square", [P, D])
        psR = [psJ[:, n * CH:n * CH + WC] for n in range(2)]

        k = kit
        tabs = k.sem("a_tables_loaded")
        w_in = [k.sem(f"a_wada_loaded{n}") for n in range(2)]
        w_free = k.sem("a_wada_used")
        silu_ok = k.sem("a_silu_ready")
        bc_ok = k.sem("a_cbcast_ready")
        cols_ok = k.sem("a_modcols_ready")
        mod_ok = k.sem("a_mod_ready")
        x_in = [k.sem(f"a_x_loaded{n}") for n in range(2)]
        sq_ok = k.sem("a_square_done")
        root_ok = k.sem("a_root_done")
        xn_ok = k.sem("a_xn_ready")
        tr_ok = k.sem("a_transposed")
        full_a = k.sem("a_full_by_act")
        full_v = k.sem("a_full_by_dve")
        hi_ok = k.sem("a_hi_done")
        lo_ok = k.sem("a_lo_done")
        br_in = [k.sem(f"a_brow_loaded{n}") for n in range(2)]
        row_ok = k.sem("a_gate_row_summed")
        grow_ok = k.sem("a_gate_row_ready")
        g_out = [k.sem(f"a_gate_row_stored{n}") for n in range(2)]
        dve = Tally(k.sem("a_dve_chain"))

        with nc.Block() as block:
            @block.sync
            def _(sp):
                sp.dma_start(c3[:], a["c3"]).then_inc(tabs, 16)

                def load_w(c, n, first=False):
                    if not first:
                        sp.wait_ge(w_free, c - 1)
                    sp.dma_start(wada[n][:], a["wada"][c]).then_inc(w_in[n], 16)

                def load_x(t, n, src, first=False):
                    if not first:
                        sp.wait_ge(xn_ok, t - 1)
                    sp.dma_start(xt[n][:], src).then_inc(x_in[n], 16)

                load_w(0, 0, True)
                load_w(1, 1, True)
                load_x(0, 0, a["x"][0:P, :], True)
                load_x(1, 1, a["x"][P:2 * P, :], True)
                with sp.Fori(1, 4) as i:
                    for n in range(2):
                        load_w(2 * i + n, n)
                with sp.Fori(1, LT // 2) as i:
                    for n in range(2):
                        load_x(2 * i + n, n, a["x"][bass.ds((2 * i + n) * P, P), :])
                for n in range(2):
                    load_x(LT + n, n, a["ctx"][n * P:(n + 1) * P, :])
                with sp.Fori(4, 8) as i:
                    for n in range(2):
                        load_w(2 * i + n, n)
                for r in range(8):
                    n = r % 2
                    if r < 2:
                        load_w(16 + r, n)
                    else:
                        sp.wait_ge(row_ok, r - 1)
                        sp.dma_start(wada[n][:], a["wada"][16 + r]).then_inc(w_in[n], 16)
                        sp.wait_ge(grow_ok, r - 1)
                    sp.dma_start(brow[n][:], a["gate_bias"][r:r + 1, :].partition_broadcast(P)).then_inc(br_in[n], 16)

            @block.scalar
            def _(act):
                act.wait_ge(tabs, 16)
                act.activation(sc3[:], c3[:], ACT.Silu).then_inc(silu_ok, 1)

                def norm(t, half, n, first):
                    act.wait_ge(x_in[n], 16 * (half + 1))
                    if not first:
                        act.wait_ge(xn_ok, t - 1)
                    act.activation(psJ[:], xt[n][:], ACT.Square, accum_out=stat[:, 0, n:n + 1]).then_inc(sq_ok, 1)
                    act.wait_ge(sq_ok, t + 1)
                    act.activation(stat[:, 1, n:n + 1], stat[:, 0, n:n + 1], ACT.Sqrt, scale=1.0 / D,
                                   bias=s.eps[:, 0:1]).then_inc(root_ok, 1)

                def affine(t, n, which, first):
                    act.wait_ge(tr_ok, t + 1)
                    if not first:
                        act.wait_ge(lo_ok, t - 1)
                        act.wait_ge(hi_ok, t - 1)
                    for q in range(KT // 2):
                        ins = act.activation(full[n][:, q, :], psT[n][:, q, :], ACT.Identity,
                                             scale=mA[:, which, q:q + 1], bias=mS[:, which, q:q + 1])
                    ins.then_inc(full_a, 1)

                norm(0, 0, 0, True)
                norm(1, 0, 1, True)
                act.wait_ge(mod_ok, 2)
                affine(0, 0, 0, True)
                norm(2, 1, 0, False)
                affine(1, 1, 0, True)
                norm(3, 1, 1, False)
                with act.Fori(1, LT // 2 - 1) as i:
                    for n in range(2):
                        affine(2 * i + n, n, 0, False)
                        norm(2 * i + n + 2, i + 1, n, False)
                for n in range(2):
                    affine(LT - 2 + n, n, 0, False)
                    norm(LT + n, LT // 2, n, False)
                for n in range(2):
                    affine(LT + n, n, 1, False)

            @block.vector
            def _(v):
                v.wait_ge(silu_ok, 1)
                for w, cc in enumerate((0, 2)):
                    ins = v.tensor_copy(cbc[:, w], sc3[:, :, cc].unsqueeze(2).to_broadcast([P, KT, P]))
                ins.then_inc(bc_ok, 1)

                def xnorm(t, n, first):
                    v.wait_ge(root_ok, t + 1)
                    dve.mark(v.reciprocal(stat[:, 2, n:n + 1], stat[:, 1, n:n + 1]))
                    v.wait_ge(dve.sem, dve.value)
                    if not first:
                        v.wait_ge(tr_ok, t - 1)
                    v.tensor_scalar(xn[n][:], xt[n][:], stat[:, 2, n:n + 1], None, ALU.mult).then_inc(xn_ok, 1)

                def affine(t, n, which, first):
                    v.wait_ge(tr_ok, t + 1)
                    if not first:
                        v.wait_ge(hi_ok, t - 1)
                    for q in range(KT // 2, KT):
                        ins = v.tensor_scalar(full[n][:, q, :], psT[n][:, q, :], mA[:, which, q:q + 1],
                                              mS[:, which, q:q + 1], ALU.mult, ALU.add)
                    ins.then_inc(full_v, 1)

                def low(t, n, cols):
                    v.wait_ge(hi_ok, t + 1)
                    v.tensor_tensor(hm_lo[:, :, cols], full[n][:], hm_hi[:, :, cols].bitcast(F32),
                                    ALU.subtract).then_inc(lo_ok, 1)

                xnorm(0, 0, True)
                xnorm(1, 1, True)
                v.wait_ge(cols_ok, 1)
                for w in range(2):
                    dve.mark(v.tensor_tensor(mS[:, w, :], psC[:, 0:KT, w], s.cols1[:, V_BADA:V_BADA + KT], ALU.add))
                    dve.mark(v.tensor_tensor(mA[:, w, :], psC[:, KT:2 * KT, w],
                                             s.cols1[:, V_BADA + KT:V_BADA + 2 * KT], ALU.add))
                    v.wait_ge(dve.sem, dve.value)
                    v.scalar_tensor_tensor(mA[:, w, :], mA[:, w, :], 1.0, s.cols1[:, V_NORM:V_NORM + KT],
                                           ALU.add, ALU.mult).then_inc(mod_ok, 1)
                v.wait_ge(mod_ok, 2)

                def cols_of(t):
                    return slice(t * P, (t + 1) * P) if isinstance(t, int) else bass.ds(t * P, P)

                affine(0, 0, 0, True)
                xnorm(2, 0, False)
                low(0, 0, cols_of(0))
                affine(1, 1, 0, True)
                xnorm(3, 1, False)
                low(1, 1, cols_of(1))
                with v.Fori(1, LT // 2 - 1) as i:
                    with dve.turn(i - 1, 2, LT // 2 - 2):
                        for n in range(2):
                            t = 2 * i + n
                            affine(t, n, 0, False)
                            xnorm(t + 2, n, False)
                            low(t, n, cols_of(t))
                for n in range(2):
                    affine(LT - 2 + n, n, 0, False)
                    xnorm(LT + n, n, False)
                    low(LT - 2 + n, n, cols_of(LT - 2 + n))
                for n in range(2):
                    affine(LT + n, n, 1, False)
                    low(LT + n, n, cols_of(LT + n))
                v.wait_ge(cols_ok, 2)
                v.tensor_tensor(s.mod2[:, 0, :], psC[:, 2 * KT:3 * KT, 2], s.cols2[:, V2_BADA:V2_BADA + KT], ALU.add)
                dve.mark(v.tensor_tensor(s.mod2[:, 1, :], psC[:, 3 * KT:4 * KT, 2],
                                         s.cols2[:, V2_BADA + KT:V2_BADA + 2 * KT], ALU.add))
                v.wait_ge(dve.sem, dve.value)
                v.tensor_scalar(s.mod2[:, 1, :], s.mod2[:, 1, :], 1.0, None, ALU.add)
                for r in range(8):
                    n = r % 2
                    v.wait_ge(row_ok, r + 1)
                    v.wait_ge(br_in[n], 16 * (r // 2 + 1))
                    if r >= 2:
                        v.wait_ge(g_out[n], 16 * (r // 2))
                    v.tensor_tensor(grow[n][:], psR[n], brow[n][:], ALU.add).then_inc(grow_ok, 1)

            @block.gpsimd
            def _(g):
                def high(t, n, cols):
                    g.wait_ge(full_a, t + 1)
                    g.wait_ge(full_v, t + 1)
                    g.tensor_copy(hm_hi[:, :, cols], full[n][:]).then_inc(hi_ok, 1)

                with g.Fori(0, TT // 2) as i:
                    for n in range(2):
                        t = 2 * i + n
                        high(t, n, bass.ds(t * P, P))
                for r in range(8):
                    g.wait_ge(grow_ok, r + 1)
                    g.dma_start(a["gate_rows"][:, r * WC:(r + 1) * WC], grow[r % 2][:]).then_inc(g_out[r % 2], 16)
                for n in range(2):
                    g.wait_ge(g_out[n], 64)

            @block.tensor
            def _(pe):
                def mod_cols(c, half, n):
                    pe.wait_ge(w_in[n], 16 * (half + 1))
                    for m in range(2):
                        for q in range(KT):
                            mm = pe.matmul(psC[:, 2 * c + m, 0:3], wada[n][:, q, m * P:(m + 1) * P], sc3[:, q, :],
                                           start=(q == 0), stop=(q == KT - 1))
                    mm.then_inc(w_free, 1)
                    return mm

                def transposes(t, n, first):
                    pe.wait_ge(xn_ok, t + 1)
                    if not first:
                        pe.wait_ge(full_a, t - 1)
                        pe.wait_ge(full_v, t - 1)
                    for q in range(KT):
                        mm = pe.transpose(psT[n][:, q, :], xn[n][:, q * P:(q + 1) * P], s.ident[:])
                    mm.then_inc(tr_ok, 1)

                pe.wait_ge(silu_ok, 1)
                with pe.Fori(0, 4) as i:
                    for n in range(2):
                        mod_cols(2 * i + n, i, n)
                pe.transpose(psT[0][:, 0, :], s.ident[:], s.ident[:]).then_inc(cols_ok, 1)
                transposes(0, 0, True)
                transposes(1, 1, True)
                with pe.Fori(1, TT // 2) as i:
                    for n in range(2):
                        transposes(2 * i + n, n, False)
                with pe.Fori(4, 8) as i:
                    for n in range(2):
                        mod_cols(2 * i + n, i, n)
                pe.wait_ge(full_a, TT)
                pe.wait_ge(full_v, TT)
                pe.transpose(psT[0][:, 0, :], s.ident[:], s.ident[:]).then_inc(cols_ok, 1)
                pe.wait_ge(bc_ok, 1)
                def gate_row(r, w, half, n, first):
                    pe.wait_ge(w_in[n], 16 * (half + 1))
                    if not first:
                        pe.wait_ge(grow_ok, r - 1)
                    for q in range(KT):
                        mm = pe.matmul(psR[n], cbc[:, w, q, :], wada[n][:, q, :],
                                       start=(q == 0), stop=(q == KT - 1))
                    mm.then_inc(row_ok, 1)

                for r in range(4):
                    gate_row(r, 0, 8 + r // 2, r % 2, r < 2)
                for r in range(4, 8):
                    gate_row(r, 1, 8 + r // 2, r % 2, False)


class Kind:

    def __init__(self, first, count, chunks, how, turned=None, stored=None, func=ACT.Identity, scale=1.0, width=P):
        self.first, self.count, self.chunks, self.how = first, count, chunks, how
        self.turned, self.stored, self.func, self.scale, self.width = turned, stored, func, scale, width
        self.groups = chunks if turned is not None else 0


class Where:

    def __init__(self, b0, i=None, turns=1):
        self.b0, self.i, self.turns = b0, i, turns

    def num(self, back=0):
        b = self.b0 - back
        return b if self.i is None else b + 2 * self.i

    def at(self, table, d=0):
        first = table[self.b0 + d]
        if self.i is None:
            return first
        rate = table[self.b0 + d + 2] - first
        for k in range(self.turns):
            assert table[self.b0 + d + 2 * k] == first + rate * k, (self.b0, d, k)
        return first + rate * self.i


RAW_W = 2 + SEQ + 3 + CTX + 1
CTX_AT = SEQ + 3


def project(nc, kit, a, s, name, kinds, plan, xT, w_dram, conv, has_ctx):
    x_hi, x_lo = xT
    kind_of = [k for k in kinds for _ in range(k.count)]
    NB = len(kind_of)
    zero = [0]
    def table(f):
        out = [0]
        for b in range(NB):
            out.append(out[-1] + f(b, kind_of[b]))
        return out + [out[-1]] * 4
    T_ch = table(lambda b, k: k.chunks)
    T_gr = table(lambda b, k: k.groups)
    T_conv = table(lambda b, k: k.how == "conv")
    T_pool = table(lambda b, k: k.how == "pool")
    T_st = [table(lambda b, k: (k.stored is not None) * (b % 2 == n)) for n in range(2)]
    T_tok = table(lambda b, k: k.turned is not None)

    def wait(eng, sem, value):
        if not isinstance(value, int) or value > 0:
            eng.wait_ge(sem, value)

    with ExitStack() as ctx:
        sb = lambda *args: kit.sbuf(ctx, *args)
        w_raw = [sb(f"{name}_w_raw{n}", [P, KT, P]) for n in range(2)]
        w_hi = [sb(f"{name}_w_hi{n}", [P, KT, P], F32R) for n in range(2)]
        w_lo = [sb(f"{name}_w_lo{n}", [P, KT, P], F32R) for n in range(2)]
        BW = 2312
        work = sb(f"{name}_work", [P, 3 * BW + TOK])
        raw, acc, act_b = (work[:, j * BW:(j + 1) * BW] for j in range(3))
        tok = work[:, 3 * BW:3 * BW + TOK].rearrange("p (t c) -> p t c", c=P)
        direct = (raw, act_b)
        box = work[:, BW:BW + 40 * GRID_C].rearrange("p (r c) -> p r c", c=GRID_C)
        boxc = work[:, BW + 2560:BW + 2560 + 32 * 72].rearrange("p (r c) -> p r c", c=72)
        inv = work[:, BW + 2560 + 2304:BW + 2560 + 2304 + SEQ]
        ps = kit.psum(ctx, f"{name}_ps", [P, 5, CH])
        psT = kit.psum(ctx, f"{name}_psT", [P, 3, 4, P])

        k = kit
        w_in = [k.sem(f"{name}_w_loaded{n}") for n in range(2)]
        hi_ok, lo_ok = k.sem(f"{name}_w_hi_ready"), k.sem(f"{name}_w_lo_ready")
        ch_ok, ev_ok = k.sem(f"{name}_chunk_done"), k.sem(f"{name}_chunk_read")
        conv_ok, silu_ok, pool_ok = k.sem(f"{name}_conv_done"), k.sem(f"{name}_silu_done"), k.sem(f"{name}_pool_done")
        tg_ok, te_ok = k.sem(f"{name}_group_turned"), k.sem(f"{name}_group_read")
        tok_out = k.sem(f"{name}_tok_stored")
        c_out = [k.sem(f"{name}_channels_stored{n}") for n in range(2)]
        pad_ok = k.sem(f"{name}_pads_zero")
        inv_in = k.sem(f"{name}_inv_loaded")
        dve = Tally(k.sem(f"{name}_dve_chain"))

        def chunk_cols(c):
            return (slice(c * CH, (c + 1) * CH), CH) if c < NCH else (slice(SEQ, TOK), CTX)

        def tile_cols(t):
            return slice(t * P, (t + 1) * P) if t < LT else slice(CTX_AT + (t - LT) * P, CTX_AT + (t - LT + 1) * P)

        def walk(eng, body, per=None):
            for piece in plan:
                if piece[0] == "one":
                    body(Where(piece[1]))
                else:
                    _, b0, turns = piece
                    with eng.Fori(0, turns) as i:
                        if per is None:
                            for d in range(2):
                                body(Where(b0 + d, i, turns))
                        else:
                            with dve.turn(i, per(b0) + per(b0 + 1), turns):
                                for d in range(2):
                                    body(Where(b0 + d, i, turns))

        with nc.Block() as block:
            @block.sync
            def _(sp):
                def load_w(w, ahead):
                    b = w.b0 + ahead
                    if b >= NB:
                        return
                    if ahead == 2:
                        sp.wait_ge(hi_ok, w.num() + 1)
                        sp.wait_ge(lo_ok, w.num() + 1)
                    sp.dma_start(w_raw[b % 2][:], w_dram[w.num() + ahead]).then_inc(w_in[b % 2], 16)

                def stores(w):
                    kd, n = kind_of[w.b0], w.b0 % 2
                    m = w.num() - kd.first
                    if kd.stored is not None:
                        if kd.how == "conv":
                            sp.wait_ge(silu_ok, w.at(T_conv, 1))
                            src = act_b[0:kd.width, 0:SEQ]
                        elif kd.how == "pool":
                            sp.wait_ge(pool_ok, w.at(T_pool, 1))
                            src = work[:, BW:BW + SEQ]
                        else:
                            sp.wait_ge(ev_ok, w.at(T_ch, 1))
                            src = direct[n][0:kd.width, 0:SEQ]
                        sp.dma_start(kd.stored[m], src).then_inc(c_out[n], 16)
                    if kd.turned is not None:
                        sp.wait_ge(te_ok, w.at(T_gr, 1))
                        tiles = kd.chunks * 4 if kd.chunks == 4 else TT
                        dst = kd.turned.rearrange("(t p) c -> p t c", p=P)
                        dst = dst if kd.width != P else dst[:, :, bass.ds(m * P, P)]
                        sp.dma_start(dst, tok[:, 0:tiles, 0:kd.width]).then_inc(tok_out, 16)

                def body(w):
                    load_w(w, 2)
                    if kind_of[w.b0].how == "pool" and (w.b0 - kind_of[w.b0].first) % 2 == 0:
                        wait(sp, pool_ok, w.at(T_pool))
                        grp = (w.num() - kind_of[w.b0].first)
                        g0 = (w.b0 - kind_of[w.b0].first) // 2
                        g = g0 if w.i is None else g0 + w.i
                        if g0 == 0:
                            wait(sp, tok_out, 16 * T_tok[w.b0])
                        sp.dma_start(inv, a["inv_count"][g:g + 1, :].partition_broadcast(P) if isinstance(g, int)
                                     else a["inv_count"][bass.ds(g, 1), :].partition_broadcast(P)).then_inc(inv_in, 16)
                    if w.b0 >= 1:
                        stores(Where(w.b0 - 1, w.i, w.turns))

                load_w(Where(0), 0)
                load_w(Where(0), 1)
                walk(sp, body)
                stores(Where(NB - 1))
                for n in range(2):
                    sp.wait_ge(c_out[n], 16 * T_st[n][NB])
                if T_tok[NB]:
                    sp.wait_ge(tok_out, 16 * T_tok[NB])

            @block.scalar
            def _(act):
                def high(w, ahead):
                    b = w.b0 + ahead
                    if b >= NB:
                        return
                    half = (w.b0 + ahead) // 2 if w.i is None else (w.b0 + ahead) // 2 + w.i
                    act.wait_ge(w_in[b % 2], 16 * (half + 1))
                    act.activation(w_hi[b % 2][:], w_raw[b % 2][:], ACT.Copy).then_inc(hi_ok, 1)

                def silu(w):
                    act.wait_ge(conv_ok, w.at(T_conv, 1))
                    wait(act, tg_ok, w.at(T_gr))
                    for n in range(2):
                        wait(act, c_out[n], 16 * w.at(T_st[n]))
                    act.activation(act_b[:, 0:conv.width], acc[:, 0:conv.width], conv.func).then_inc(silu_ok, 1)

                def body(w):
                    kd, n = kind_of[w.b0], w.b0 % 2
                    before = kind_of[w.b0 - 1] if w.b0 else None
                    if before is not None and before.how == "conv":
                        silu(Where(w.b0 - 1, w.i, w.turns))
                    for c in range(kd.chunks):
                        act.wait_ge(ch_ok, w.at(T_ch) + c + 1)
                        cols, width = chunk_cols(c)
                        if c == 0:
                            if kd.how == "copy":
                                wait(act, tg_ok, w.at(T_gr, -1) if w.b0 else 0)
                                for q in range(2):
                                    if q == n or (before is not None and before.how == "conv") or \
                                            (w.b0 > 1 and kind_of[w.b0 - 2].how == "conv"):
                                        wait(act, c_out[q], 16 * w.at(T_st[q]))
                            else:
                                wait(act, conv_ok if kd.how == "conv" else pool_ok,
                                     w.at(T_conv if kd.how == "conv" else T_pool))
                                if kd.how == "pool" and before.how != "pool":
                                    for q in range(2):
                                        wait(act, c_out[q], 16 * w.at(T_st[q]))
                                    wait(act, tg_ok, w.at(T_gr))
                                if w.b0 == kinds[0].first:
                                    act.wait_ge(pad_ok, 1)
                        src = ps[0:P, c, 0:width]
                        if kd.how == "conv":
                            at = conv.left + c * CH if c < NCH else conv.left + CTX_AT
                            act.activation(raw[:, at:at + width], src, ACT.Identity).then_inc(ev_ok, 1)
                        elif kd.how == "pool":
                            act.activation(raw[:, cols], src, ACT.Identity).then_inc(ev_ok, 1)
                        else:
                            at = c * CH if c < NCH else CTX_AT
                            act.activation(direct[n][:, at:at + width], src, kd.func,
                                           scale=kd.scale).then_inc(ev_ok, 1)
                        if c == 0:
                            high(w, 1)

                high(Where(0), 0)
                walk(act, body)
                if kind_of[NB - 1].how == "conv":
                    silu(Where(NB - 1))

            @block.vector
            def _(v):
                def low(w, ahead):
                    b = w.b0 + ahead
                    if b >= NB:
                        return
                    v.wait_ge(hi_ok, w.num() + ahead + 1)
                    v.tensor_tensor(w_lo[b % 2][:], w_raw[b % 2][:], w_hi[b % 2][:].bitcast(F32),
                                    ALU.subtract).then_inc(lo_ok, 1)

                def read_groups(w):
                    kd = kind_of[w.b0]
                    for g in range(kd.groups):
                        v.wait_ge(tg_ok, w.at(T_gr) + g + 1)
                        if g == 0:
                            wait(v, tok_out, 16 * w.at(T_tok))
                        cnt = 4 if g < 4 else CT
                        v.tensor_copy(tok[:, 4 * g:4 * g + cnt, 0:kd.width],
                                      psT[:, g % 3, 0:cnt, 0:kd.width]).then_inc(te_ok, 1)

                def step(ins):
                    dve.mark(ins)
                    v.wait_ge(dve.sem, dve.value)

                def conv_block(w):
                    m = w.num() - kind_of[w.b0].first + conv.block0[kind_of[w.b0].first]
                    tap = lambda q: conv.tab[:, bass.ds(conv.w_at + q * conv.stride + m, 1)] if w.i is not None \
                        else conv.tab[:, conv.w_at + q * conv.stride + m:conv.w_at + q * conv.stride + m + 1]
                    bias = conv.tab[:, bass.ds(conv.b_at + m, 1)] if w.i is not None \
                        else conv.tab[:, conv.b_at + m:conv.b_at + m + 1]
                    v.wait_ge(ev_ok, w.at(T_ch, 1))
                    wait(v, silu_ok, w.at(T_conv))
                    W = conv.width
                    step(v.tensor_scalar(acc[:, 0:W], raw[:, 0:W], tap(0), bias, ALU.mult, ALU.add))
                    for q in range(1, 4):
                        ins = v.scalar_tensor_tensor(acc[:, 0:W], raw[:, q:q + W], tap(q), acc[:, 0:W],
                                                     ALU.mult, ALU.add)
                        if q < 3:
                            step(ins)
                    ins.then_inc(conv_ok, 1)

                def pool_block(w):
                    g = (w.b0 - kind_of[w.b0].first) // 2
                    win = WINDOWS[g]
                    u = raw[:, 0:SEQ].rearrange("p (r c) -> p r c", c=GRID_C)
                    v.wait_ge(ev_ok, w.at(T_ch, 1))
                    for q in range(2):
                        wait(v, c_out[q], 16 * T_st[q][w.b0])
                    if w.b0 == kind_of[w.b0].first:
                        wait(v, tok_out, 16 * T_tok[w.b0])

                    def spans(dst, src, n, cut):
                        v.memset(cut(dst, 0, 7), 0.0)
                        v.tensor_copy(cut(dst, 7, 8), cut(src, 0, 1))
                        v.tensor_copy(cut(dst, n + 7, n + 8), cut(src, n - 1, n))
                        step(v.tensor_tensor(cut(dst, 8, n + 7), cut(src, 0, n - 1), cut(src, 1, n), ALU.add))
                        half = 2
                        while half < win:
                            step(v.tensor_tensor(cut(dst, 0, n + 8 - half), cut(dst, 0, n + 8 - half),
                                                 cut(dst, half, n + 8), ALU.add))
                            half *= 2
                        return cut(dst, 8 - win // 2, 8 - win // 2 + n)

                    rows = spans(box, u, GRID_R, lambda x, i, j: x[:, i:j, :])
                    both = spans(boxc, rows, GRID_C, lambda x, i, j: x[:, :, i:j])
                    v.wait_ge(inv_in, 16 * (g + 1))
                    d = box[:, 0:GRID_R, :]
                    step(v.tensor_tensor(d, both, inv.rearrange("p (r c) -> p r c", c=GRID_C), ALU.mult))
                    v.tensor_tensor(d, d, u, ALU.subtract).then_inc(pool_ok, 1)

                def body(w):
                    kd = kind_of[w.b0]
                    low(w, 1)
                    if w.b0 >= 1:
                        read_groups(Where(w.b0 - 1, w.i, w.turns))
                    if kd.how == "conv":
                        conv_block(w)
                    if kd.how == "pool":
                        pool_block(w)

                v.memset(raw, 0.0).then_inc(pad_ok, 1)
                low(Where(0), 0)
                for piece in plan:
                    if piece[0] == "one":
                        body(Where(piece[1]))
                    elif kind_of[piece[1]].how == "pool":
                        for b in range(piece[1], piece[1] + 2 * piece[2]):
                            body(Where(b))
                    else:
                        _, b0, turns = piece
                        per = sum(3 * (kind_of[b0 + d].how == "conv") for d in range(2))
                        with v.Fori(0, turns) as i:
                            with dve.turn(i, per, turns):
                                for d in range(2):
                                    body(Where(b0 + d, i, turns))
                if kind_of[NB - 1].groups:
                    read_groups(Where(NB - 1))

            @block.tensor
            def _(pe):
                def turn(w, groups):
                    kd, n = kind_of[w.b0], w.b0 % 2
                    src = act_b if kd.how == "conv" else direct[n]
                    for g in groups:
                        if g == groups[0]:
                            if kd.how == "conv":
                                pe.wait_ge(silu_ok, w.at(T_conv, 1))
                            else:
                                pe.wait_ge(ev_ok, w.at(T_ch, 1))
                        wait(pe, te_ok, w.at(T_gr) + max(0, g - 2))
                        for q in range(4 if g < 4 else CT):
                            mm = pe.transpose(psT[:, g % 3, q, :], src[:, tile_cols(4 * g + q)], s.ident[:])
                        mm.then_inc(tg_ok, 1)

                def body(w):
                    kd, n = kind_of[w.b0], w.b0 % 2
                    before = kind_of[w.b0 - 1] if w.b0 else None
                    pe.wait_ge(lo_ok, w.num() + 1)
                    for c in range(kd.chunks):
                        cols, width = chunk_cols(c)
                        if before is not None:
                            pe.wait_ge(ev_ok, w.at(T_ch, -1) + min(c, before.chunks - 1) + 1)
                        for q in range(KT):
                            for j, (wt, xx) in enumerate(((w_hi, x_hi), (w_hi, x_lo), (w_lo, x_hi))):
                                mm = pe.matmul(ps[:, c, 0:width], wt[n][:, q, :], xx[:, q, cols],
                                               start=(q == 0 and j == 0), stop=(q == KT - 1 and j == 2))
                        mm.then_inc(ch_ok, 1)
                        if before is not None and before.groups:
                            prev = Where(w.b0 - 1, w.i, w.turns)
                            if c == kd.chunks - 2:
                                turn(prev, [0, 1])
                            if c == kd.chunks - 1:
                                turn(prev, list(range(2, before.groups)))

                walk(pe, body)
                if kind_of[NB - 1].groups:
                    turn(Where(NB - 1), list(range(kind_of[NB - 1].groups)))


class Conv:

    def __init__(self, tab, w_at, b_at, stride, block0, left, width, func):
        self.tab, self.w_at, self.b_at, self.stride, self.block0 = tab, w_at, b_at, stride, block0
        self.left, self.width, self.func = left, width, func


def projection(nc, kit, a, s, hmT):
    kinds = [
        Kind(XS0, 8, 5, "conv", turned=a["xs_tok"]),
        Kind(B0, 4, 5, "conv", turned=a["b_tok"], stored=a["bT"]),
        Kind(C0, 4, 5, "conv", stored=a["cT"]),
        Kind(DT0, 1, 5, "copy", turned=a["dt_tok"], width=NDH),
        Kind(ZS0, 8, 4, "copy", turned=a["z_tok"], func=ACT.Silu),
        Kind(ZP0, 8, 4, "copy", stored=a["zpT"], func=ACT.Silu),
        Kind(U0, 8, 4, "pool", stored=a["dT"]),
    ]
    conv = Conv(s.cols1, V_CONVW, V_CONVB, 16, {XS0: 0, B0: 8, C0: 12}, 2, SEQ + 3 + CTX, ACT.Silu)
    plan = [("one", 0), ("one", 1), ("loop", 2, 3), ("one", 8), ("one", 9), ("loop", 10, 1)] + \
           [("one", b) for b in range(12, 19)] + [("loop", 19, 3), ("one", 25), ("one", 26), ("loop", 27, 3)] + \
           [("one", 33), ("one", 34), ("loop", 35, 2), ("one", 39), ("one", 40)]
    project(nc, kit, a, s, "p1", kinds, plan, hmT, a["w_in"], conv, True)


LOG1P_ODD = [1.0 / j for j in (15, 13, 11, 9, 7, 5, 3)]


def softplus(v, step, exp, out, x, t):
    step(v.scalar_tensor_tensor(t[0], x, -1.0, x, ALU.mult, ALU.min))
    exp()
    step(v.tensor_scalar(t[1], t[0], 2.0, None, ALU.add))
    step(v.reciprocal(t[2], t[1]))
    step(v.tensor_tensor(t[0], t[0], t[2], ALU.mult))
    step(v.tensor_tensor(t[1], t[0], t[0], ALU.mult))
    step(v.tensor_scalar(t[2], t[1], LOG1P_ODD[0], None, ALU.mult))
    for c in LOG1P_ODD[1:]:
        step(v.scalar_tensor_tensor(t[2], t[2], c, t[1], ALU.add, ALU.mult))
    step(v.scalar_tensor_tensor(t[2], t[2], 1.0, t[0], ALU.add, ALU.mult))
    step(v.tensor_scalar(t[0], x, 0.0, None, ALU.max))
    step(v.scalar_tensor_tensor(out, t[2], 2.0, t[0], ALU.mult, ALU.add))


def ssd_decays(nc, kit, a, s, r):
    F = TT * NDH
    with ExitStack() as ctx:
        sb = lambda *args: kit.sbuf(ctx, *args)
        bias, alog = sb("dt_bias_row", [P, NDH]), sb("a_log_row", [P, NDH])
        xr, adt, tot = sb("dt_raw", [P, TT, NDH]), sb("adt", [P, TT, NDH]), sb("acum_end", [P, TT, NDH])
        t = [sb(f"sp_tmp{n}", [P, TT, NDH]) for n in range(3)]
        sel = [sb(f"sel_{n}", [P, P]) for n in ("last", "first")]
        rows, sums = sb("adt_rows", [HEADS, 2, TOK]), sb("acum_rows_sb", [HEADS, 2, TOK])
        keepm = [sb(f"chunk_keep{n}", [HEADS, TOK]) for n in range(2)]
        psA = [kit.psum(ctx, f"psA{n}", [HEADS, 4, P]) for n in range(2)]
        psB = kit.psum(ctx, "psB", [P, 2, 512])
        psE = kit.psum(ctx, "psE", [P, 2, 512])
        k = kit
        ld, ek_ok, e_done = k.sem("d_loaded"), k.sem("d_exp_asked"), k.sem("d_exp_done")
        adt_ok, tr_ok, rd_ok = k.sem("d_adt_ready"), k.sem("d_rows_turned"), k.sem("d_rows_read")
        scan_ok, back_ok, ac_ok, end_ok = (k.sem(n) for n in ("d_scanned", "d_sums_turned", "d_acum_ready", "d_ends_ready"))
        st = k.sem("d_rows_stored")
        dve = Tally(k.sem("d_dve_chain"))
        with nc.Block() as block:
            @block.sync
            def _(sp):
                for dst, src in ((bias[:], a["dt_bias"].partition_broadcast(P)), (alog[:], a["a_log"].partition_broadcast(P)),
                                 (xr[:], a["dt_tok"].rearrange("(t p) c -> p t c", p=P)),
                                 (sel[0][:], a["sel_last"]), (sel[1][:], a["sel_first"]),
                                 (keepm[0][:], a["keep_fwd"]), (keepm[1][:], a["keep_bwd"]),
                                 (r.dskip[:], a["d_skip"].partition_broadcast(P))):
                    sp.dma_start(dst, src).then_inc(ld, 16)
                sp.wait_ge(scan_ok, 2)
                for d in range(2):
                    sp.dma_start(a["acum_rows"][:, d * HEADS:(d + 1) * HEADS, :].rearrange("t h l -> h t l"),
                                 sums[:, d].rearrange("h (t l) -> h t l", l=P)).then_inc(st, 16)
                sp.wait_ge(st, 32)

            @block.scalar
            def _(act):
                act.wait_ge(ld, 128)
                act.activation(alog[:], alog[:], ACT.Exp).then_inc(e_done, 1)
                act.wait_ge(ek_ok, 1)
                act.activation(t[0][:], t[0][:], ACT.Exp).then_inc(e_done, 1)
                act.wait_ge(ac_ok, 4)
                act.activation(r.eac[:], r.acum[:], ACT.Exp).then_inc(e_done, 1)
                act.wait_ge(ek_ok, 2)
                act.activation(r.wst[:], t[0][:], ACT.Exp).then_inc(e_done, 1)
                act.activation(r.cdec[:], tot[:], ACT.Exp).then_inc(e_done, 1)

            @block.vector
            def _(v):
                def step(ins):
                    dve.mark(ins)
                    v.wait_ge(dve.sem, dve.value)

                def ask():
                    v.nop().then_inc(ek_ok, 1)
                    v.wait_ge(e_done, 2)

                v.wait_ge(ld, 128)
                step(v.tensor_tensor(xr[:], xr[:], bias[:].unsqueeze(1).to_broadcast([P, TT, NDH]), ALU.add))
                softplus(v, step, ask, r.dt[:], xr[:], [x[:] for x in t])
                step(v.scalar_tensor_tensor(adt[:], alog[:].unsqueeze(1).to_broadcast([P, TT, NDH]), -1.0, r.dt[:],
                                            ALU.mult, ALU.mult))
                v.nop().then_inc(adt_ok, 1)
                for d in range(2):
                    for g in range(5):
                        q = 5 * d + g
                        cnt = 4 if g < 4 else 2
                        v.wait_ge(tr_ok, q + 1)
                        v.tensor_copy(rows[:, d, g * CH:g * CH + cnt * P].rearrange("h (t l) -> h t l", l=P),
                                      psA[q % 2][:, 0:cnt, :]).then_inc(rd_ok, 1)
                v.wait_ge(rd_ok, 10)
                v.tensor_tensor_scan(sums[:, 0, :], keepm[0][:], rows[:, 0, :], 0.0, ALU.mult, ALU.add).then_inc(scan_ok, 1)
                v.tensor_tensor_scan(sums[:, 1, ::-1], keepm[1][:, ::-1], rows[:, 1, ::-1], 0.0, ALU.mult,
                                     ALU.add).then_inc(scan_ok, 1)
                for d in range(2):
                    v.wait_ge(back_ok, d + 1)
                    v.tensor_copy(r.acum[:, :, d * HEADS:(d + 1) * HEADS],
                                  psB[:, d, 0:TT * HEADS].rearrange("p (t h) -> p t h", h=HEADS)).then_inc(ac_ok, 1)
                for d in range(2):
                    v.wait_ge(end_ok, d + 1)
                    v.tensor_copy(tot[:, :, d * HEADS:(d + 1) * HEADS],
                                  psE[:, d, 0:TT * HEADS].rearrange("p (t h) -> p t h", h=HEADS)).then_inc(ac_ok, 1)
                v.wait_ge(ac_ok, 4)
                step(v.tensor_tensor(t[0][:], tot[:], r.acum[:], ALU.subtract))
                v.nop().then_inc(ek_ok, 1)
                v.wait_ge(e_done, 4)
                v.tensor_tensor(r.wst[:], r.wst[:], r.dt[:], ALU.mult)

            @block.tensor
            def _(pe):
                pe.wait_ge(adt_ok, 1)
                for d in range(2):
                    for g in range(5):
                        q = 5 * d + g
                        if q >= 2:
                            pe.wait_ge(rd_ok, q - 1)
                        for j in range(4 if g < 4 else 2):
                            mm = pe.transpose(psA[q % 2][:, j, :], adt[:, 4 * g + j, d * HEADS:(d + 1) * HEADS], s.ident[:])
                        mm.then_inc(tr_ok, 1)
                for d in range(2):
                    pe.wait_ge(scan_ok, d + 1)
                    for c in range(TT):
                        mm = pe.transpose(psB[:, d, c * HEADS:(c + 1) * HEADS], sums[:, d, c * P:(c + 1) * P],
                                          s.ident[0:HEADS, 0:HEADS])
                    mm.then_inc(back_ok, 1)
                for d in range(2):
                    pe.wait_ge(ac_ok, d + 1)
                    pe.matmul(psE[:, d, 0:TT * HEADS].rearrange("p (t h) -> p t h", h=HEADS), sel[d][:],
                              r.acum[:, :, d * HEADS:(d + 1) * HEADS], start=True, stop=True).then_inc(end_ok, 1)


def heads_of(row):
    return row.unsqueeze(2).to_broadcast([P, HEADS, HD])


def by_head(t):
    return t.rearrange("p (h d) -> p h d", d=HD)


def ssd_states(nc, kit, a, s, r):
    STEPS = 19
    with ExitStack() as ctx:
        sb = lambda *args: kit.sbuf(ctx, *args)
        xs = [sb(f"st_xs{n}", [P, W_HALF]) for n in range(2)]
        bt = [sb(f"st_b{n}", [P, GROUPS * NS]) for n in range(2)]
        xw = [sb(f"st_xw{n}", [P, W_HALF]) for n in range(2)]
        mid = sb("st_mid", [P, W_HALF])
        psS = [kit.psum(ctx, f"psS{n}", [P, W_HALF]) for n in range(2)]
        k = kit
        ld = [k.sem(f"st_loaded{n}") for n in range(2)]
        zero_ok, xw_ok, s_ok, h_ok = (k.sem(f"st_{n}") for n in ("zeroed", "weighted", "summed", "state_ready"))
        dve = Tally(k.sem("st_dve_chain"))

        def chunk(j):
            if isinstance(j, int):
                return j - 1 if j >= 17 else 17 - j
            return j * -1 + 17

        def tok(t, c):
            return t[c * P:(c + 1) * P, :] if isinstance(c, int) else t[bass.ds(c * P, P), :]

        def one(t, c):
            return t[:, c, :]

        def walk(eng, body, count=0, tally=None):
            for j in range(2):
                body(j, 0, j)
            with eng.Fori(1, 8) as i:
                if tally is None:
                    for n in range(2):
                        body(2 * i + n, i, n)
                else:
                    with tally.turn(i - 1, 2 * count, 7):
                        for n in range(2):
                            body(2 * i + n, i, n)
            for j in range(16, STEPS):
                body(j, j // 2, j % 2)

        with nc.Block() as block:
            @block.sync
            def _(sp):
                def load(j, n):
                    c = chunk(j)
                    if not isinstance(j, int) or j >= 2:
                        sp.wait_ge(s_ok, j - 1)
                    sp.dma_start(xs[n][:], tok(a["xs_tok"], c)).then_inc(ld[n], 16)
                    sp.dma_start(bt[n][:], tok(a["b_tok"], c)).then_inc(ld[n], 16)

                load(0, 0)
                load(1, 1)
                with sp.Fori(1, 8) as i:
                    for n in range(2):
                        load(2 * i + n, n)
                for j in range(16, STEPS):
                    load(j, j % 2)

            @block.gpsimd
            def _(g):
                def body(j, half, n):
                    d = 0 if isinstance(j, int) and j >= 17 else 1
                    c = chunk(j)
                    weight = heads_of(one(r.wst, c)[:, d * HEADS:(d + 1) * HEADS])
                    g.wait_ge(ld[n], 32 * (half + 1))
                    if not isinstance(j, int) or j >= 2:
                        g.wait_ge(s_ok, j - 1)
                    g.tensor_tensor(by_head(xw[n][:]), by_head(xs[n][:]), weight, ALU.mult).then_inc(xw_ok, 1)
                walk(g, body)

            @block.tensor
            def _(pe):
                def body(j, half, n):
                    pe.wait_ge(xw_ok, j + 1)
                    if not isinstance(j, int) or j >= 2:
                        pe.wait_ge(h_ok, j - 1)
                    for grp in range(GROUPS):
                        mm = pe.matmul(psS[n][:, grp * 256:(grp + 1) * 256], bt[n][:, grp * NS:(grp + 1) * NS],
                                       xw[n][:, grp * 256:(grp + 1) * 256], start=True, stop=True)
                    mm.then_inc(s_ok, 1)
                walk(pe, body)

            @block.vector
            def _(v):
                v.memset(r.hb[:, 17, :], 0.0).then_inc(zero_ok, 1)
                v.memset(r.hf[0][:], 0.0).then_inc(zero_ok, 1)
                v.wait_ge(zero_ok, 2)

                def body(j, half, n):
                    c = chunk(j)
                    if isinstance(j, int) and j >= 17:
                        src, dst, d = r.hf[j - 17][:], r.hf[18 - j][:], 0
                    else:
                        src, dst, d = r.hb[:, c, :], r.hb[:, c - 1, :], 1
                    decay = heads_of(one(r.cdec, c)[:, d * HEADS:(d + 1) * HEADS])
                    v.wait_ge(s_ok, j + 1)
                    dve.mark(v.tensor_tensor(by_head(mid[:]), by_head(src), decay, ALU.mult))
                    v.wait_ge(dve.sem, dve.value)
                    v.tensor_tensor(dst, mid[:], psS[n][:], ALU.add).then_inc(h_ok, 1)
                    v.wait_ge(h_ok, j + 1)
                walk(v, body, 1, dve)


def ssd_outputs(nc, kit, a, s, r):
    with ExitStack() as ctx:
        sb = lambda *args: kit.sbuf(ctx, *args)
        two = lambda name, shape: [sb(f"{name}{n}", shape) for n in range(2)]
        rowb, xs, bt, zt = two("y_decay", [P, NDH, P]), two("y_xs", [P, W_HALF]), two("y_b", [P, 512]), two("y_z", [P, W_HALF])
        bT, cT = two("y_bT", [P, GROUPS, P]), two("y_cT", [P, GROUPS, P])
        xd = two("y_xd", [P, 2, W_HALF])
        xw, xk = two("y_xw", [P, W_HALF]), sb("y_xskip", [P, W_HALF])
        cbm = two("y_cb", [P, 2, GROUPS, P])
        y, t2 = two("y_out", [P, W_HALF]), sb("y_t2", [P, W_HALF])
        mid = sb("y_mid", [P, W_HALF])
        tri = sb("y_masks", [P, 2, P])
        psCB = kit.psum(ctx, "psCB", [P, GROUPS, P])
        psS = kit.psum(ctx, "psSt", [P, W_HALF])
        psY = kit.psum(ctx, "psY", [P, W_HALF])
        psO = kit.psum(ctx, "psO", [P, W_HALF])
        k = kit
        names = ("xw_ok", "xd_ok", "cb_ok", "cbm_ok", "s_ok", "h_ok", "segf_ok", "expf_ok", "expb_ok", "m_ok",
                 "off_f_ok", "off_b_ok", "t1_ok", "t2_ok", "yd_ok", "g_ok", "relu_ok")
        S = k.sems("y_", names)
        ld = [k.sem(f"y_loaded{n}") for n in range(2)]
        st = [k.sem(f"y_stored{n}") for n in range(2)]
        mk_in = k.sem("y_masks_loaded")
        dve = Tally(k.sem("y_dve_chain"))
        NC = LT

        def tokens(t, c):
            return t[c * P:(c + 1) * P, :] if isinstance(c, int) else t[bass.ds(c * P, P), :]

        def cols(t, c):
            t = t.rearrange("g n l -> n g l")
            return t[:, :, c * P:(c + 1) * P] if isinstance(c, int) else t[:, :, bass.ds(c * P, P)]

        def part(t, c, d):
            return t[:, c, d * HEADS:(d + 1) * HEADS]

        with nc.Block() as block:
            @block.sync
            def _(sp):
                sp.dma_start(tri[:, 0], a["upper"]).then_inc(mk_in, 16)
                sp.dma_start(tri[:, 1], a["lower"]).then_inc(mk_in, 16)

                def load(c, n):
                    row = a["acum_rows"][c:c + 1] if isinstance(c, int) else a["acum_rows"][bass.ds(c, 1)]
                    sp.dma_start(rowb[n][:].rearrange("p h l -> p (h l)"),
                                 row.rearrange("o h l -> o (h l)").partition_broadcast(P)).then_inc(ld[n], 16)
                    for dst, src in ((xs[n][:], tokens(a["xs_tok"], c)), (bt[n][:], tokens(a["b_tok"], c)),
                                     (zt[n][:], tokens(a["z_tok"], c)), (bT[n][:], cols(a["bT"], c)), (cT[n][:], cols(a["cT"], c))):
                        sp.dma_start(dst, src).then_inc(ld[n], 16)

                def store(c, n):
                    sp.wait_ge(S["g_ok"], c + 1)
                    sp.dma_start(tokens(a["g_tok"], c), y[n][:]).then_inc(st[n], 16)

                load(0, 0)
                load(1, 1)
                with sp.Fori(0, NC // 2 - 1) as i:
                    for n in range(2):
                        store(2 * i + n, n)
                        load(2 * i + n + 2, n)
                for n in range(2):
                    store(NC - 2 + n, n)
                for n in range(2):
                    sp.wait_ge(st[n], 16 * NC // 2)

            @block.gpsimd
            def _(g):
                with g.Fori(0, NC // 2) as i:
                    for n in range(2):
                        c = 2 * i + n
                        g.wait_ge(ld[n], 96 * (i + 1))
                        g.tensor_tensor(by_head(xw[n][:]), by_head(xs[n][:]), heads_of(part(r.wst, c, 0)),
                                        ALU.mult).then_inc(S["xw_ok"], 1)
                        for d in range(2):
                            g.tensor_tensor(by_head(xd[n][:, d, :]), by_head(xs[n][:]), heads_of(part(r.dt, c, d)),
                                            ALU.mult).then_inc(S["xd_ok"], 1)
                        g.wait_ge(S["t1_ok"], c)
                        g.tensor_tensor(by_head(xk[:]), by_head(xs[n][:]), heads_of(r.dskip[:]),
                                        ALU.mult).then_inc(S["xd_ok"], 1)

            @block.scalar
            def _(act):
                with act.Fori(0, NC // 2) as i:
                    for n in range(2):
                        c = 2 * i + n
                        act.wait_ge(ld[n], 96 * (i + 1))
                        for h in range(HEADS, NDH):
                            ins = act.activation(rowb[n][:, h, :], rowb[n][:, h, :], ACT.Relu, scale=-1.0,
                                                 bias=r.acum[:, c, h:h + 1])
                        ins.then_inc(S["relu_ok"], 1)
                        act.wait_ge(S["relu_ok"], c + 1)
                        act.activation(rowb[n][:, HEADS:NDH, :], rowb[n][:, HEADS:NDH, :], ACT.Exp,
                                       scale=-1.0).then_inc(S["expb_ok"], 1)
                        act.wait_ge(S["segf_ok"], c + 1)
                        act.activation(rowb[n][:, 0:HEADS, :], rowb[n][:, 0:HEADS, :], ACT.Exp).then_inc(S["expf_ok"], 1)

            @block.vector
            def _(v):
                def step(ins):
                    dve.mark(ins)
                    v.wait_ge(dve.sem, dve.value)

                def front(c, half, n):
                    v.wait_ge(ld[n], 96 * (half + 1))
                    for h in range(HEADS):
                        ins = v.tensor_scalar(rowb[n][:, h, :], rowb[n][:, h, :], r.acum[:, c, h:h + 1], 0.0,
                                              ALU.subtract, ALU.min)
                    ins.then_inc(S["segf_ok"], 1)
                    v.wait_ge(S["cb_ok"], c + 1)
                    for d in range(2):
                        ins = v.tensor_tensor(cbm[n][:, d], psCB[:], tri[:, d].unsqueeze(1).to_broadcast([P, GROUPS, P]),
                                              ALU.mult)
                        ins.then_inc(S["cbm_ok"], 1)
                    if not isinstance(c, int) or c > 0:
                        v.wait_ge(S["h_ok"], c)
                    step(v.tensor_tensor(by_head(mid[:]), by_head(r.hf[n][:]), heads_of(part(r.cdec, c, 0)), ALU.mult))
                    v.wait_ge(S["s_ok"], c + 1)
                    if not isinstance(c, int) or c > 0:
                        v.wait_ge(S["off_f_ok"], c)
                    v.tensor_tensor(r.hf[1 - n][:], mid[:], psS[:], ALU.add).then_inc(S["h_ok"], 1)
                    for d, e in enumerate((S["expf_ok"], S["expb_ok"])):
                        v.wait_ge(e, c + 1)
                        v.wait_ge(S["cbm_ok"], 2 * c + d + 1)
                        m = rowb[n][:, d * HEADS:(d + 1) * HEADS, :].rearrange("p (g q) l -> p g q l", g=GROUPS)
                        v.tensor_tensor(m, m, cbm[n][:, d].unsqueeze(2).to_broadcast([P, GROUPS, HPG, P]),
                                        ALU.mult).then_inc(S["m_ok"], 1)

                def back(c, half, n):
                    v.wait_ge(S["off_f_ok"], c + 1)
                    if not isinstance(half, int) or half > 0:
                        v.wait_ge(st[n], 16 * half)
                    step(v.tensor_tensor(by_head(y[n][:]), by_head(psO[:]), heads_of(part(r.eac, c, 0)), ALU.mult))
                    v.wait_ge(S["yd_ok"], c + 1)
                    v.tensor_tensor(y[n][:], y[n][:], psY[:], ALU.add).then_inc(S["t1_ok"], 1)
                    v.wait_ge(S["off_b_ok"], c + 1)
                    step(v.tensor_tensor(by_head(t2[:]), by_head(psO[:]), heads_of(part(r.eac, c, 1)), ALU.mult))
                    step(v.tensor_tensor(y[n][:], y[n][:], t2[:], ALU.add))
                    v.tensor_tensor(y[n][:], y[n][:], zt[n][:], ALU.mult).then_inc(S["g_ok"], 1)

                v.wait_ge(mk_in, 32)
                front(0, 0, 0)
                front(1, 0, 1)
                back(0, 0, 0)
                with v.Fori(1, NC // 2) as i:
                    with dve.turn(i - 1, 8, NC // 2 - 1):
                        front(2 * i, i, 0)
                        back(2 * i - 1, i - 1, 1)
                        front(2 * i + 1, i, 1)
                        back(2 * i, i, 0)
                back(NC - 1, NC // 2 - 1, 1)

            @block.tensor
            def _(pe):
                def early(c, half, n):
                    pe.wait_ge(ld[n], 96 * (half + 1))
                    first = isinstance(c, int) and c == 0
                    if not first:
                        pe.wait_ge(S["cbm_ok"], 2 * c)
                    for g in range(GROUPS):
                        mm = pe.matmul(psCB[:, g, :], bT[n][:, g, :], cT[n][:, g, :], start=True, stop=True)
                    mm.then_inc(S["cb_ok"], 1)
                    pe.wait_ge(S["xw_ok"], c + 1)
                    if not first:
                        pe.wait_ge(S["h_ok"], c)
                    for g in range(GROUPS):
                        mm = pe.matmul(psS[:, g * 256:(g + 1) * 256], bt[n][:, g * NS:(g + 1) * NS],
                                       xw[n][:, g * 256:(g + 1) * 256], start=True, stop=True)
                    mm.then_inc(S["s_ok"], 1)

                def offset(c, state):
                    for g in range(GROUPS):
                        mm = pe.matmul(psO[:, g * 256:(g + 1) * 256], cT[c][:, g, :], state[:, g * 256:(g + 1) * 256],
                                       start=True, stop=True)
                    return mm

                def late(c, n):
                    first = isinstance(c, int) and c == 0
                    if not first:
                        pe.wait_ge(S["h_ok"], c)
                        pe.wait_ge(S["g_ok"], c)
                    offset(n, r.hf[n]).then_inc(S["off_f_ok"], 1)
                    pe.wait_ge(S["m_ok"], 2 * c + 2)
                    pe.wait_ge(S["xd_ok"], 3 * c + 3)
                    for q in range(2):
                        pe.matmul(psY[:, q * CH:(q + 1) * CH], s.ident[:], xk[:, q * CH:(q + 1) * CH],
                                  start=True, stop=False, skip_group_check=True)
                        for h in range(8 * q, 8 * q + 8):
                            for d in range(2):
                                mm = pe.matmul(psY[:, h * HD:(h + 1) * HD], rowb[n][:, d * HEADS + h, :],
                                               xd[n][:, d, h * HD:(h + 1) * HD], start=False,
                                               stop=(h == 8 * q + 7 and d == 1), skip_group_check=True)
                    mm.then_inc(S["yd_ok"], 1)
                    pe.wait_ge(S["t1_ok"], c + 1)
                    offset(n, r.hb[:, c, :]).then_inc(S["off_b_ok"], 1)

                early(0, 0, 0)
                with pe.Fori(0, NC // 2 - 1) as i:
                    early(2 * i + 1, i, 1)
                    late(2 * i, 0)
                    early(2 * i + 2, i + 1, 0)
                    late(2 * i + 1, 1)
                early(NC - 1, NC // 2 - 1, 1)
                late(NC - 2, 0)
                late(NC - 1, 1)


def ssd(nc, kit, a, s):
    with ExitStack() as ctx:
        sb = lambda *args: kit.sbuf(ctx, *args)
        r = Names()
        r.dt, r.acum, r.eac, r.wst, r.cdec = (sb("ssd_" + n, [P, TT, NDH]) for n in ("dt", "acum", "eac", "wst", "cdec"))
        r.dskip = sb("ssd_dskip", [P, HEADS])
        ssd_decays(nc, kit, a, s, r)
        r.hb = sb("ssd_hb", [P, LT + 2, W_HALF])
        r.hf = [sb(f"ssd_hf{n}", [P, W_HALF]) for n in range(2)]
        ssd_states(nc, kit, a, s, r)
        ssd_outputs(nc, kit, a, s, r)


def walk_tiles(eng, body, tally=None, per=0):
    body(0, 0)
    with eng.Fori(0, LT // 2 - 1) as i:
        if tally is None:
            for n in (1, 0):
                body(2 * i + 2 - n, n)
        else:
            with tally.turn(i, 2 * per, LT // 2 - 1):
                for n in (1, 0):
                    body(2 * i + 2 - n, n)
    body(LT - 1, 1)


def starts(t):
    return isinstance(t, int) and t == 0


def ends(t):
    return isinstance(t, int) and t == LT - 1


def rows_at(t, i):
    return t[i * P:(i + 1) * P, :] if isinstance(i, int) else t[bass.ds(i * P, P), :]


def cols_at(t, i):
    t = t.rearrange("k c n -> c k n")
    return t[:, :, i * P:(i + 1) * P] if isinstance(i, int) else t[:, :, bass.ds(i * P, P)]


def mix_out(nc, kit, a, s):
    MT = 2 * KT
    with ExitStack() as ctx:
        sb = lambda *args: kit.sbuf(ctx, *args)
        w_hi, w_lo = sb("wo_hi", [P, MT, D], F32R), sb("wo_lo", [P, MT, D], F32R)
        pw = sb("pool_w_sb", [P, 4, 2, 256])
        gate, fnorm = sb("gate_row_sb", [P, D]), sb("final_norm_row", [P, D])
        dt_, zp, g, xt = (sb(n, [P, D]) for n in ("m_d", "m_zp", "m_g", "m_x"))
        piece = (dt_, zp, g, xt)
        y_hi = [sb(f"m_y_hi{n}", [P, MT, P], F32R) for n in range(2)]
        y_lo = [sb(f"m_y_lo{n}", [P, MT, P], F32R) for n in range(2)]
        rt, hn = sb("m_res", [P, D]), sb("m_hn", [P, D])
        h2t = sb("m_h2", [P, D])
        junk = sb("m_junk", [P, D], mybir.dt.bfloat16)
        st4 = sb("m_group_stat", [P, 3, GROUPS])
        st1 = sb("m_stat", [P, 8])
        bn = sb("m_bn", [P, 2, 6])
        mv, spare = sb("m_meanvar", [P, 2]), sb("m_spare", [P, 1])
        psP, psG, psH = (kit.psum(ctx, n, [P, KT, P]) for n in ("psPool", "psG", "psH"))
        psM = kit.psum(ctx, "psMix", [P, 2, CH])
        tiles = lambda t: t[:].rearrange("p (k n) -> p k n", n=P)
        k = kit
        S = k.sems("m_", ("rows_in", "scaled", "w_hi_ok", "w_lo_ok", "ssq", "root4", "gs", "yp", "hi_p", "hi_g", "lo_p", "lo_g",
                  "pool", "turn_g", "turn_h", "half", "r", "sq", "root", "x1", "mv", "root2", "hn", "ev_a", "ev_v",
                  "d_in", "zp_in", "g_in", "x_in", "x1_out", "h2_out", "sum_ok"))
        p_in = [k.sem(f"m_piece_loaded{n}") for n in range(4)]
        dve = Tally(k.sem("m_dve_chain"))

        with nc.Block() as block:
            @block.sync
            def _(sp):
                for dst, src in ((gate[:], a["gate_rows"][:, 0:D]), (fnorm[:], a["final_norm"].partition_broadcast(P)),
                                 (pw[:], a["pool_w"])):
                    sp.dma_start(dst, src).then_inc(S["rows_in"], 16)
                for q in range(MT):
                    if q >= 4:
                        sp.wait_ge(S["w_lo_ok"], q - 3)
                    sp.dma_start(piece[q % 4][:], a["w_out"][:, q, :]).then_inc(p_in[q % 4], 16)
                sp.wait_ge(S["w_lo_ok"], MT)

                def load(t):
                    if not starts(t):
                        sp.wait_ge(S["pool"], t)
                    sp.dma_start(tiles(dt_), cols_at(a["dT"], t)).then_inc(S["d_in"], 16)
                    if not starts(t):
                        sp.wait_ge(S["lo_p"], t)
                    sp.dma_start(tiles(zp), cols_at(a["zpT"], t)).then_inc(S["zp_in"], 16)
                    if not starts(t):
                        sp.wait_ge(S["turn_g"], t)
                    sp.dma_start(g[:], rows_at(a["g_tok"], t)).then_inc(S["g_in"], 16)

                load(0)
                sp.dma_start(xt[:], rows_at(a["x"], 0)).then_inc(S["x_in"], 16)
                load(1)

                def body(t, n):
                    if not ends(t) and not (isinstance(t, int) and t == LT - 2):
                        load(t + 2)
                    sp.wait_ge(S["x1"], t + 1)
                    if not ends(t):
                        sp.dma_start(xt[:], rows_at(a["x"], t + 1)).then_inc(S["x_in"], 16)
                    sp.dma_start(rows_at(a["x1"], t), rt[:]).then_inc(S["x1_out"], 16)

                def h2(t):
                    sp.wait_ge(S["ev_a"], t + 1)
                    sp.wait_ge(S["ev_v"], t + 1)
                    sp.dma_start(cols_at(a["h2T"], t), tiles(h2t)).then_inc(S["h2_out"], 16)

                body(0, 0)
                with sp.Fori(1, LT - 2) as t:
                    body(t, 0)
                    h2(t - 1)
                body(LT - 2, 0)
                h2(LT - 3)
                body(LT - 1, 1)
                h2(LT - 2)
                h2(LT - 1)
                sp.wait_ge(S["x1_out"], 16 * LT)
                sp.wait_ge(S["h2_out"], 16 * LT)

            @block.scalar
            def _(act):
                for q in range(MT):
                    v_at = V_PSCALE + q if q < KT else V_SNORM + q - KT
                    act.wait_ge(S["scaled"], q + 1)
                    act.activation(w_hi[:, q, :], piece[q % 4][:], ACT.Copy,
                                   scale=s.cols1[:, v_at:v_at + 1]).then_inc(S["w_hi_ok"], 1)

                def squares(t):
                    act.wait_ge(S["g_in"], 16 * (t + 1))
                    if not starts(t):
                        act.wait_ge(S["gs"], t)
                    for q in range(GROUPS):
                        ins = act.activation(junk[:, q * 256:(q + 1) * 256], g[:, q * 256:(q + 1) * 256], ACT.Square,
                                             accum_out=st4[:, 0, q:q + 1])
                        ins.then_inc(S["ssq"], 1)
                    act.wait_ge(S["ssq"], GROUPS * (t + 1))
                    act.activation(st4[:, 1, :], st4[:, 0, :], ACT.Sqrt, scale=1.0 / 256,
                                   bias=s.eps[:, 0:1]).then_inc(S["root4"], 1)

                def highs(t, n):
                    act.wait_ge(S["yp"], t + 1)
                    if not starts(t) and not (isinstance(t, int) and t == 1):
                        act.wait_ge(S["half"], 2 * (t - 1))
                    act.activation(y_hi[n][:, 0:KT, :], tiles(zp), ACT.Copy).then_inc(S["hi_p"], 1)
                    act.wait_ge(S["turn_g"], t + 1)
                    act.activation(y_hi[n][:, KT:MT, :], psG[:], ACT.Copy).then_inc(S["hi_g"], 1)

                def evacuate(t):
                    act.wait_ge(S["turn_h"], t + 1)
                    if not starts(t):
                        act.wait_ge(S["h2_out"], 16 * t)
                    for q in range(KT // 2):
                        ins = act.activation(tiles(h2t)[:, q, :], psH[:, q, :], ACT.Identity,
                                             scale=s.mod2[:, 1, q:q + 1], bias=s.mod2[:, 0, q:q + 1])
                    ins.then_inc(S["ev_a"], 1)

                def body(t, n):
                    if not ends(t):
                        squares(t + 1)
                        highs(t + 1, 1 - n)
                    if not starts(t):
                        evacuate(t - 1)
                    act.wait_ge(S["r"], 2 * (t + 1))
                    for q in range(2):
                        ins = act.activation(hn[:, q * CH:(q + 1) * CH], rt[:, q * CH:(q + 1) * CH], ACT.Square,
                                             accum_out=st1[:, q:q + 1])
                        ins.then_inc(S["sq"], 1)
                    act.wait_ge(S["sum_ok"], t + 1)
                    act.activation(st1[:, 3:4], st1[:, 2:3], ACT.Sqrt, scale=1.0 / D, bias=s.eps[:, 0:1]).then_inc(S["root"], 1)
                    act.wait_ge(S["mv"], t + 1)
                    act.activation(st1[:, 5:6], mv[:, 1:2], ACT.Sqrt, bias=s.eps[:, 1:2]).then_inc(S["root2"], 1)

                squares(0)
                highs(0, 0)
                walk_tiles(act, body)
                evacuate(LT - 1)

            @block.vector
            def _(v):
                def step(ins):
                    dve.mark(ins)
                    v.wait_ge(dve.sem, dve.value)

                v.wait_ge(S["rows_in"], 48)
                for q in range(MT):
                    b = piece[q % 4]
                    v_at = V_PSCALE + q if q < KT else V_SNORM + q - KT
                    v.wait_ge(p_in[q % 4], 16 * (q // 4 + 1))
                    v.tensor_tensor(b[:], b[:], gate[:], ALU.mult).then_inc(S["scaled"], 1)
                    v.wait_ge(S["w_hi_ok"], q + 1)
                    v.scalar_tensor_tensor(w_lo[:, q, :], b[:], s.cols1[:, v_at:v_at + 1], w_hi[:, q, :].bitcast(F32),
                                           ALU.mult, ALU.subtract).then_inc(S["w_lo_ok"], 1)

                def normed_g(t):
                    v.wait_ge(S["root4"], t + 1)
                    step(v.reciprocal(st4[:, 2, :], st4[:, 1, :]))
                    g4 = g[:].rearrange("p (q c) -> p q c", c=256)
                    v.tensor_tensor(g4, g4, st4[:, 2, :].unsqueeze(2).to_broadcast([P, GROUPS, 256]),
                                    ALU.mult).then_inc(S["gs"], 1)

                def operands(t, n):
                    v.wait_ge(S["pool"], t + 1)
                    v.wait_ge(S["zp_in"], 16 * (t + 1))
                    v.tensor_tensor(tiles(zp), psP[:], tiles(zp), ALU.mult).then_inc(S["yp"], 1)
                    v.wait_ge(S["hi_p"], t + 1)
                    v.tensor_tensor(y_lo[n][:, 0:KT, :], tiles(zp), y_hi[n][:, 0:KT, :].bitcast(F32),
                                    ALU.subtract).then_inc(S["lo_p"], 1)
                    v.wait_ge(S["hi_g"], t + 1)
                    v.tensor_tensor(y_lo[n][:, KT:MT, :], psG[:], y_hi[n][:, KT:MT, :].bitcast(F32),
                                    ALU.subtract).then_inc(S["lo_g"], 1)

                def residual(t, q):
                    v.wait_ge(S["half"], 2 * t + q + 1)
                    if q == 0:
                        v.wait_ge(S["x_in"], 16 * (t + 1))
                        if not starts(t):
                            v.wait_ge(S["x1_out"], 16 * t)
                            v.wait_ge(S["hn"], t)
                    v.tensor_tensor(rt[:, q * CH:(q + 1) * CH], psM[:, q, :], xt[:, q * CH:(q + 1) * CH],
                                    ALU.add).then_inc(S["r"], 1)

                def evacuate(t):
                    v.wait_ge(S["turn_h"], t + 1)
                    if not starts(t):
                        v.wait_ge(S["h2_out"], 16 * t)
                    for q in range(KT // 2, KT):
                        ins = v.tensor_scalar(tiles(h2t)[:, q, :], psH[:, q, :], s.mod2[:, 1, q:q + 1],
                                              s.mod2[:, 0, q:q + 1], ALU.mult, ALU.add)
                    ins.then_inc(S["ev_v"], 1)

                def body(t, n):
                    if not ends(t):
                        normed_g(t + 1)
                    residual(t, 0)
                    if not ends(t):
                        operands(t + 1, 1 - n)
                    if not starts(t):
                        evacuate(t - 1)
                    residual(t, 1)
                    v.wait_ge(S["sq"], 2 * (t + 1))
                    v.tensor_tensor(st1[:, 2:3], st1[:, 0:1], st1[:, 1:2], ALU.add).then_inc(S["sum_ok"], 1)
                    v.wait_ge(S["root"], t + 1)
                    step(v.reciprocal(st1[:, 4:5], st1[:, 3:4]))
                    v.wait_ge(S["r"], 2 * (t + 1))
                    v.scalar_tensor_tensor(rt[:], rt[:], st1[:, 4:5], fnorm[:], ALU.mult, ALU.mult).then_inc(S["x1"], 1)
                    v.wait_ge(S["x1"], t + 1)
                    v.bn_stats(bn[:, 0, :], rt[:, 0:CH])
                    step(v.bn_stats(bn[:, 1, :], rt[:, CH:D]))
                    v.memset(spare[:], 0.0)
                    v.bn_aggr(mv[:], bn[:].rearrange("p a b -> p (a b)")).then_inc(S["mv"], 1)
                    v.wait_ge(S["root2"], t + 1)
                    step(v.reciprocal(st1[:, 6:7], st1[:, 5:6]))
                    v.tensor_scalar(hn[:], rt[:], mv[:, 0:1], st1[:, 6:7], ALU.subtract, ALU.mult).then_inc(S["hn"], 1)

                normed_g(0)
                operands(0, 0)
                body(0, 0)
                with v.Fori(0, LT // 2 - 1) as i:
                    with dve.turn(i, 8, LT // 2 - 1):
                        for n in (1, 0):
                            body(2 * i + 2 - n, n)
                body(LT - 1, 1)
                evacuate(LT - 1)

            @block.tensor
            def _(pe):
                def front(t, n):
                    pe.wait_ge(S["d_in"], 16 * (t + 1))
                    if not starts(t):
                        pe.wait_ge(S["yp"], t)
                    for o in range(KT):
                        for q in range(2):
                            mm = pe.matmul(psP[:, o, :], pw[:, o // 2, q, (o % 2) * P:(o % 2 + 1) * P],
                                           tiles(dt_)[:, 2 * (o // 2) + q, :], start=(q == 0), stop=(q == 1))
                    mm.then_inc(S["pool"], 1)
                    pe.wait_ge(S["gs"], t + 1)
                    if not starts(t):
                        pe.wait_ge(S["lo_g"], t)
                    for q in range(KT):
                        mm = pe.transpose(psG[:, q, :], g[:, q * P:(q + 1) * P], s.ident[:])
                    mm.then_inc(S["turn_g"], 1)

                def turned_norm(t):
                    pe.wait_ge(S["hn"], t + 1)
                    if not starts(t):
                        pe.wait_ge(S["ev_a"], t)
                        pe.wait_ge(S["ev_v"], t)
                    for q in range(KT):
                        mm = pe.transpose(psH[:, q, :], hn[:, q * P:(q + 1) * P], s.ident[:])
                    mm.then_inc(S["turn_h"], 1)

                def half(t, n, h):
                    if h == 0:
                        pe.wait_ge(S["lo_g"], t + 1)
                    if not starts(t):
                        pe.wait_ge(S["r"], 2 * t + h - 1)
                    for q in range(MT):
                        for j, (y, w) in enumerate(((y_hi, w_hi), (y_hi, w_lo), (y_lo, w_hi))):
                            mm = pe.matmul(psM[:, h, :], y[n][:, q, :], w[:, q, h * CH:(h + 1) * CH],
                                           start=(q == 0 and j == 0), stop=(q == MT - 1 and j == 2))
                    mm.then_inc(S["half"], 1)

                def body(t, n):
                    half(t, n, 0)
                    if not ends(t):
                        front(t + 1, 1 - n)
                    if not starts(t):
                        turned_norm(t - 1)
                    half(t, n, 1)

                pe.wait_ge(S["rows_in"], 48)
                front(0, 0)
                pe.wait_ge(S["w_lo_ok"], MT)
                walk_tiles(pe, body)
                turned_norm(LT - 1)


def split_h2(nc, kit, a, hT):
    hi, lo = hT
    with ExitStack() as ctx:
        h = [kit.sbuf(ctx, f"h2_raw{n}", [P, SEQ]) for n in range(2)]
        ld = [kit.sem(f"h2_loaded{n}") for n in range(2)]
        hi_ok, lo_ok = kit.sem("h2_hi_ready"), kit.sem("h2_lo_ready")
        with nc.Block() as block:
            @block.sync
            def _(sp):
                for q in range(KT):
                    if q >= 2:
                        sp.wait_ge(lo_ok, q - 1)
                    sp.dma_start(h[q % 2][:], a["h2T"][q]).then_inc(ld[q % 2], 16)

            @block.scalar
            def _(act):
                for q in range(KT):
                    act.wait_ge(ld[q % 2], 16 * (q // 2 + 1))
                    act.activation(hi[:, q, :], h[q % 2][:], ACT.Copy).then_inc(hi_ok, 1)

            @block.vector
            def _(v):
                for q in range(KT):
                    v.wait_ge(hi_ok, q + 1)
                    v.tensor_tensor(lo[:, q, :], h[q % 2][:], hi[:, q, :].bitcast(F32), ALU.subtract).then_inc(lo_ok, 1)


def projection2(nc, kit, a, s):
    with ExitStack() as ctx:
        hT = (kit.sbuf(ctx, "h2T_hi", [P, KT, SEQ], F32R), kit.sbuf(ctx, "h2T_lo", [P, KT, SEQ], F32R))
        split_h2(nc, kit, a, hT)
        kinds = [
            Kind(XR0, 4, 4, "conv", stored=a["xcT"]),
            Kind(ZR0, 4, 4, "copy", stored=a["zrT"], func=ACT.Silu),
            Kind(QK0, 8, 4, "copy", stored=a["qkT"]),
            Kind(VZ0, 8, 4, "copy", turned=a["va_tok"]),
            Kind(FL0, 1, 4, "copy", stored=a["flT"], width=NH2),
        ]
        conv = Conv(s.cols2, V2_CONVW, V2_CONVB, 4, {XR0: 0}, 3, SEQ, ACT.Identity)
        plan = [("one", b) for b in range(10)] + [("loop", 10, 3), ("one", 16), ("one", 17), ("loop", 18, 2)] + \
               [("one", b) for b in range(22, NBLK2)]
        project(nc, kit, a, s, "p2", kinds, plan, hT, a["w_in_2"], conv, False)


def lru(nc, kit, a, s):
    NT = W2 // P
    with ExitStack() as ctx:
        sb = lambda *args: kit.sbuf(ctx, *args)
        xc, rr, ii, rt, zr = (sb(f"l_{n}", [P, NT, SEQ]) for n in ("xc", "gate_a", "gate_x", "root", "zr"))
        inv = [sb(f"l_inv{n}", [P, SEQ]) for n in range(2)]
        dec = [sb(f"l_decay{n}", [P, SEQ]) for n in range(2)]
        wg = sb("l_gate_w", [P, 2, NT, P])
        sp_t = [sb(f"l_sp{n}", [P, NT]) for n in range(3)]
        lam, halfc = sb("l_neg_lambda", [P, NT]), sb("l_half_c", [P, NT])
        ones = sb("l_ones", [P, 2])
        ms = sb("l_mean_square", [P, 2, LT])
        ps = kit.psum(ctx, "l_ps", [P, 4, CH])
        psQ = kit.psum(ctx, "l_psQ", [P, LT, 2])
        k = kit
        S = k.sems("l_", ("w_zero", "w_in", "gate", "sig", "ask", "exp", "halfc", "tanh", "root", "ix", "u", "h",
                          "sq", "hz", "out", "sum", "rms"))
        x_in, z_in = [k.sem(f"l_x_loaded{n}") for n in range(NT)], k.sem("l_z_loaded")
        dve = Tally(k.sem("l_dve_chain"))
        with nc.Block() as block:
            @block.sync
            def _(sp):
                for q in range(NT):
                    sp.dma_start(xc[:, q, :], a["xcT"][q]).then_inc(x_in[q], 16)
                sp.wait_ge(S["w_zero"], 1)
                for g, w in enumerate((a["w_gate_a"], a["w_gate_x"])):
                    wb = w.rearrange("(t h) d e -> h d t e", h=2)
                    for h in range(2):
                        sp.dma_start(wg[h * 64:(h + 1) * 64, g, :, h * 64:(h + 1) * 64], wb[h]).then_inc(S["w_in"], 16)
                sp.dma_start(zr[:], a["zrT"].rearrange("k p n -> p k n")).then_inc(z_in, 16)
                for q in range(NT):
                    sp.wait_ge(S["hz"], q + 1)
                    sp.dma_start(a["hzT"][q], zr[:, q, :]).then_inc(S["out"], 16)
                sp.wait_ge(S["out"], 16 * NT)

            @block.tensor
            def _(pe):
                pe.wait_ge(S["w_in"], 64)
                for q in range(NT):
                    pe.wait_ge(x_in[q], 16)
                    for g in range(2):
                        for c in range(4):
                            m = (2 * q + g) * 4 + c
                            if m >= 4:
                                pe.wait_ge(S["sig"], m - 3)
                            pe.matmul(ps[:, c, :], wg[:, g, q, :], xc[:, q, c * CH:(c + 1) * CH], start=True,
                                      stop=True).then_inc(S["gate"], 1)
                pe.wait_ge(S["sq"], NT)
                for t in range(LT):
                    for q in range(NT):
                        mm = pe.matmul(psQ[:, t, :], rr[:, q, t * P:(t + 1) * P], ones[:], start=(q == 0),
                                       stop=(q == NT - 1))
                mm.then_inc(S["sum"], 1)

            @block.scalar
            def _(act):
                act.wait_ge(S["ask"], 1)
                act.activation(sp_t[0][:], sp_t[0][:], ACT.Exp).then_inc(S["exp"], 1)
                for q in range(NT):
                    for g, (dst, at) in enumerate(((rr, V2_BA), (ii, V2_BX))):
                        for c in range(4):
                            act.wait_ge(S["gate"], (2 * q + g) * 4 + c + 1)
                            act.activation(dst[:, q, c * CH:(c + 1) * CH], ps[:, c, :], ACT.Sigmoid,
                                           bias=s.cols2[:, at + q:at + q + 1]).then_inc(S["sig"], 1)
                act.wait_ge(S["halfc"], 1)
                act.wait_ge(S["sig"], 32)
                for q in range(NT):
                    act.activation(rr[:, q, :], rr[:, q, :], ACT.Tanh, scale=halfc[:, q:q + 1]).then_inc(S["tanh"], 1)
                for q in range(NT):
                    act.wait_ge(S["tanh"], q + 1)
                    act.activation(rt[:, q, :], rr[:, q, :], ACT.Sqrt).then_inc(S["root"], 1)
                for q in range(NT):
                    act.wait_ge(S["h"], q + 1)
                    act.activation(rr[:, q, :], xc[:, q, :], ACT.Square).then_inc(S["sq"], 1)
                act.wait_ge(S["sum"], 1)
                act.activation(ms[:, 0, :], psQ[:, :, 0], ACT.Sqrt, scale=1.0 / W2, bias=s.eps[:, 1:2]).then_inc(S["rms"], 1)

            @block.gpsimd
            def _(g):
                g.memset(wg[:], 0.0).then_inc(S["w_zero"], 1)
                for q in range(NT):
                    g.wait_ge(S["sig"], 8 * (q + 1))
                    g.tensor_tensor(ii[:, q, :], ii[:, q, :], xc[:, q, :], ALU.mult).then_inc(S["ix"], 1)

            @block.vector
            def _(v):
                def step(ins):
                    dve.mark(ins)
                    v.wait_ge(dve.sem, dve.value)

                def ask():
                    v.nop().then_inc(S["ask"], 1)
                    v.wait_ge(S["exp"], 1)

                step(v.memset(ones[:], 1.0))
                step(v.tensor_scalar(lam[:], s.cols2[:, V2_LAM:V2_LAM + NT], -1.0, None, ALU.mult))
                softplus(v, step, ask, halfc[:], lam[:], [t[:] for t in sp_t])
                v.tensor_scalar(halfc[:], halfc[:], LRU_C / 2, None, ALU.mult).then_inc(S["halfc"], 1)
                for q in range(NT):
                    iv, de = inv[q % 2], dec[q % 2]
                    v.wait_ge(S["tanh"], q + 1)
                    step(v.tensor_scalar(iv[:], rr[:, q, :], 1.0, None, ALU.add))
                    step(v.reciprocal(iv[:], iv[:]))
                    step(v.tensor_scalar(de[:], iv[:], 2.0, -1.0, ALU.mult, ALU.add))
                    v.wait_ge(S["root"], q + 1)
                    step(v.scalar_tensor_tensor(iv[:], rt[:, q, :], 2.0, iv[:], ALU.mult, ALU.mult))
                    v.wait_ge(S["ix"], q + 1)
                    step(v.tensor_tensor(ii[:, q, :], ii[:, q, :], iv[:], ALU.mult))
                    v.tensor_tensor_scan(xc[:, q, :], de[:], ii[:, q, :], 0.0, ALU.mult, ALU.add).then_inc(S["h"], 1)
                    v.wait_ge(S["h"], q + 1)
                    v.wait_ge(z_in, 16)
                    v.tensor_tensor(zr[:, q, :], zr[:, q, :], xc[:, q, :], ALU.mult).then_inc(S["hz"], 1)
                v.wait_ge(S["rms"], 1)
                v.reciprocal(s.rstd_r[:], ms[:, 0, :])


def forget_sums(nc, kit, a, s):
    with ExitStack() as ctx:
        sb = lambda *args: kit.sbuf(ctx, *args)
        x, out = sb("f_x", [P, P]), sb("f_out", [P, P])
        t = [sb(f"f_sp{n}", [P, P]) for n in range(3)]
        b = sb("f_bias", [P, 1])
        rows, one, sums = sb("f_rows", [NH2, SEQ]), sb("f_ones", [NH2, SEQ]), sb("f_sums", [NH2, SEQ])
        scaled = [sb(f"f_scaled{n}", [NH2, SEQ]) for n in range(2)]
        S = kit.sems("f_", ("fl_in", "ask", "exp", "soft", "soft_out", "rows_in", "sums", "out"))
        dve = Tally(kit.sem("f_dve_chain"))
        with nc.Block() as block:
            @block.sync
            def _(sp):
                sp.dma_start(x[:], a["flT"].rearrange("o h (s l) -> (o h s) l", l=P)).then_inc(S["fl_in"], 16)
                sp.dma_start(b[:], a["b_fgate"]).then_inc(S["fl_in"], 16)
                sp.wait_ge(S["soft"], 1)
                sp.dma_start(a["softf"], out[:]).then_inc(S["soft_out"], 16)
                sp.wait_ge(S["soft_out"], 16)
                sp.dma_start(rows[:], a["softf"].rearrange("(h s) l -> h (s l)", h=NH2)).then_inc(S["rows_in"], 16)
                sp.wait_ge(S["sums"], 2)
                for n in range(2):
                    sp.dma_start(a["forget"][n], scaled[n][:]).then_inc(S["out"], 16)
                sp.wait_ge(S["out"], 32)

            @block.scalar
            def _(act):
                act.wait_ge(S["ask"], 1)
                act.activation(t[0][:], t[0][:], ACT.Exp).then_inc(S["exp"], 1)

            @block.vector
            def _(v):
                def step(ins):
                    dve.mark(ins)
                    v.wait_ge(dve.sem, dve.value)

                def ask():
                    v.nop().then_inc(S["ask"], 1)
                    v.wait_ge(S["exp"], 1)

                step(v.memset(one[:], 1.0))
                v.wait_ge(S["fl_in"], 32)
                step(v.tensor_scalar(x[:], x[:], b[:], -1.0, ALU.add, ALU.mult))
                softplus(v, step, ask, out[:], x[:], [q[:] for q in t])
                v.nop().then_inc(S["soft"], 1)
                v.wait_ge(S["rows_in"], 16)
                step(v.tensor_tensor_scan(sums[:], one[:], rows[:], 0.0, ALU.mult, ALU.add))
                for n, c in enumerate((-8.0, 8.0)):
                    v.tensor_scalar(scaled[n][:], sums[:], c, None, ALU.mult).then_inc(S["sums"], 1)


def attention(nc, kit, a, s, y):
    KD, VD = HD2 + 2, HD2 + 1
    QT = SEQ // P
    groups = [j // 4 + 1 for j in range(QT)]
    before = [sum(groups[:j]) for j in range(QT + 1)]
    GH = before[QT]
    with ExitStack() as ctx:
        sb = lambda *args: kit.sbuf(ctx, *args)
        qa = [sb(f"t_q{n}", [KD, SEQ]) for n in range(2)]
        ka = [sb(f"t_k{n}", [KD, SEQ]) for n in range(2)]
        va = [sb(f"t_v{n}", [P, QT, VD + 1]) for n in range(2)]
        pr = [sb(f"t_prob{n}", [P, SEQ]) for n in range(2)]
        pt = [sb(f"t_prob_turned{n}", [P, QT, P]) for n in range(2)]
        causal = sb("t_causal", [P, P])
        mx, top = sb("t_chunk_max", [P, 4]), sb("t_max", [P, 4])
        psS = kit.psum(ctx, "t_psS", [P, 4, CH])
        psT = kit.psum(ctx, "t_psT", [P, 3, 4, P])
        psO = kit.psum(ctx, "t_psO", [P, VD])
        S = kit.sems("t_", ("ones", "mask_in", "chunk", "max", "prob", "turned", "turned_out", "o", "y"))
        ld = [kit.sem(f"t_loaded{n}") for n in range(2)]
        dve = Tally(kit.sem("t_dve_chain"))
        NP = NH2 // 2

        def walk(eng, head):
            with eng.Fori(0, NP - 1) as i:
                for n in range(2):
                    head(2 * i + n, i, n, False)
            for n in range(2):
                head(NH2 - 2 + n, NP - 1, n, n == 1)

        with nc.Block() as block:
            @block.sync
            def _(sp):
                sp.dma_start(causal[:], a["causal"]).then_inc(S["mask_in"], 16)
                heads = a["qkT"].rearrange("b (h d) n -> (b h) d n", d=HD2)
                va_heads = a["va_tok"].rearrange("(t p) (h d) -> h p t d", p=P, d=HD2)

                def load(h, n):
                    sp.dma_start(qa[n][0:HD2, :], heads[h]).then_inc(ld[n], 16)
                    sp.dma_start(ka[n][0:HD2, :], heads[h + NH2]).then_inc(ld[n], 16)
                    sp.dma_start(qa[n][HD2 + 1:HD2 + 2, :], row(a["forget"][0], h)).then_inc(ld[n], 16)
                    sp.dma_start(ka[n][HD2:HD2 + 1, :], row(a["forget"][1], h)).then_inc(ld[n], 16)
                    sp.dma_start(va[n][:, :, 0:HD2], va_heads[h]).then_inc(ld[n], 16)

                def row(t, h):
                    return t[h:h + 1, :] if isinstance(h, int) else t[bass.ds(h, 1), :]

                sp.wait_ge(S["ones"], 1)
                load(0, 0)
                load(1, 1)
                with sp.Fori(0, NP - 1) as i:
                    for n in range(2):
                        sp.wait_ge(S["y"], (2 * i + n + 1) * QT + 1)
                        load(2 * i + n + 2, n)

            @block.tensor
            def _(pe):
                def logits(h, i, n, j):
                    if j == 0:
                        pe.wait_ge(ld[n], 80 * (i + 1))
                    pe.wait_ge(S["prob"], h * QT + j + 1)
                    for c in range(groups[j]):
                        w = min(CH, (j + 1) * P - c * CH)
                        pe.matmul(psS[:, c, 0:w], qa[n][:, j * P:(j + 1) * P], ka[n][:, c * CH:c * CH + w],
                                  start=True, stop=True).then_inc(S["chunk"], 1)

                def turn(h, n, j, g):
                    pe.wait_ge(S["turned_out"], h * GH + before[j] + max(0, g - 2) + 1)
                    for q in range(4 * g, min(4 * g + 4, j + 1)):
                        mm = pe.transpose(psT[:, g % 3, q % 4, :],
                                          pr[j % 2][:, q * P:(q + 1) * P], s.ident[:])
                    mm.then_inc(S["turned"], 1)

                def apply(h, n, j, g):
                    if g == 0:
                        pe.wait_ge(S["y"], h * QT + j + 1)
                    pe.wait_ge(S["turned_out"], h * GH + before[j] + g + 2)
                    for q in range(4 * g, min(4 * g + 4, j + 1)):
                        mm = pe.matmul(psO[:], pt[j % 2][:, q, :], va[n][:, q, 0:VD], start=(q == 0), stop=(q == j))
                    if g == groups[j] - 1:
                        mm.then_inc(S["o"], 1)

                def head(h, i, n, last):
                    for j in range(QT):
                        if j < QT - 1:
                            logits(h, i, n, j + 1)
                        elif not last:
                            logits(h + 1, i + n, 1 - n, 0)
                        pe.wait_ge(S["prob"], h * QT + j + 2)
                        for g in range(min(3, groups[j])):
                            turn(h, n, j, g)
                        for g in range(groups[j]):
                            apply(h, n, j, g)
                            if g + 3 < groups[j]:
                                turn(h, n, j, g + 3)

                logits(0, 0, 0, 0)
                walk(pe, head)

            @block.scalar
            def _(act):
                act.nop().then_inc(S["prob"], 1)

                def head(h, i, n, last):
                    for j in range(QT):
                        act.wait_ge(S["max"], h * QT + j + 1)
                        w = (j + 1) * P
                        act.activation(pr[j % 2][:, 0:w], psS[:].rearrange("p c n -> p (c n)")[:, 0:w], ACT.Exp,
                                       scale=1.0 / 8, bias=top[:, 1:2]).then_inc(S["prob"], 1)
                walk(act, head)

            @block.vector
            def _(v):
                def step(ins):
                    dve.mark(ins)
                    v.wait_ge(dve.sem, dve.value)

                def maxima(h, j):
                    for c in range(groups[j]):
                        v.wait_ge(S["chunk"], h * GH + before[j] + c + 1)
                        w = min(CH, (j + 1) * P - c * CH)
                        if c == groups[j] - 1:
                            d = psS[:, c, w - P:w]
                            step(v.tensor_tensor(d, d, causal[:], ALU.add))
                        ins = v.reduce_max(mx[:, c:c + 1], psS[:, c, 0:w], axis=AX_X)
                    step(ins)
                    step(v.reduce_max(top[:, 0:1], mx[:, 0:groups[j]], axis=AX_X))
                    v.tensor_scalar(top[:, 1:2], top[:, 0:1], -1.0 / 8, None, ALU.mult).then_inc(S["max"], 1)

                def read_turned(h, j):
                    for g in range(groups[j]):
                        v.wait_ge(S["turned"], h * GH + before[j] + g + 1)
                        cnt = min(4, j + 1 - 4 * g)
                        v.tensor_copy(pt[j % 2][:, 4 * g:4 * g + cnt, :],
                                      psT[:, g % 3, 0:cnt, :]).then_inc(S["turned_out"], 1)

                def normal(h, j):
                    v.wait_ge(S["o"], h * QT + j + 1)
                    step(v.reciprocal(top[:, 2:3], psO[:, HD2:HD2 + 1]))
                    dst = y[:, j, h * HD2:(h + 1) * HD2] if isinstance(h, int) else y[:, j, bass.ds(h * HD2, HD2)]
                    v.tensor_scalar(dst, psO[:, 0:HD2], top[:, 2:3], None, ALU.mult).then_inc(S["y"], 1)

                def head(h, i, n, last):
                    for j in range(QT):
                        if j < QT - 1:
                            maxima(h, j + 1)
                        elif not last:
                            maxima(h + 1, 0)
                        read_turned(h, j)
                        normal(h, j)

                for n in range(2):
                    step(v.memset(qa[n][HD2:HD2 + 2, :], 1.0))
                    step(v.memset(ka[n][HD2:HD2 + 2, :], 1.0))
                    step(v.memset(va[n][:, :, HD2:HD2 + 1], 1.0))
                v.nop().then_inc(S["ones"], 1)
                v.nop().then_inc(S["turned_out"], 1)
                v.nop().then_inc(S["y"], 1)
                v.wait_ge(S["mask_in"], 16)
                maxima(0, 0)
                with v.Fori(0, NP - 1) as i:
                    with dve.turn(i, 8 * QT, NP - 1):
                        for n in range(2):
                            head(2 * i + n, i, n, False)
                for n in range(2):
                    head(NH2 - 2 + n, NP - 1, n, n == 1)


def out2(nc, kit, a, s, y):
    NT = W2 // P
    with ExitStack() as ctx:
        sb = lambda *args: kit.sbuf(ctx, *args)
        w_hi, w_lo = sb("o_w_hi", [P, 2 * NT, D], F32R), sb("o_w_lo", [P, 2 * NT, D], F32R)
        gate, gain, bias = (sb(f"o_{n}", [P, D]) for n in ("gate", "gain", "bias"))
        piece = [sb(f"o_piece{n}", [P, D]) for n in range(2)]
        za = sb("o_za", [P, LT, W2])
        junk = sb("o_junk", [P, W2], mybir.dt.bfloat16)
        ms = sb("o_mean_square", [P, 3, LT])
        ga = [sb(f"o_gated{n}", [P, W2]) for n in range(2)]
        hz = [sb(f"o_hz{n}", [P, NT, P]) for n in range(2)]
        x = [sb(f"o_x{n}", [P, D]) for n in range(2)]
        yh = [sb(f"o_y_hi{n}", [P, 2 * NT, P], F32R) for n in range(2)]
        yl = [sb(f"o_y_lo{n}", [P, 2 * NT, P], F32R) for n in range(2)]
        spare = sb("o_spare", [P, 1])
        bn, mv, st = sb("o_bn", [P, 2, 6]), sb("o_mv", [P, 2]), sb("o_st", [P, 2])
        psA, psR = (kit.psum(ctx, f"o_ps{n}", [P, 2, CH]) for n in "AR")
        psG = [kit.psum(ctx, f"o_psG{n}", [P, NT, P]) for n in range(2)]
        S = kit.sems("o_", ("rows_in", "scaled", "w_hi", "w_lo", "za_in", "za", "sq", "root", "ya", "turn", "hi_r",
                            "hi_a", "lo_r", "lo_a", "prod", "res", "mv", "root2", "norm", "y"))
        p_in, hz_in, x_in, out = ([kit.sem(f"o_{m}{n}") for n in range(2)] for m in
                                  ("piece_loaded", "hz_loaded", "x_loaded", "stored"))
        dve = Tally(kit.sem("o_dve_chain"))
        half = LT // 2

        def walk(eng, body, tally=None, per=0):
            for n in range(2):
                body(n, 0, n)
            with eng.Fori(1, half - 1) as i:
                if tally is None:
                    for n in range(2):
                        body(2 * i + n, i, n)
                else:
                    with tally.turn(i - 1, 2 * per, half - 2):
                        for n in range(2):
                            body(2 * i + n, i, n)
            for n in range(2):
                body(LT - 2 + n, half - 1, n)

        def late(t):
            return not isinstance(t, int) or t >= 2

        with nc.Block() as block:
            @block.sync
            def _(sp):
                for dst, src in ((gate[:], a["gate_rows"][:, D:2 * D]), (gain[:], a["ln_gain"].partition_broadcast(P)),
                                 (bias[:], a["ln_bias"].partition_broadcast(P))):
                    sp.dma_start(dst, src).then_inc(S["rows_in"], 16)
                for q in range(2 * NT):
                    if q >= 2:
                        sp.wait_ge(S["w_lo"], q - 1)
                    sp.dma_start(piece[q % 2][:], a["w_out_2"][:, q, :]).then_inc(p_in[q % 2], 16)

                def load(t, n):
                    sp.dma_start(hz[n][:], cols_at(a["hzT"], t)).then_inc(hz_in[n], 16)
                    sp.dma_start(x[n][:], rows_at(a["x1"], t)).then_inc(x_in[n], 16)

                load(0, 0)
                load(1, 1)

                def body(t, i, n):
                    sp.wait_ge(S["y"], t + 1)
                    sp.dma_start(rows_at(a["out"], t), x[n][:]).then_inc(out[n], 16)
                    if not isinstance(t, int) or t < LT - 2:
                        sp.wait_ge(out[n], 16 * (i + 1))
                        load(t + 2, n)
                walk(sp, body)
                for n in range(2):
                    sp.wait_ge(out[n], 16 * half)

            @block.gpsimd
            def _(g):
                g.dma_start(za[:], a["va_tok"].rearrange("(t p) c -> p t c", p=P)[:, :, W2:2 * W2]).then_inc(S["za_in"], 16)

                def body(t, i, n):
                    g.wait_ge(S["norm"], t + 1)
                    g.tensor_tensor(x[n][:], x[n][:], bias[:], ALU.add).then_inc(S["y"], 1)
                g.wait_ge(S["rows_in"], 48)
                walk(g, body)

            @block.scalar
            def _(act):
                for q in range(2 * NT):
                    v_at = V2_NLRU + q
                    act.wait_ge(S["scaled"], q + 1)
                    act.activation(w_hi[:, q, :], piece[q % 2][:], ACT.Copy,
                                   scale=s.cols2[:, v_at:v_at + 1]).then_inc(S["w_hi"], 1)
                for t in range(LT):
                    ins = act.activation(junk[:], y[:, t, :], ACT.Square, accum_out=ms[:, 0, t:t + 1])
                    ins.then_inc(S["sq"], 1)
                    act.wait_ge(S["sq"], t + 1)
                act.wait_ge(S["za_in"], 16)
                for q in range(4):
                    act.activation(za[:, 4 * q:4 * q + 4, :], za[:, 4 * q:4 * q + 4, :], ACT.Silu).then_inc(S["za"], 1)
                act.activation(ms[:, 1, :], ms[:, 0, :], ACT.Sqrt, scale=1.0 / W2, bias=s.eps[:, 1:2]).then_inc(S["root"], 1)

                def highs(t, i, n):
                    act.wait_ge(hz_in[n], 16 * (i + 1))
                    if late(t):
                        act.wait_ge(S["prod"], 2 * (t - 1))
                    act.activation(yh[n][:, 0:NT, :], hz[n][:], ACT.Copy).then_inc(S["hi_r"], 1)
                    act.wait_ge(S["turn"], t + 1)
                    act.activation(yh[n][:, NT:2 * NT, :], psG[n][:], ACT.Copy).then_inc(S["hi_a"], 1)

                def body(t, i, n):
                    if not ends(t):
                        highs(t + 1, i + n, 1 - n)
                    act.wait_ge(S["mv"], t + 1)
                    act.activation(st[:, 0:1], mv[:, 1:2], ACT.Sqrt, bias=s.eps[:, 1:2]).then_inc(S["root2"], 1)
                highs(0, 0, 0)
                walk(act, body)

            @block.vector
            def _(v):
                def step(ins):
                    dve.mark(ins)
                    v.wait_ge(dve.sem, dve.value)

                v.wait_ge(S["rows_in"], 48)
                for q in range(2 * NT):
                    b, v_at = piece[q % 2], V2_NLRU + q
                    v.wait_ge(p_in[q % 2], 16 * (q // 2 + 1))
                    v.tensor_tensor(b[:], b[:], gate[:], ALU.mult).then_inc(S["scaled"], 1)
                    v.wait_ge(S["w_hi"], q + 1)
                    v.scalar_tensor_tensor(w_lo[:, q, :], b[:], s.cols2[:, v_at:v_at + 1], w_hi[:, q, :].bitcast(F32),
                                           ALU.mult, ALU.subtract).then_inc(S["w_lo"], 1)
                v.wait_ge(S["za"], 4)
                v.wait_ge(S["root"], 1)
                step(v.reciprocal(ms[:, 2, :], ms[:, 1, :]))

                def gated(t, n):
                    if late(t):
                        v.wait_ge(S["turn"], t - 1)
                    v.scalar_tensor_tensor(ga[n][:], y[:, t, :], ms[:, 2, t:t + 1] if isinstance(t, int) else ms[:, 2, bass.ds(t, 1)],
                                           za[:, t, :], ALU.mult, ALU.mult).then_inc(S["ya"], 1)

                def lows(t, i, n):
                    for m, (hi_ok, lo_ok, src) in enumerate(((S["hi_r"], S["lo_r"], hz[n]), (S["hi_a"], S["lo_a"], psG[n]))):
                        v.wait_ge(hi_ok, t + 1)
                        v.tensor_tensor(yl[n][:, m * NT:(m + 1) * NT, :], src[:],
                                        yh[n][:, m * NT:(m + 1) * NT, :].bitcast(F32), ALU.subtract).then_inc(lo_ok, 1)

                def body(t, i, n):
                    if not isinstance(t, int) or t < LT - 2:
                        gated(t + 2, n)
                    if not ends(t):
                        lows(t + 1, i + n, 1 - n)
                    v.wait_ge(x_in[n], 16 * (i + 1))
                    v.wait_ge(S["prod"], 2 * (t + 1))
                    step(v.scalar_tensor_tensor(x[n][:], x[n][:], ALPHA, psA[:].rearrange("p h c -> p (h c)"),
                                                ALU.mult, ALU.add))
                    r1 = s.rstd_r[:, t:t + 1] if isinstance(t, int) else s.rstd_r[:, bass.ds(t, 1)]
                    v.scalar_tensor_tensor(x[n][:], psR[:].rearrange("p h c -> p (h c)"), r1, x[n][:], ALU.mult,
                                           ALU.add).then_inc(S["res"], 1)
                    v.wait_ge(S["res"], t + 1)
                    v.bn_stats(bn[:, 0, :], x[n][:, 0:CH])
                    step(v.bn_stats(bn[:, 1, :], x[n][:, CH:D]))
                    v.memset(spare[:], 0.0)
                    v.bn_aggr(mv[:], bn[:].rearrange("p a b -> p (a b)")).then_inc(S["mv"], 1)
                    v.wait_ge(S["root2"], t + 1)
                    step(v.reciprocal(st[:, 1:2], st[:, 0:1]))
                    step(v.tensor_scalar(x[n][:], x[n][:], mv[:, 0:1], st[:, 1:2], ALU.subtract, ALU.mult))
                    v.tensor_tensor(x[n][:], x[n][:], gain[:], ALU.mult).then_inc(S["norm"], 1)

                gated(0, 0)
                gated(1, 1)
                lows(0, 0, 0)
                for n in range(2):
                    body(n, 0, n)
                with v.Fori(1, half - 1) as i:
                    with dve.turn(i - 1, 8, half - 2):
                        for n in range(2):
                            body(2 * i + n, i, n)
                for n in range(2):
                    body(LT - 2 + n, half - 1, n)

            @block.tensor
            def _(pe):
                def turn(t, n):
                    pe.wait_ge(S["ya"], t + 1)
                    if late(t):
                        pe.wait_ge(S["lo_a"], t - 1)
                    for q in range(NT):
                        mm = pe.transpose(psG[n][:, q, :], ga[n][:, q * P:(q + 1) * P], s.ident[:])
                    mm.then_inc(S["turn"], 1)

                def body(t, i, n):
                    if not ends(t):
                        turn(t + 1, 1 - n)
                    pe.wait_ge(S["lo_r"], t + 1)
                    pe.wait_ge(S["lo_a"], t + 1)
                    if not starts(t):
                        pe.wait_ge(S["res"], t)
                    for m, acc in enumerate((psR, psA)):
                        for h in range(2):
                            for q in range(m * NT, (m + 1) * NT):
                                for j, (yy, w) in enumerate(((yh, w_hi), (yh, w_lo), (yl, w_hi))):
                                    mm = pe.matmul(acc[:, h, :], yy[n][:, q, :], w[:, q, h * CH:(h + 1) * CH],
                                                   start=(q == m * NT and j == 0), stop=(q == (m + 1) * NT - 1 and j == 2))
                        mm.then_inc(S["prod"], 1)

                turn(0, 0)
                pe.wait_ge(S["w_lo"], 2 * NT)
                walk(pe, body)


def packed(inputs):
    i = {k: np.asarray(v) for k, v in inputs.items()}
    tiles = lambda v: np.ascontiguousarray(v.reshape(-1, P).T)

    def rows(w):
        return w.reshape(-1, P, w.shape[1]).transpose(1, 0, 2)

    def blocks(w, width):
        return np.ascontiguousarray(rows(w).reshape(P, -1, w.shape[1] // width, width).transpose(2, 0, 1, 3))

    w1, w2 = i["w_in"][0], i["w_in_2"][0]
    pad = lambda w: np.concatenate([w, np.zeros((w.shape[0], P - w.shape[1]), w.dtype)], 1)
    w_in = np.concatenate([w1[:, 3072:5120], pad(w1[:, 5120:]), w1[:, 2048:3072], w1[:, 1024:2048], w1[:, 0:1024]], 1)
    w_in_2 = np.concatenate([w2[:, :3072], pad(w2[:, 3072:])], 1)
    ada1, ada2 = i["w_ada"][0], i["w_ada_2"][0]
    wada = np.concatenate([ada1[:, :2 * D], ada2[:, :2 * D], ada1[:, 2 * D:], ada2[:, 2 * D:]], 1)
    c3 = np.stack([i["c"][0], i["c_ctx"], i["c_2"][0]], 1)
    cols1 = np.concatenate([tiles(v) for v in (i["b_ada"][0], i["norm_w"][0], i["conv_b"][0], i["conv_w"][0],
                                               i["pool_scale"][0], i["ssd_norm_w"][0])], 1)
    cols2 = np.concatenate([tiles(v) for v in (i["b_ada_2"][0], i["conv_w_2"][0], i["conv_b_2"][0],
                                               i["b_gate_a_2"][0], i["b_gate_x_2"][0], i["lru_lambda_2"][0],
                                               i["norm_lru_2"][0], i["norm_attn_2"][0])], 1)
    f = np.float32
    r = np.arange(P)
    def inv_count(n, w):
        t = np.arange(n)
        return 1.0 / (np.minimum(t + w - w // 2, n) - np.maximum(t - w // 2, 0))
    inv = np.stack([np.outer(inv_count(GRID_R, w), inv_count(GRID_C, w)).reshape(-1) for w in WINDOWS]).astype(f)
    upper = (r[:, None] <= r[None, :]).astype(f)
    return {
        "x": i["x"][0], "ctx": i["ctx"][0], "cols1": cols1, "cols2": cols2, "ident": np.eye(P, dtype=f),
        "c3": np.ascontiguousarray(c3.reshape(KT, P, 3).transpose(1, 0, 2)),
        "wada": blocks(wada, 256), "gate_bias": np.concatenate([i["b_ada"][0, 2 * D:], i["b_ada_2"][0, 2 * D:]]).reshape(8, 256),
        "w_in": blocks(w_in, P), "w_in_2": blocks(w_in_2, P), "inv_count": inv,
        "sel_last": np.outer(r == P - 1, np.ones(P)).astype(f), "sel_first": np.outer(r == 0, np.ones(P)).astype(f),
        "keep_fwd": np.tile((np.arange(TOK) % P != 0).astype(f), (HEADS, 1)),
        "keep_bwd": np.tile((np.arange(TOK) % P != P - 1).astype(f), (HEADS, 1)),
        "upper": upper, "lower": np.ascontiguousarray(upper.T),
        "causal": ((upper.T - 1) * 1e30).astype(f),
        "dt_bias": i["dt_bias"][0].reshape(1, NDH), "a_log": i["a_log"][0].reshape(1, NDH),
        "d_skip": i["d_skip"][0].reshape(1, HEADS),
        "pool_w": np.ascontiguousarray(i["pool_w"][0].reshape(4, 2, P, 256).transpose(2, 0, 1, 3)),
        "w_out": np.ascontiguousarray(rows(i["w_out"][0])), "final_norm": i["final_norm_w"].reshape(1, D),
        "b_fgate": np.repeat(i["b_fgate_2"][0], P // NH2).reshape(P, 1),
        "w_gate_a": i["w_gate_a_2"][0], "w_gate_x": i["w_gate_x_2"][0],
        "w_out_2": np.ascontiguousarray(rows(i["w_out_2"][0])),
        "ln_gain": i["ln_gain_2"][0].reshape(1, D), "ln_bias": i["ln_bias_2"][0].reshape(1, D),
    }


SCRATCH = {"gate_rows": [P, 2 * D],
           "xs_tok": [TOK, W_HALF], "b_tok": [TOK, GROUPS * NS], "z_tok": [SEQ, W_HALF], "dt_tok": [TOK, NDH],
           "bT": [4, P, SEQ], "cT": [4, P, SEQ], "zpT": [8, P, SEQ], "dT": [8, P, SEQ],
           "acum_rows": [TT, NDH, P], "g_tok": [SEQ, W_HALF],
           "x1": [SEQ, D], "h2T": [KT, P, SEQ],
           "xcT": [4, P, SEQ], "zrT": [4, P, SEQ], "qkT": [8, P, SEQ], "va_tok": [SEQ, 2 * W2], "flT": [1, NH2, SEQ],
           "softf": [P, P], "forget": [2, NH2, SEQ], "hzT": [4, P, SEQ]}


def tables(nc, kit, a, s):
    ok = kit.sem("tables_loaded")
    with nc.Block() as block:
        @block.sync
        def _(sp):
            for dst, src in ((s.cols1, a["cols1"]), (s.cols2, a["cols2"]), (s.ident, a["ident"])):
                sp.dma_start(dst[:], src).then_inc(ok, 16)
            sp.wait_ge(ok, 48)

        @block.vector
        def _(v):
            v.memset(s.eps[:, 0:1], EPS)
            v.memset(s.eps[:, 1:2], LN_EPS)


def program(nc, a):
    kit, s = Kit(nc), Names()
    with ExitStack() as keep:
        s.cols1, s.cols2 = kit.sbuf(keep, "cols1", [P, P]), kit.sbuf(keep, "cols2", [P, 64])
        s.ident = kit.sbuf(keep, "ident", [P, P])
        s.eps = kit.sbuf(keep, "eps", [P, 2])
        s.mod2 = kit.sbuf(keep, "mod2", [P, 2, KT])
        s.rstd_r = kit.sbuf(keep, "rstd_r", [P, LT])
        tables(nc, kit, a, s)
        with ExitStack() as proj:
            hmT = (kit.sbuf(proj, "hmT_hi", [P, KT, TOK], F32R), kit.sbuf(proj, "hmT_lo", [P, KT, TOK], F32R))
            modulation(nc, kit, a, s, hmT)
            projection(nc, kit, a, s, hmT)
        kit.end_phase()
        ssd(nc, kit, a, s)
        mix_out(nc, kit, a, s)
        kit.end_phase()
        projection2(nc, kit, a, s)
        lru(nc, kit, a, s)
        with ExitStack() as att:
            y = kit.sbuf(att, "att_y", [P, LT, W2])
            forget_sums(nc, kit, a, s)
            attention(nc, kit, a, s, y)
            out2(nc, kit, a, s, y)


def kernel(**inputs):
    import concourse.bacc as bacc
    from concourse.bass_utils import run_bass_kernel_spmd

    arrays = packed(inputs)
    nc = bacc.Bacc("TRN2", target_bir_lowering=False, num_devices=1)
    a = {name: nc.dram_tensor(f"in_{name}", v.shape, mybir.dt.from_np(v.dtype), kind="ExternalInput").ap()
         for name, v in arrays.items()}
    for name, shape in SCRATCH.items():
        a[name] = nc.dram_tensor(f"scratch_{name}", shape, F32, kind="Internal").ap()
    a["out"] = nc.dram_tensor("out", [SEQ, D], F32, kind="ExternalOutput").ap()
    program(nc, a)
    r = run_bass_kernel_spmd(nc, [{f"in_{k}": v for k, v in arrays.items()}], core_ids=[0])
    return r.results[0]["out"].reshape(1, SEQ, D)
```

```python
from contextlib import ExitStack, contextmanager

import numpy as np

import concourse.bass as bass
from concourse import mybir

ALU = mybir.AluOpType
ACT = mybir.ActivationFunctionType
AX_X = mybir.AxisListType.X
F32 = mybir.dt.float32
F32R = mybir.dt.float32r

P = 128
D = 1024
KT = D // P
SEQ, CTX = 2048, 256
TOK = SEQ + CTX
LT, CT = SEQ // P, CTX // P
TT = LT + CT
CH = 512
NCH = SEQ // CH
EPS = 1e-6

W_HALF = 1024
HEADS, GROUPS, HPG, HD, NS = 16, 4, 4, 64, 128
NDH = 2 * HEADS
WINDOWS = (2, 4, 8, 16)
GRID_R, GRID_C = 32, 64
XS0, B0, C0, DT0, ZS0, ZP0, U0, NBLK = 0, 8, 12, 16, 17, 25, 33, 41

V_BADA, V_NORM, V_CONVB, V_CONVW, V_PSCALE, V_SNORM = 0, 24, 32, 48, 112, 120
V2_BADA, V2_CONVW, V2_CONVB, V2_BA, V2_BX, V2_LAM, V2_NLRU, V2_NATT = 0, 24, 40, 44, 48, 52, 56, 60

XR0, ZR0, QK0, VZ0, FL0, NBLK2 = 0, 4, 8, 16, 24, 25
NH2, HD2 = 8, 64
W2 = NH2 * HD2
LRU_C = 8.0
ALPHA = 2.0 ** 0.25
LN_EPS = 1e-5


class Tally:

    def __init__(self, sem):
        self.sem, self.base, self.local = sem, 0, 0

    @property
    def value(self):
        return self.base + self.local

    def mark(self, ins):
        ins.then_inc(self.sem, 1)
        self.local += 1
        return ins

    @contextmanager
    def turn(self, i, per, turns):
        before = self.base + self.local
        self.base, self.local = before + i * per, 0
        yield
        assert self.local == per, (self.local, per)
        self.base, self.local = before + per * turns, 0


class Names:
    pass


class Kit:

    def __init__(self, nc):
        self.nc, self.in_use = nc, []

    def sbuf(self, ctx, name, shape, dt=F32):
        return ctx.enter_context(self.nc.sbuf_tensor(name, shape, dt))

    def psum(self, ctx, name, shape):
        return ctx.enter_context(self.nc.psum_tensor(name, shape, F32))

    def sem(self, name):
        self.in_use.append(self.nc.alloc_semaphore(name))
        return self.in_use[-1]

    def end_phase(self):
        self.nc.all_engine_barrier()
        self.nc.clear_and_free_semaphores(self.in_use)
        self.in_use = []
        self.nc.all_engine_barrier()

    def sems(self, prefix, names):
        return {n: self.sem(prefix + n) for n in names}


def modulation(nc, kit, a, s, hmT):
    hm_hi, hm_lo = hmT
    with ExitStack() as ctx:
        sb = lambda *args: kit.sbuf(ctx, *args)
        ps = lambda *args: kit.psum(ctx, *args)
        WC = 256
        wada = [sb(f"wada{n}", [P, KT, WC]) for n in range(2)]
        c3 = sb("c3", [P, KT, 3])
        sc3 = sb("silu_c3", [P, KT, 3])
        cbc = sb("c_bcast", [P, 2, KT, P])
        xt = [sb(f"xt{n}", [P, D]) for n in range(2)]
        xn = [sb(f"xn{n}", [P, D]) for n in range(2)]
        full = [sb(f"hm_full{n}", [P, KT, P]) for n in range(2)]
        stat = sb("hm_stat", [P, 4, 2])
        mA = sb("mod_scale", [P, 2, KT])
        mS = sb("mod_shift", [P, 2, KT])
        brow = [sb(f"b_gate_row{n}", [P, WC]) for n in range(2)]
        grow = [sb(f"gate_row{n}", [P, WC]) for n in range(2)]
        psC = ps("ps_modcols", [P, 32, 4])
        psT = [ps(f"ps_hmT{n}", [P, KT, P]) for n in range(2)]
        psJ = ps("ps_square", [P, D])
        psR = [psJ[:, n * CH:n * CH + WC] for n in range(2)]

        k = kit
        tabs = k.sem("a_tables_loaded")
        w_in = [k.sem(f"a_wada_loaded{n}") for n in range(2)]
        w_free = k.sem("a_wada_used")
        silu_ok = k.sem("a_silu_ready")
        bc_ok = k.sem("a_cbcast_ready")
        cols_ok = k.sem("a_modcols_ready")
        mod_ok = k.sem("a_mod_ready")
        x_in = [k.sem(f"a_x_loaded{n}") for n in range(2)]
        sq_ok = k.sem("a_square_done")
        root_ok = k.sem("a_root_done")
        xn_ok = k.sem("a_xn_ready")
        tr_ok = k.sem("a_transposed")
        full_a = k.sem("a_full_by_act")
        full_v = k.sem("a_full_by_dve")
        hi_ok = k.sem("a_hi_done")
        lo_ok = k.sem("a_lo_done")
        br_in = [k.sem(f"a_brow_loaded{n}") for n in range(2)]
        row_ok = k.sem("a_gate_row_summed")
        grow_ok = k.sem("a_gate_row_ready")
        g_out = [k.sem(f"a_gate_row_stored{n}") for n in range(2)]
        dve = Tally(k.sem("a_dve_chain"))

        with nc.Block() as block:
            @block.sync
            def _(sp):
                sp.dma_start(c3[:], a["c3"]).then_inc(tabs, 16)

                def load_w(c, n, first=False):
                    if not first:
                        sp.wait_ge(w_free, c - 1)
                    sp.dma_start(wada[n][:], a["wada"][c]).then_inc(w_in[n], 16)

                def load_x(t, n, src, first=False):
                    if not first:
                        sp.wait_ge(xn_ok, t - 1)
                    sp.dma_start(xt[n][:], src).then_inc(x_in[n], 16)

                load_w(0, 0, True)
                load_w(1, 1, True)
                load_x(0, 0, a["x"][0:P, :], True)
                load_x(1, 1, a["x"][P:2 * P, :], True)
                with sp.Fori(1, 4) as i:
                    for n in range(2):
                        load_w(2 * i + n, n)
                with sp.Fori(1, LT // 2) as i:
                    for n in range(2):
                        load_x(2 * i + n, n, a["x"][bass.ds((2 * i + n) * P, P), :])
                for n in range(2):
                    load_x(LT + n, n, a["ctx"][n * P:(n + 1) * P, :])
                with sp.Fori(4, 8) as i:
                    for n in range(2):
                        load_w(2 * i + n, n)
                for r in range(8):
                    n = r % 2
                    if r < 2:
                        load_w(16 + r, n)
                    else:
                        sp.wait_ge(row_ok, r - 1)
                        sp.dma_start(wada[n][:], a["wada"][16 + r]).then_inc(w_in[n], 16)
                        sp.wait_ge(grow_ok, r - 1)
                    sp.dma_start(brow[n][:], a["gate_bias"][r:r + 1, :].partition_broadcast(P)).then_inc(br_in[n], 16)

            @block.scalar
            def _(act):
                act.wait_ge(tabs, 16)
                act.activation(sc3[:], c3[:], ACT.Silu).then_inc(silu_ok, 1)

                def norm(t, half, n, first):
                    act.wait_ge(x_in[n], 16 * (half + 1))
                    if not first:
                        act.wait_ge(xn_ok, t - 1)
                    act.activation(psJ[:], xt[n][:], ACT.Square, accum_out=stat[:, 0, n:n + 1]).then_inc(sq_ok, 1)
                    act.wait_ge(sq_ok, t + 1)
                    act.activation(stat[:, 1, n:n + 1], stat[:, 0, n:n + 1], ACT.Sqrt, scale=1.0 / D,
                                   bias=s.eps[:, 0:1]).then_inc(root_ok, 1)

                def affine(t, n, which, first):
                    act.wait_ge(tr_ok, t + 1)
                    if not first:
                        act.wait_ge(lo_ok, t - 1)
                        act.wait_ge(hi_ok, t - 1)
                    for q in range(KT // 2):
                        ins = act.activation(full[n][:, q, :], psT[n][:, q, :], ACT.Identity,
                                             scale=mA[:, which, q:q + 1], bias=mS[:, which, q:q + 1])
                    ins.then_inc(full_a, 1)

                norm(0, 0, 0, True)
                norm(1, 0, 1, True)
                act.wait_ge(mod_ok, 2)
                affine(0, 0, 0, True)
                norm(2, 1, 0, False)
                affine(1, 1, 0, True)
                norm(3, 1, 1, False)
                with act.Fori(1, LT // 2 - 1) as i:
                    for n in range(2):
                        affine(2 * i + n, n, 0, False)
                        norm(2 * i + n + 2, i + 1, n, False)
                for n in range(2):
                    affine(LT - 2 + n, n, 0, False)
                    norm(LT + n, LT // 2, n, False)
                for n in range(2):
                    affine(LT + n, n, 1, False)

            @block.vector
            def _(v):
                v.wait_ge(silu_ok, 1)
                for w, cc in enumerate((0, 2)):
                    ins = v.tensor_copy(cbc[:, w], sc3[:, :, cc].unsqueeze(2).to_broadcast([P, KT, P]))
                ins.then_inc(bc_ok, 1)

                def xnorm(t, n, first):
                    v.wait_ge(root_ok, t + 1)
                    dve.mark(v.reciprocal(stat[:, 2, n:n + 1], stat[:, 1, n:n + 1]))
                    v.wait_ge(dve.sem, dve.value)
                    if not first:
                        v.wait_ge(tr_ok, t - 1)
                    v.tensor_scalar(xn[n][:], xt[n][:], stat[:, 2, n:n + 1], None, ALU.mult).then_inc(xn_ok, 1)

                def affine(t, n, which, first):
                    v.wait_ge(tr_ok, t + 1)
                    if not first:
                        v.wait_ge(hi_ok, t - 1)
                    for q in range(KT // 2, KT):
                        ins = v.tensor_scalar(full[n][:, q, :], psT[n][:, q, :], mA[:, which, q:q + 1],
                                              mS[:, which, q:q + 1], ALU.mult, ALU.add)
                    ins.then_inc(full_v, 1)

                def low(t, n, cols):
                    v.wait_ge(hi_ok, t + 1)
                    v.tensor_tensor(hm_lo[:, :, cols], full[n][:], hm_hi[:, :, cols].bitcast(F32),
                                    ALU.subtract).then_inc(lo_ok, 1)

                xnorm(0, 0, True)
                xnorm(1, 1, True)
                v.wait_ge(cols_ok, 1)
                for w in range(2):
                    dve.mark(v.tensor_tensor(mS[:, w, :], psC[:, 0:KT, w], s.cols1[:, V_BADA:V_BADA + KT], ALU.add))
                    dve.mark(v.tensor_tensor(mA[:, w, :], psC[:, KT:2 * KT, w],
                                             s.cols1[:, V_BADA + KT:V_BADA + 2 * KT], ALU.add))
                    v.wait_ge(dve.sem, dve.value)
                    v.scalar_tensor_tensor(mA[:, w, :], mA[:, w, :], 1.0, s.cols1[:, V_NORM:V_NORM + KT],
                                           ALU.add, ALU.mult).then_inc(mod_ok, 1)
                v.wait_ge(mod_ok, 2)

                def cols_of(t):
                    return slice(t * P, (t + 1) * P) if isinstance(t, int) else bass.ds(t * P, P)

                affine(0, 0, 0, True)
                xnorm(2, 0, False)
                low(0, 0, cols_of(0))
                affine(1, 1, 0, True)
                xnorm(3, 1, False)
                low(1, 1, cols_of(1))
                with v.Fori(1, LT // 2 - 1) as i:
                    with dve.turn(i - 1, 2, LT // 2 - 2):
                        for n in range(2):
                            t = 2 * i + n
                            affine(t, n, 0, False)
                            xnorm(t + 2, n, False)
                            low(t, n, cols_of(t))
                for n in range(2):
                    affine(LT - 2 + n, n, 0, False)
                    xnorm(LT + n, n, False)
                    low(LT - 2 + n, n, cols_of(LT - 2 + n))
                for n in range(2):
                    affine(LT + n, n, 1, False)
                    low(LT + n, n, cols_of(LT + n))
                v.wait_ge(cols_ok, 2)
                v.tensor_tensor(s.mod2[:, 0, :], psC[:, 2 * KT:3 * KT, 2], s.cols2[:, V2_BADA:V2_BADA + KT], ALU.add)
                dve.mark(v.tensor_tensor(s.mod2[:, 1, :], psC[:, 3 * KT:4 * KT, 2],
                                         s.cols2[:, V2_BADA + KT:V2_BADA + 2 * KT], ALU.add))
                v.wait_ge(dve.sem, dve.value)
                v.tensor_scalar(s.mod2[:, 1, :], s.mod2[:, 1, :], 1.0, None, ALU.add)
                for r in range(8):
                    n = r % 2
                    v.wait_ge(row_ok, r + 1)
                    v.wait_ge(br_in[n], 16 * (r // 2 + 1))
                    if r >= 2:
                        v.wait_ge(g_out[n], 16 * (r // 2))
                    v.tensor_tensor(grow[n][:], psR[n], brow[n][:], ALU.add).then_inc(grow_ok, 1)

            @block.gpsimd
            def _(g):
                def high(t, n, cols):
                    g.wait_ge(full_a, t + 1)
                    g.wait_ge(full_v, t + 1)
                    g.tensor_copy(hm_hi[:, :, cols], full[n][:]).then_inc(hi_ok, 1)

                with g.Fori(0, TT // 2) as i:
                    for n in range(2):
                        t = 2 * i + n
                        high(t, n, bass.ds(t * P, P))
                for r in range(8):
                    g.wait_ge(grow_ok, r + 1)
                    g.dma_start(a["gate_rows"][:, r * WC:(r + 1) * WC], grow[r % 2][:]).then_inc(g_out[r % 2], 16)
                for n in range(2):
                    g.wait_ge(g_out[n], 64)

            @block.tensor
            def _(pe):
                def mod_cols(c, half, n):
                    pe.wait_ge(w_in[n], 16 * (half + 1))
                    for m in range(2):
                        for q in range(KT):
                            mm = pe.matmul(psC[:, 2 * c + m, 0:3], wada[n][:, q, m * P:(m + 1) * P], sc3[:, q, :],
                                           start=(q == 0), stop=(q == KT - 1))
                    mm.then_inc(w_free, 1)
                    return mm

                def transposes(t, n, first):
                    pe.wait_ge(xn_ok, t + 1)
                    if not first:
                        pe.wait_ge(full_a, t - 1)
                        pe.wait_ge(full_v, t - 1)
                    for q in range(KT):
                        mm = pe.transpose(psT[n][:, q, :], xn[n][:, q * P:(q + 1) * P], s.ident[:])
                    mm.then_inc(tr_ok, 1)

                pe.wait_ge(silu_ok, 1)
                with pe.Fori(0, 4) as i:
                    for n in range(2):
                        mod_cols(2 * i + n, i, n)
                pe.transpose(psT[0][:, 0, :], s.ident[:], s.ident[:]).then_inc(cols_ok, 1)
                transposes(0, 0, True)
                transposes(1, 1, True)
                with pe.Fori(1, TT // 2) as i:
                    for n in range(2):
                        transposes(2 * i + n, n, False)
                with pe.Fori(4, 8) as i:
                    for n in range(2):
                        mod_cols(2 * i + n, i, n)
                pe.wait_ge(full_a, TT)
                pe.wait_ge(full_v, TT)
                pe.transpose(psT[0][:, 0, :], s.ident[:], s.ident[:]).then_inc(cols_ok, 1)
                pe.wait_ge(bc_ok, 1)
                def gate_row(r, w, half, n, first):
                    pe.wait_ge(w_in[n], 16 * (half + 1))
                    if not first:
                        pe.wait_ge(grow_ok, r - 1)
                    for q in range(KT):
                        mm = pe.matmul(psR[n], cbc[:, w, q, :], wada[n][:, q, :],
                                       start=(q == 0), stop=(q == KT - 1))
                    mm.then_inc(row_ok, 1)

                for r in range(4):
                    gate_row(r, 0, 8 + r // 2, r % 2, r < 2)
                for r in range(4, 8):
                    gate_row(r, 1, 8 + r // 2, r % 2, False)


class Kind:

    def __init__(self, first, count, chunks, how, turned=None, stored=None, func=ACT.Identity, scale=1.0, width=P):
        self.first, self.count, self.chunks, self.how = first, count, chunks, how
        self.turned, self.stored, self.func, self.scale, self.width = turned, stored, func, scale, width
        self.groups = chunks if turned is not None else 0


class Where:

    def __init__(self, b0, i=None, turns=1):
        self.b0, self.i, self.turns = b0, i, turns

    def num(self, back=0):
        b = self.b0 - back
        return b if self.i is None else b + 2 * self.i

    def at(self, table, d=0):
        first = table[self.b0 + d]
        if self.i is None:
            return first
        rate = table[self.b0 + d + 2] - first
        for k in range(self.turns):
            assert table[self.b0 + d + 2 * k] == first + rate * k, (self.b0, d, k)
        return first + rate * self.i


RAW_W = 2 + SEQ + 3 + CTX + 1
CTX_AT = SEQ + 3


def project(nc, kit, a, s, name, kinds, plan, xT, w_dram, conv, has_ctx):
    x_hi, x_lo = xT
    kind_of = [k for k in kinds for _ in range(k.count)]
    NB = len(kind_of)
    zero = [0]
    def table(f):
        out = [0]
        for b in range(NB):
            out.append(out[-1] + f(b, kind_of[b]))
        return out + [out[-1]] * 4
    T_ch = table(lambda b, k: k.chunks)
    T_gr = table(lambda b, k: k.groups)
    T_conv = table(lambda b, k: k.how == "conv")
    T_pool = table(lambda b, k: k.how == "pool")
    T_st = [table(lambda b, k: (k.stored is not None) * (b % 2 == n)) for n in range(2)]
    T_tok = table(lambda b, k: k.turned is not None)

    def wait(eng, sem, value):
        if not isinstance(value, int) or value > 0:
            eng.wait_ge(sem, value)

    with ExitStack() as ctx:
        sb = lambda *args: kit.sbuf(ctx, *args)
        w_raw = [sb(f"{name}_w_raw{n}", [P, KT, P]) for n in range(2)]
        w_hi = [sb(f"{name}_w_hi{n}", [P, KT, P], F32R) for n in range(2)]
        w_lo = [sb(f"{name}_w_lo{n}", [P, KT, P], F32R) for n in range(2)]
        BW = 2312
        work = sb(f"{name}_work", [P, 3 * BW + TOK])
        raw, acc, act_b = (work[:, j * BW:(j + 1) * BW] for j in range(3))
        tok = work[:, 3 * BW:3 * BW + TOK].rearrange("p (t c) -> p t c", c=P)
        direct = (raw, act_b)
        box = work[:, BW:BW + 40 * GRID_C].rearrange("p (r c) -> p r c", c=GRID_C)
        boxc = work[:, BW + 2560:BW + 2560 + 32 * 72].rearrange("p (r c) -> p r c", c=72)
        inv = work[:, BW + 2560 + 2304:BW + 2560 + 2304 + SEQ]
        ps = kit.psum(ctx, f"{name}_ps", [P, 5, CH])
        psT = kit.psum(ctx, f"{name}_psT", [P, 3, 4, P])

        k = kit
        w_in = [k.sem(f"{name}_w_loaded{n}") for n in range(2)]
        hi_ok, lo_ok = k.sem(f"{name}_w_hi_ready"), k.sem(f"{name}_w_lo_ready")
        ch_ok, ev_ok = k.sem(f"{name}_chunk_done"), k.sem(f"{name}_chunk_read")
        conv_ok, silu_ok, pool_ok = k.sem(f"{name}_conv_done"), k.sem(f"{name}_silu_done"), k.sem(f"{name}_pool_done")
        tg_ok, te_ok = k.sem(f"{name}_group_turned"), k.sem(f"{name}_group_read")
        tok_out = k.sem(f"{name}_tok_stored")
        c_out = [k.sem(f"{name}_channels_stored{n}") for n in range(2)]
        pad_ok = k.sem(f"{name}_pads_zero")
        inv_in = k.sem(f"{name}_inv_loaded")
        dve = Tally(k.sem(f"{name}_dve_chain"))

        def chunk_cols(c):
            return (slice(c * CH, (c + 1) * CH), CH) if c < NCH else (slice(SEQ, TOK), CTX)

        def tile_cols(t):
            return slice(t * P, (t + 1) * P) if t < LT else slice(CTX_AT + (t - LT) * P, CTX_AT + (t - LT + 1) * P)

        def walk(eng, body, per=None):
            for piece in plan:
                if piece[0] == "one":
                    body(Where(piece[1]))
                else:
                    _, b0, turns = piece
                    with eng.Fori(0, turns) as i:
                        if per is None:
                            for d in range(2):
                                body(Where(b0 + d, i, turns))
                        else:
                            with dve.turn(i, per(b0) + per(b0 + 1), turns):
                                for d in range(2):
                                    body(Where(b0 + d, i, turns))

        with nc.Block() as block:
            @block.sync
            def _(sp):
                def load_w(w, ahead):
                    b = w.b0 + ahead
                    if b >= NB:
                        return
                    if ahead == 2:
                        sp.wait_ge(hi_ok, w.num() + 1)
                        sp.wait_ge(lo_ok, w.num() + 1)
                    sp.dma_start(w_raw[b % 2][:], w_dram[w.num() + ahead]).then_inc(w_in[b % 2], 16)

                def stores(w):
                    kd, n = kind_of[w.b0], w.b0 % 2
                    m = w.num() - kd.first
                    if kd.stored is not None:
                        if kd.how == "conv":
                            sp.wait_ge(silu_ok, w.at(T_conv, 1))
                            src = act_b[0:kd.width, 0:SEQ]
                        elif kd.how == "pool":
                            sp.wait_ge(pool_ok, w.at(T_pool, 1))
                            src = work[:, BW:BW + SEQ]
                        else:
                            sp.wait_ge(ev_ok, w.at(T_ch, 1))
                            src = direct[n][0:kd.width, 0:SEQ]
                        sp.dma_start(kd.stored[m], src).then_inc(c_out[n], 16)
                    if kd.turned is not None:
                        sp.wait_ge(te_ok, w.at(T_gr, 1))
                        tiles = kd.chunks * 4 if kd.chunks == 4 else TT
                        dst = kd.turned.rearrange("(t p) c -> p t c", p=P)
                        dst = dst if kd.width != P else dst[:, :, bass.ds(m * P, P)]
                        sp.dma_start(dst, tok[:, 0:tiles, 0:kd.width]).then_inc(tok_out, 16)

                def body(w):
                    load_w(w, 2)
                    if kind_of[w.b0].how == "pool" and (w.b0 - kind_of[w.b0].first) % 2 == 0:
                        wait(sp, pool_ok, w.at(T_pool))
                        grp = (w.num() - kind_of[w.b0].first)
                        g0 = (w.b0 - kind_of[w.b0].first) // 2
                        g = g0 if w.i is None else g0 + w.i
                        if g0 == 0:
                            wait(sp, tok_out, 16 * T_tok[w.b0])
                        sp.dma_start(inv, a["inv_count"][g:g + 1, :].partition_broadcast(P) if isinstance(g, int)
                                     else a["inv_count"][bass.ds(g, 1), :].partition_broadcast(P)).then_inc(inv_in, 16)
                    if w.b0 >= 1:
                        stores(Where(w.b0 - 1, w.i, w.turns))

                load_w(Where(0), 0)
                load_w(Where(0), 1)
                walk(sp, body)
                stores(Where(NB - 1))
                for n in range(2):
                    sp.wait_ge(c_out[n], 16 * T_st[n][NB])
                if T_tok[NB]:
                    sp.wait_ge(tok_out, 16 * T_tok[NB])

            @block.scalar
            def _(act):
                def high(w, ahead):
                    b = w.b0 + ahead
                    if b >= NB:
                        return
                    half = (w.b0 + ahead) // 2 if w.i is None else (w.b0 + ahead) // 2 + w.i
                    act.wait_ge(w_in[b % 2], 16 * (half + 1))
                    act.activation(w_hi[b % 2][:], w_raw[b % 2][:], ACT.Copy).then_inc(hi_ok, 1)

                def silu(w):
                    act.wait_ge(conv_ok, w.at(T_conv, 1))
                    wait(act, tg_ok, w.at(T_gr))
                    for n in range(2):
                        wait(act, c_out[n], 16 * w.at(T_st[n]))
                    act.activation(act_b[:, 0:conv.width], acc[:, 0:conv.width], conv.func).then_inc(silu_ok, 1)

                def body(w):
                    kd, n = kind_of[w.b0], w.b0 % 2
                    before = kind_of[w.b0 - 1] if w.b0 else None
                    if before is not None and before.how == "conv":
                        silu(Where(w.b0 - 1, w.i, w.turns))
                    for c in range(kd.chunks):
                        act.wait_ge(ch_ok, w.at(T_ch) + c + 1)
                        cols, width = chunk_cols(c)
                        if c == 0:
                            if kd.how == "copy":
                                wait(act, tg_ok, w.at(T_gr, -1) if w.b0 else 0)
                                for q in range(2):
                                    if q == n or (before is not None and before.how == "conv") or \
                                            (w.b0 > 1 and kind_of[w.b0 - 2].how == "conv"):
                                        wait(act, c_out[q], 16 * w.at(T_st[q]))
                            else:
                                wait(act, conv_ok if kd.how == "conv" else pool_ok,
                                     w.at(T_conv if kd.how == "conv" else T_pool))
                                if kd.how == "pool" and before.how != "pool":
                                    for q in range(2):
                                        wait(act, c_out[q], 16 * w.at(T_st[q]))
                                    wait(act, tg_ok, w.at(T_gr))
                                if w.b0 == kinds[0].first:
                                    act.wait_ge(pad_ok, 1)
                        src = ps[0:P, c, 0:width]
                        if kd.how == "conv":
                            at = conv.left + c * CH if c < NCH else conv.left + CTX_AT
                            act.activation(raw[:, at:at + width], src, ACT.Identity).then_inc(ev_ok, 1)
                        elif kd.how == "pool":
                            act.activation(raw[:, cols], src, ACT.Identity).then_inc(ev_ok, 1)
                        else:
                            at = c * CH if c < NCH else CTX_AT
                            act.activation(direct[n][:, at:at + width], src, kd.func,
                                           scale=kd.scale).then_inc(ev_ok, 1)
                        if c == 0:
                            high(w, 1)

                high(Where(0), 0)
                walk(act, body)
                if kind_of[NB - 1].how == "conv":
                    silu(Where(NB - 1))

            @block.vector
            def _(v):
                def low(w, ahead):
                    b = w.b0 + ahead
                    if b >= NB:
                        return
                    v.wait_ge(hi_ok, w.num() + ahead + 1)
                    v.tensor_tensor(w_lo[b % 2][:], w_raw[b % 2][:], w_hi[b % 2][:].bitcast(F32),
                                    ALU.subtract).then_inc(lo_ok, 1)

                def read_groups(w):
                    kd = kind_of[w.b0]
                    for g in range(kd.groups):
                        v.wait_ge(tg_ok, w.at(T_gr) + g + 1)
                        if g == 0:
                            wait(v, tok_out, 16 * w.at(T_tok))
                        cnt = 4 if g < 4 else CT
                        v.tensor_copy(tok[:, 4 * g:4 * g + cnt, 0:kd.width],
                                      psT[:, g % 3, 0:cnt, 0:kd.width]).then_inc(te_ok, 1)

                def step(ins):
                    dve.mark(ins)
                    v.wait_ge(dve.sem, dve.value)

                def conv_block(w):
                    m = w.num() - kind_of[w.b0].first + conv.block0[kind_of[w.b0].first]
                    tap = lambda q: conv.tab[:, bass.ds(conv.w_at + q * conv.stride + m, 1)] if w.i is not None \
                        else conv.tab[:, conv.w_at + q * conv.stride + m:conv.w_at + q * conv.stride + m + 1]
                    bias = conv.tab[:, bass.ds(conv.b_at + m, 1)] if w.i is not None \
                        else conv.tab[:, conv.b_at + m:conv.b_at + m + 1]
                    v.wait_ge(ev_ok, w.at(T_ch, 1))
                    wait(v, silu_ok, w.at(T_conv))
                    W = conv.width
                    step(v.tensor_scalar(acc[:, 0:W], raw[:, 0:W], tap(0), bias, ALU.mult, ALU.add))
                    for q in range(1, 4):
                        ins = v.scalar_tensor_tensor(acc[:, 0:W], raw[:, q:q + W], tap(q), acc[:, 0:W],
                                                     ALU.mult, ALU.add)
                        if q < 3:
                            step(ins)
                    ins.then_inc(conv_ok, 1)

                def pool_block(w):
                    g = (w.b0 - kind_of[w.b0].first) // 2
                    win = WINDOWS[g]
                    u = raw[:, 0:SEQ].rearrange("p (r c) -> p r c", c=GRID_C)
                    v.wait_ge(ev_ok, w.at(T_ch, 1))
                    for q in range(2):
                        wait(v, c_out[q], 16 * T_st[q][w.b0])
                    if w.b0 == kind_of[w.b0].first:
                        wait(v, tok_out, 16 * T_tok[w.b0])

                    def spans(dst, src, n, cut):
                        v.memset(cut(dst, 0, 7), 0.0)
                        v.tensor_copy(cut(dst, 7, 8), cut(src, 0, 1))
                        v.tensor_copy(cut(dst, n + 7, n + 8), cut(src, n - 1, n))
                        step(v.tensor_tensor(cut(dst, 8, n + 7), cut(src, 0, n - 1), cut(src, 1, n), ALU.add))
                        half = 2
                        while half < win:
                            step(v.tensor_tensor(cut(dst, 0, n + 8 - half), cut(dst, 0, n + 8 - half),
                                                 cut(dst, half, n + 8), ALU.add))
                            half *= 2
                        return cut(dst, 8 - win // 2, 8 - win // 2 + n)

                    rows = spans(box, u, GRID_R, lambda x, i, j: x[:, i:j, :])
                    both = spans(boxc, rows, GRID_C, lambda x, i, j: x[:, :, i:j])
                    v.wait_ge(inv_in, 16 * (g + 1))
                    d = box[:, 0:GRID_R, :]
                    step(v.tensor_tensor(d, both, inv.rearrange("p (r c) -> p r c", c=GRID_C), ALU.mult))
                    v.tensor_tensor(d, d, u, ALU.subtract).then_inc(pool_ok, 1)

                def body(w):
                    kd = kind_of[w.b0]
                    low(w, 1)
                    if w.b0 >= 1:
                        read_groups(Where(w.b0 - 1, w.i, w.turns))
                    if kd.how == "conv":
                        conv_block(w)
                    if kd.how == "pool":
                        pool_block(w)

                v.memset(raw, 0.0).then_inc(pad_ok, 1)
                low(Where(0), 0)
                for piece in plan:
                    if piece[0] == "one":
                        body(Where(piece[1]))
                    elif kind_of[piece[1]].how == "pool":
                        for b in range(piece[1], piece[1] + 2 * piece[2]):
                            body(Where(b))
                    else:
                        _, b0, turns = piece
                        per = sum(3 * (kind_of[b0 + d].how == "conv") for d in range(2))
                        with v.Fori(0, turns) as i:
                            with dve.turn(i, per, turns):
                                for d in range(2):
                                    body(Where(b0 + d, i, turns))
                if kind_of[NB - 1].groups:
                    read_groups(Where(NB - 1))

            @block.tensor
            def _(pe):
                def turn(w, groups):
                    kd, n = kind_of[w.b0], w.b0 % 2
                    src = act_b if kd.how == "conv" else direct[n]
                    for g in groups:
                        if g == groups[0]:
                            if kd.how == "conv":
                                pe.wait_ge(silu_ok, w.at(T_conv, 1))
                            else:
                                pe.wait_ge(ev_ok, w.at(T_ch, 1))
                        wait(pe, te_ok, w.at(T_gr) + max(0, g - 2))
                        for q in range(4 if g < 4 else CT):
                            mm = pe.transpose(psT[:, g % 3, q, :], src[:, tile_cols(4 * g + q)], s.ident[:])
                        mm.then_inc(tg_ok, 1)

                def body(w):
                    kd, n = kind_of[w.b0], w.b0 % 2
                    before = kind_of[w.b0 - 1] if w.b0 else None
                    pe.wait_ge(lo_ok, w.num() + 1)
                    for c in range(kd.chunks):
                        cols, width = chunk_cols(c)
                        if before is not None:
                            pe.wait_ge(ev_ok, w.at(T_ch, -1) + min(c, before.chunks - 1) + 1)
                        for q in range(KT):
                            for j, (wt, xx) in enumerate(((w_hi, x_hi), (w_hi, x_lo), (w_lo, x_hi))):
                                mm = pe.matmul(ps[:, c, 0:width], wt[n][:, q, :], xx[:, q, cols],
                                               start=(q == 0 and j == 0), stop=(q == KT - 1 and j == 2))
                        mm.then_inc(ch_ok, 1)
                        if before is not None and before.groups:
                            prev = Where(w.b0 - 1, w.i, w.turns)
                            if c == kd.chunks - 2:
                                turn(prev, [0, 1])
                            if c == kd.chunks - 1:
                                turn(prev, list(range(2, before.groups)))

                walk(pe, body)
                if kind_of[NB - 1].groups:
                    turn(Where(NB - 1), list(range(kind_of[NB - 1].groups)))


class Conv:

    def __init__(self, tab, w_at, b_at, stride, block0, left, width, func):
        self.tab, self.w_at, self.b_at, self.stride, self.block0 = tab, w_at, b_at, stride, block0
        self.left, self.width, self.func = left, width, func


def projection(nc, kit, a, s, hmT):
    kinds = [
        Kind(XS0, 8, 5, "conv", turned=a["xs_tok"]),
        Kind(B0, 4, 5, "conv", turned=a["b_tok"], stored=a["bT"]),
        Kind(C0, 4, 5, "conv", stored=a["cT"]),
        Kind(DT0, 1, 5, "copy", turned=a["dt_tok"], width=NDH),
        Kind(ZS0, 8, 4, "copy", turned=a["z_tok"], func=ACT.Silu),
        Kind(ZP0, 8, 4, "copy", stored=a["zpT"], func=ACT.Silu),
        Kind(U0, 8, 4, "pool", stored=a["dT"]),
    ]
    conv = Conv(s.cols1, V_CONVW, V_CONVB, 16, {XS0: 0, B0: 8, C0: 12}, 2, SEQ + 3 + CTX, ACT.Silu)
    plan = [("one", 0), ("one", 1), ("loop", 2, 3), ("one", 8), ("one", 9), ("loop", 10, 1)] + \
           [("one", b) for b in range(12, 19)] + [("loop", 19, 3), ("one", 25), ("one", 26), ("loop", 27, 3)] + \
           [("one", 33), ("one", 34), ("loop", 35, 2), ("one", 39), ("one", 40)]
    project(nc, kit, a, s, "p1", kinds, plan, hmT, a["w_in"], conv, True)


LOG1P_ODD = [1.0 / j for j in (15, 13, 11, 9, 7, 5, 3)]


def softplus(v, step, exp, out, x, t):
    step(v.scalar_tensor_tensor(t[0], x, -1.0, x, ALU.mult, ALU.min))
    exp()
    step(v.tensor_scalar(t[1], t[0], 2.0, None, ALU.add))
    step(v.reciprocal(t[2], t[1]))
    step(v.tensor_tensor(t[0], t[0], t[2], ALU.mult))
    step(v.tensor_tensor(t[1], t[0], t[0], ALU.mult))
    step(v.tensor_scalar(t[2], t[1], LOG1P_ODD[0], None, ALU.mult))
    for c in LOG1P_ODD[1:]:
        step(v.scalar_tensor_tensor(t[2], t[2], c, t[1], ALU.add, ALU.mult))
    step(v.scalar_tensor_tensor(t[2], t[2], 1.0, t[0], ALU.add, ALU.mult))
    step(v.tensor_scalar(t[0], x, 0.0, None, ALU.max))
    step(v.scalar_tensor_tensor(out, t[2], 2.0, t[0], ALU.mult, ALU.add))


def ssd_decays(nc, kit, a, s, r):
    F = TT * NDH
    with ExitStack() as ctx:
        sb = lambda *args: kit.sbuf(ctx, *args)
        bias, alog = sb("dt_bias_row", [P, NDH]), sb("a_log_row", [P, NDH])
        xr, adt, tot = sb("dt_raw", [P, TT, NDH]), sb("adt", [P, TT, NDH]), sb("acum_end", [P, TT, NDH])
        t = [sb(f"sp_tmp{n}", [P, TT, NDH]) for n in range(3)]
        sel = [sb(f"sel_{n}", [P, P]) for n in ("last", "first")]
        rows, sums = sb("adt_rows", [HEADS, 2, TOK]), sb("acum_rows_sb", [HEADS, 2, TOK])
        parts = [sb(f"acum_part{n}", [HEADS, 2, TOK], F32R) for n in range(2)]
        keepm = [sb(f"chunk_keep{n}", [HEADS, TOK]) for n in range(2)]
        psA = [kit.psum(ctx, f"psA{n}", [HEADS, 4, P]) for n in range(2)]
        psB = kit.psum(ctx, "psB", [P, 2, 512])
        psE = kit.psum(ctx, "psE", [P, 2, 512])
        k = kit
        ld, ek_ok, e_done = k.sem("d_loaded"), k.sem("d_exp_asked"), k.sem("d_exp_done")
        adt_ok, tr_ok, rd_ok = k.sem("d_adt_ready"), k.sem("d_rows_turned"), k.sem("d_rows_read")
        scan_ok, back_ok, ac_ok, end_ok = (k.sem(n) for n in ("d_scanned", "d_sums_turned", "d_acum_ready", "d_ends_ready"))
        st, part_ok = k.sem("d_rows_stored"), k.sem("d_part_ready")
        dve = Tally(k.sem("d_dve_chain"))
        with nc.Block() as block:
            @block.sync
            def _(sp):
                for dst, src in ((bias[:], a["dt_bias"].partition_broadcast(P)), (alog[:], a["a_log"].partition_broadcast(P)),
                                 (xr[:], a["dt_tok"].rearrange("(t p) c -> p t c", p=P)),
                                 (sel[0][:], a["sel_last"]), (sel[1][:], a["sel_first"]),
                                 (keepm[0][:], a["keep_fwd"]), (keepm[1][:], a["keep_bwd"]),
                                 (r.dskip[:], a["d_skip"].partition_broadcast(P))):
                    sp.dma_start(dst, src).then_inc(ld, 16)
                for m in range(2):
                    sp.wait_ge(part_ok, m + 1)
                    for d in range(2):
                        sp.dma_start(a["acum_rows"][m, :, d * HEADS:(d + 1) * HEADS, :].rearrange("t h l -> h t l"),
                                     parts[m][:, d].rearrange("h (t l) -> h t l", l=P).bitcast(F32)).then_inc(st, 16)
                sp.wait_ge(st, 64)

            @block.scalar
            def _(act):
                act.wait_ge(ld, 128)
                act.activation(alog[:], alog[:], ACT.Exp).then_inc(e_done, 1)
                act.wait_ge(ek_ok, 1)
                act.activation(t[0][:], t[0][:], ACT.Exp).then_inc(e_done, 1)
                act.wait_ge(ac_ok, 4)
                act.activation(r.eac[:], r.acum[:], ACT.Exp).then_inc(e_done, 1)
                act.wait_ge(ek_ok, 2)
                act.activation(r.wst[:], t[0][:], ACT.Exp).then_inc(e_done, 1)
                act.activation(r.cdec[:], tot[:], ACT.Exp).then_inc(e_done, 1)

            @block.vector
            def _(v):
                def step(ins):
                    dve.mark(ins)
                    v.wait_ge(dve.sem, dve.value)

                def ask():
                    v.nop().then_inc(ek_ok, 1)
                    v.wait_ge(e_done, 2)

                v.wait_ge(ld, 128)
                step(v.tensor_tensor(xr[:], xr[:], bias[:].unsqueeze(1).to_broadcast([P, TT, NDH]), ALU.add))
                softplus(v, step, ask, r.dt[:], xr[:], [x[:] for x in t])
                step(v.scalar_tensor_tensor(adt[:], alog[:].unsqueeze(1).to_broadcast([P, TT, NDH]), -1.0, r.dt[:],
                                            ALU.mult, ALU.mult))
                v.nop().then_inc(adt_ok, 1)
                for d in range(2):
                    for g in range(5):
                        q = 5 * d + g
                        cnt = 4 if g < 4 else 2
                        v.wait_ge(tr_ok, q + 1)
                        v.tensor_copy(rows[:, d, g * CH:g * CH + cnt * P].rearrange("h (t l) -> h t l", l=P),
                                      psA[q % 2][:, 0:cnt, :]).then_inc(rd_ok, 1)
                v.wait_ge(rd_ok, 10)
                v.tensor_tensor_scan(sums[:, 0, :], keepm[0][:], rows[:, 0, :], 0.0, ALU.mult, ALU.add).then_inc(scan_ok, 1)
                v.tensor_tensor_scan(sums[:, 1, ::-1], keepm[1][:, ::-1], rows[:, 1, ::-1], 0.0, ALU.mult,
                                     ALU.add).then_inc(scan_ok, 1)
                for d in range(2):
                    v.wait_ge(back_ok, d + 1)
                    v.tensor_copy(r.acum[:, :, d * HEADS:(d + 1) * HEADS],
                                  psB[:, d, 0:TT * HEADS].rearrange("p (t h) -> p t h", h=HEADS)).then_inc(ac_ok, 1)
                for d in range(2):
                    v.wait_ge(end_ok, d + 1)
                    v.tensor_copy(tot[:, :, d * HEADS:(d + 1) * HEADS],
                                  psE[:, d, 0:TT * HEADS].rearrange("p (t h) -> p t h", h=HEADS)).then_inc(ac_ok, 1)
                v.wait_ge(scan_ok, 2)
                v.tensor_copy(parts[0][:], sums[:]).then_inc(part_ok, 1)
                v.wait_ge(part_ok, 1)
                v.tensor_tensor(parts[1][:], sums[:], parts[0][:].bitcast(F32), ALU.subtract).then_inc(part_ok, 1)
                v.wait_ge(ac_ok, 4)
                step(v.tensor_tensor(t[0][:], tot[:], r.acum[:], ALU.subtract))
                v.nop().then_inc(ek_ok, 1)
                v.wait_ge(e_done, 4)
                v.tensor_tensor(r.wst[:], r.wst[:], r.dt[:], ALU.mult)

            @block.tensor
            def _(pe):
                pe.wait_ge(adt_ok, 1)
                for d in range(2):
                    for g in range(5):
                        q = 5 * d + g
                        if q >= 2:
                            pe.wait_ge(rd_ok, q - 1)
                        for j in range(4 if g < 4 else 2):
                            mm = pe.transpose(psA[q % 2][:, j, :], adt[:, 4 * g + j, d * HEADS:(d + 1) * HEADS], s.ident[:])
                        mm.then_inc(tr_ok, 1)
                for d in range(2):
                    pe.wait_ge(scan_ok, d + 1)
                    for c in range(TT):
                        mm = pe.transpose(psB[:, d, c * HEADS:(c + 1) * HEADS], sums[:, d, c * P:(c + 1) * P],
                                          s.ident[0:HEADS, 0:HEADS])
                    mm.then_inc(back_ok, 1)
                for d in range(2):
                    pe.wait_ge(ac_ok, d + 1)
                    pe.matmul(psE[:, d, 0:TT * HEADS].rearrange("p (t h) -> p t h", h=HEADS), sel[d][:],
                              r.acum[:, :, d * HEADS:(d + 1) * HEADS], start=True, stop=True).then_inc(end_ok, 1)


def heads_of(row):
    return row.unsqueeze(2).to_broadcast([P, HEADS, HD])


def by_head(t):
    return t.rearrange("p (h d) -> p h d", d=HD)


def ssd_states(nc, kit, a, s, r):
    STEPS = 19
    with ExitStack() as ctx:
        sb = lambda *args: kit.sbuf(ctx, *args)
        xs = [sb(f"st_xs{n}", [P, W_HALF]) for n in range(2)]
        bt = [sb(f"st_b{n}", [P, GROUPS * NS]) for n in range(2)]
        xw = [sb(f"st_xw{n}", [P, W_HALF]) for n in range(2)]
        mid = sb("st_mid", [P, W_HALF])
        psS = [kit.psum(ctx, f"psS{n}", [P, W_HALF]) for n in range(2)]
        k = kit
        ld = [k.sem(f"st_loaded{n}") for n in range(2)]
        zero_ok, xw_ok, s_ok, h_ok = (k.sem(f"st_{n}") for n in ("zeroed", "weighted", "summed", "state_ready"))
        dve = Tally(k.sem("st_dve_chain"))

        def chunk(j):
            if isinstance(j, int):
                return j - 1 if j >= 17 else 17 - j
            return j * -1 + 17

        def tok(t, c):
            return t[c * P:(c + 1) * P, :] if isinstance(c, int) else t[bass.ds(c * P, P), :]

        def one(t, c):
            return t[:, c, :]

        def walk(eng, body, count=0, tally=None):
            for j in range(2):
                body(j, 0, j)
            with eng.Fori(1, 8) as i:
                if tally is None:
                    for n in range(2):
                        body(2 * i + n, i, n)
                else:
                    with tally.turn(i - 1, 2 * count, 7):
                        for n in range(2):
                            body(2 * i + n, i, n)
            for j in range(16, STEPS):
                body(j, j // 2, j % 2)

        with nc.Block() as block:
            @block.sync
            def _(sp):
                def load(j, n):
                    c = chunk(j)
                    if not isinstance(j, int) or j >= 2:
                        sp.wait_ge(s_ok, j - 1)
                    sp.dma_start(xs[n][:], tok(a["xs_tok"], c)).then_inc(ld[n], 16)
                    sp.dma_start(bt[n][:], tok(a["b_tok"], c)).then_inc(ld[n], 16)

                load(0, 0)
                load(1, 1)
                with sp.Fori(1, 8) as i:
                    for n in range(2):
                        load(2 * i + n, n)
                for j in range(16, STEPS):
                    load(j, j % 2)

            @block.gpsimd
            def _(g):
                def body(j, half, n):
                    d = 0 if isinstance(j, int) and j >= 17 else 1
                    c = chunk(j)
                    weight = heads_of(one(r.wst, c)[:, d * HEADS:(d + 1) * HEADS])
                    g.wait_ge(ld[n], 32 * (half + 1))
                    if not isinstance(j, int) or j >= 2:
                        g.wait_ge(s_ok, j - 1)
                    g.tensor_tensor(by_head(xw[n][:]), by_head(xs[n][:]), weight, ALU.mult).then_inc(xw_ok, 1)
                walk(g, body)

            @block.tensor
            def _(pe):
                def body(j, half, n):
                    pe.wait_ge(xw_ok, j + 1)
                    if not isinstance(j, int) or j >= 2:
                        pe.wait_ge(h_ok, j - 1)
                    for grp in range(GROUPS):
                        mm = pe.matmul(psS[n][:, grp * 256:(grp + 1) * 256], bt[n][:, grp * NS:(grp + 1) * NS],
                                       xw[n][:, grp * 256:(grp + 1) * 256], start=True, stop=True)
                    mm.then_inc(s_ok, 1)
                walk(pe, body)

            @block.vector
            def _(v):
                v.memset(r.hb[:, 17, :], 0.0).then_inc(zero_ok, 1)
                v.memset(r.hf[0][:], 0.0).then_inc(zero_ok, 1)
                v.wait_ge(zero_ok, 2)

                def body(j, half, n):
                    c = chunk(j)
                    if isinstance(j, int) and j >= 17:
                        src, dst, d = r.hf[j - 17][:], r.hf[18 - j][:], 0
                    else:
                        src, dst, d = r.hb[:, c, :], r.hb[:, c - 1, :], 1
                    decay = heads_of(one(r.cdec, c)[:, d * HEADS:(d + 1) * HEADS])
                    v.wait_ge(s_ok, j + 1)
                    dve.mark(v.tensor_tensor(by_head(mid[:]), by_head(src), decay, ALU.mult))
                    v.wait_ge(dve.sem, dve.value)
                    v.tensor_tensor(dst, mid[:], psS[n][:], ALU.add).then_inc(h_ok, 1)
                    v.wait_ge(h_ok, j + 1)
                walk(v, body, 1, dve)


def ssd_outputs(nc, kit, a, s, r):
    with ExitStack() as ctx:
        sb = lambda *args: kit.sbuf(ctx, *args)
        two = lambda name, shape: [sb(f"{name}{n}", shape) for n in range(2)]
        dec, xs, bt, zt = two("y_decay", [P, NDH, P]), two("y_xs", [P, W_HALF]), two("y_b", [P, 512]), sb("y_z", [P, W_HALF])
        seg_r, seg_l = sb("y_seg_r", [10, NDH * P], F32R), sb("y_seg_l", [10, 8, P], F32R)
        bT, cT = two("y_bT", [P, GROUPS, P]), two("y_cT", [P, GROUPS, P])
        xd = two("y_xd", [P, 2, W_HALF])
        xw, xk = sb("y_xw", [P, W_HALF]), sb("y_xskip", [P, W_HALF])
        cb = two("y_cb", [P, GROUPS, P])
        y, tmp = sb("y_out", [P, W_HALF]), sb("y_tmp", [P, W_HALF])
        tri, tri_r = sb("y_masks", [P, 2, P]), sb("y_masks_r", [P, 2, P], F32R)
        ident_r = sb("y_ident", [P, P], F32R)
        psCB = kit.psum(ctx, "psCB", [P, GROUPS, P])
        psE = kit.psum(ctx, "psSeg", [P, 4, P])
        psS = kit.psum(ctx, "psSt", [P, W_HALF])
        psY = kit.psum(ctx, "psY", [P, W_HALF])
        psO = kit.psum(ctx, "psO", [P, W_HALF])
        k = kit
        names = ("xw_ok", "xd_ok", "cb_ok", "cbm_ok", "s_ok", "h_ok", "seg_ok", "exp_ok", "m_ok", "ready",
                 "off_f_ok", "off_b_ok", "t1_ok", "t2_ok", "yd_ok", "g_ok")
        S = k.sems("y_", names)
        ld = [k.sem(f"y_loaded{n}") for n in range(2)]
        c_in = [k.sem(f"y_cT_loaded{n}") for n in range(2)]
        st, z_in = k.sem("y_stored"), k.sem("y_z_loaded")
        mk_in, const_in, row_in = k.sem("y_masks_loaded"), k.sem("y_seg_constants_loaded"), k.sem("y_seg_rows_loaded")
        dve = Tally(k.sem("y_dve_chain"))
        NC = LT

        def tokens(t, c):
            return t[c * P:(c + 1) * P, :] if isinstance(c, int) else t[bass.ds(c * P, P), :]

        def cols(t, c):
            t = t.rearrange("g n l -> n g l")
            return t[:, :, c * P:(c + 1) * P] if isinstance(c, int) else t[:, :, bass.ds(c * P, P)]

        def part(t, c, d):
            return t[:, c, d * HEADS:(d + 1) * HEADS]

        with nc.Block() as block:
            @block.sync
            def _(sp):
                sp.dma_start(tri[:, 0], a["causal_turned"]).then_inc(mk_in, 16)
                sp.dma_start(tri[:, 1], a["causal"]).then_inc(mk_in, 16)

                def load_b(c, n):
                    sp.dma_start(bt[n][:], tokens(a["b_tok"], c)).then_inc(ld[n], 16)
                    sp.dma_start(bT[n][:], cols(a["bT"], c)).then_inc(ld[n], 16)

                def load_x(c, n):
                    sp.dma_start(xs[n][:], tokens(a["xs_tok"], c)).then_inc(ld[n], 16)

                def load_c(c, n):
                    sp.dma_start(cT[n][:], cols(a["cT"], c)).then_inc(c_in[n], 16)

                def body(c, n):
                    if not isinstance(c, int) or c < NC - 2:
                        sp.wait_ge(S["s_ok"], c + 1)
                        load_b(c + 2, n)
                        sp.wait_ge(S["xd_ok"], 3 * c + 3)
                        load_x(c + 2, n)
                        sp.wait_ge(S["off_b_ok"], c + 1)
                        load_c(c + 2, n)
                    sp.wait_ge(S["g_ok"], c + 1)
                    sp.dma_start(tokens(a["g_tok"], c), y[:]).then_inc(st, 16)
                    if not isinstance(c, int) or c < NC - 1:
                        sp.dma_start(zt[:], tokens(a["z_tok"], c + 1)).then_inc(z_in, 16)

                for n in range(2):
                    load_b(n, n)
                    load_c(n, n)
                    load_x(n, n)
                sp.dma_start(zt[:], tokens(a["z_tok"], 0)).then_inc(z_in, 16)
                with sp.Fori(0, NC // 2 - 1) as i:
                    for n in range(2):
                        body(2 * i + n, n)
                for n in range(2):
                    body(NC - 2 + n, n)
                sp.wait_ge(st, 16 * NC)

            @block.gpsimd
            def _(g):
                def rows(c):
                    both = a["acum_rows"][:, c:c + 1] if isinstance(c, int) else a["acum_rows"][:, bass.ds(c, 1)]
                    g.dma_start(seg_r[0:2, :], both.rearrange("m o h l -> m (o h l)")).then_inc(row_in, 16)
                    for m in range(2):
                        g.dma_start(seg_l[2 + 4 * m:6 + 4 * m],
                                    both[m].rearrange("o (q j) l -> j (o q) l", j=4)).then_inc(row_in, 16)

                def body(c, half, n, last):
                    g.wait_ge(ld[n], 48 * (half + 1))
                    if not isinstance(c, int) or c > 0:
                        g.wait_ge(S["s_ok"], c)
                    g.tensor_tensor(by_head(xw[:]), by_head(xs[n][:]), heads_of(part(r.wst, c, 0)),
                                    ALU.mult).then_inc(S["xw_ok"], 1)
                    for d in range(2):
                        if d == 1:
                            g.wait_ge(S["seg_ok"], 8 * c + 8)
                        g.tensor_tensor(by_head(xd[n][:, d, :]), by_head(xs[n][:]), heads_of(part(r.dt, c, d)),
                                        ALU.mult).then_inc(S["xd_ok"], 1)
                    if not last:
                        rows(c + 1)
                    if not isinstance(c, int) or c > 0:
                        g.wait_ge(S["t1_ok"], c)
                    g.tensor_tensor(by_head(xk[:]), by_head(xs[n][:]), heads_of(r.dskip[:]),
                                    ALU.mult).then_inc(S["xd_ok"], 1)

                g.dma_start(seg_r[:], a["seg_r"]).then_inc(const_in, 16)
                g.dma_start(seg_l[:], a["seg_l"]).then_inc(const_in, 16)
                g.wait_ge(const_in, 32)
                rows(0)
                for n in range(2):
                    body(n, 0, n, False)
                with g.Fori(1, NC // 2 - 1) as i:
                    for n in range(2):
                        body(2 * i + n, i, n, False)
                for n in range(2):
                    body(NC - 2 + n, NC // 2 - 1, n, n == 1)

            @block.scalar
            def _(act):
                def body(c, half, n):
                    for q in range(8):
                        act.wait_ge(S["seg_ok"], 8 * c + q + 1)
                        if q == 0 and (not isinstance(c, int) or c > 1):
                            act.wait_ge(S["yd_ok"], c - 1)
                        act.activation(dec[n][:, 4 * q:4 * q + 4, :], psE[:], ACT.Exp).then_inc(S["exp_ok"], 1)

                for n in range(2):
                    body(n, 0, n)
                with act.Fori(1, NC // 2) as i:
                    for n in range(2):
                        body(2 * i + n, i, n)

            @block.vector
            def _(v):
                def step(ins):
                    dve.mark(ins)
                    v.wait_ge(dve.sem, dve.value)

                def front(c, half, n):
                    v.wait_ge(S["cb_ok"], c + 1)
                    v.tensor_copy(cb[n][:], psCB[:]).then_inc(S["cbm_ok"], 1)
                    if not isinstance(c, int) or c > 0:
                        v.wait_ge(S["h_ok"], c)
                    if not isinstance(c, int) or c > 1:
                        v.wait_ge(S["g_ok"], c - 1)
                    step(v.tensor_tensor(by_head(tmp[:]), by_head(r.hf[n][:]), heads_of(part(r.cdec, c, 0)), ALU.mult))
                    v.wait_ge(S["s_ok"], c + 1)
                    if not isinstance(c, int) or c > 0:
                        v.wait_ge(S["off_f_ok"], c)
                    v.tensor_tensor(r.hf[1 - n][:], tmp[:], psS[:], ALU.add).then_inc(S["h_ok"], 1)

                def products(c, n, directions):
                    v.wait_ge(S["cbm_ok"], c + 1)
                    for d in directions:
                        v.wait_ge(S["exp_ok"], 8 * c + 4 * d + 4)
                        m = dec[n][:, d * HEADS:(d + 1) * HEADS, :].rearrange("p (g q) l -> p g q l", g=GROUPS)
                        v.tensor_tensor(m, m, cb[n][:].unsqueeze(2).to_broadcast([P, GROUPS, HPG, P]),
                                        ALU.mult).then_inc(S["m_ok"], 1)

                def forward(c, n):
                    v.wait_ge(S["off_f_ok"], c + 1)
                    if not isinstance(c, int) or c > 0:
                        v.wait_ge(st, 16 * c)
                    step(v.tensor_tensor(by_head(y[:]), by_head(psO[:]), heads_of(part(r.eac, c, 0)), ALU.mult))
                    v.wait_ge(S["yd_ok"], c + 1)
                    v.tensor_tensor(y[:], y[:], psY[:], ALU.add).then_inc(S["t1_ok"], 1)

                def backward(c, n, last=False):
                    v.wait_ge(S["off_b_ok"], c + 1)
                    v.wait_ge(S["h_ok"], c + (1 if last else 2))
                    v.tensor_tensor(by_head(tmp[:]), by_head(psO[:]), heads_of(part(r.eac, c, 1)),
                                    ALU.mult).then_inc(S["t2_ok"], 1)
                    v.wait_ge(S["t2_ok"], c + 1)
                    v.wait_ge(S["t1_ok"], c + 1)
                    step(v.tensor_tensor(y[:], y[:], tmp[:], ALU.add))
                    v.wait_ge(z_in, 16 * (c + 1))
                    v.tensor_tensor(y[:], y[:], zt[:], ALU.mult).then_inc(S["g_ok"], 1)

                def body(c, n):
                    front(c + 1, 0, 1 - n)
                    products(c + 1, 1 - n, (0,))
                    forward(c, n)
                    products(c + 1, 1 - n, (1,))
                    backward(c, n)

                v.wait_ge(mk_in, 32)
                v.tensor_copy(tri_r[:], tri[:]).then_inc(S["ready"], 1)
                v.tensor_copy(ident_r[:], s.ident[:]).then_inc(S["ready"], 1)
                front(0, 0, 0)
                products(0, 0, (0, 1))
                body(0, 0)
                with v.Fori(0, NC // 2 - 1) as i:
                    with dve.turn(i, 6, NC // 2 - 1):
                        for n in (1, 0):
                            body(2 * i + 2 - n, n)
                forward(NC - 1, 1)
                backward(NC - 1, 1, True)

            @block.tensor
            def _(pe):
                def early(c, half, n):
                    pe.wait_ge(ld[n], 48 * (half + 1))
                    pe.wait_ge(c_in[n], 16 * (half + 1))
                    first = isinstance(c, int) and c == 0
                    if not first:
                        pe.wait_ge(S["cbm_ok"], c)
                    for g in range(GROUPS):
                        mm = pe.matmul(psCB[:, g, :], bT[n][:, g, :], cT[n][:, g, :], start=True, stop=True)
                    mm.then_inc(S["cb_ok"], 1)
                    pe.wait_ge(S["xw_ok"], c + 1)
                    if not first:
                        pe.wait_ge(S["h_ok"], c)
                    for g in range(GROUPS):
                        mm = pe.matmul(psS[:, g * 256:(g + 1) * 256], bt[n][:, g * NS:(g + 1) * NS],
                                       xw[:, g * 256:(g + 1) * 256], start=True, stop=True)
                    mm.then_inc(S["s_ok"], 1)

                def offset(c, state):
                    for g in range(GROUPS):
                        mm = pe.matmul(psO[:, g * 256:(g + 1) * 256], cT[c][:, g, :], state[:, g * 256:(g + 1) * 256],
                                       start=True, stop=True)
                    return mm

                def exponents(c, q):
                    if q == 0:
                        pe.wait_ge(row_in, 48 * (c + 1))
                    if not isinstance(c, int) or c > 0 or q > 0:
                        pe.wait_ge(S["exp_ok"], 8 * c + q)
                    out = psE[:].rearrange("p h l -> p (h l)")
                    pe.matmul(out, seg_l[:, q, :], seg_r[:, q * CH:(q + 1) * CH], start=True, stop=False)
                    pe.matmul(psE[:], ident_r[:], tri_r[:, q // 4].unsqueeze(1).to_broadcast([P, 4, P]), start=False,
                              stop=True).then_inc(S["seg_ok"], 1)

                beside = (2, 4, 5, 7, 9, 11, 13, 15)

                def inside(c, n, q, last):
                    pe.matmul(psY[:, q * CH:(q + 1) * CH], s.ident[:], xk[:, q * CH:(q + 1) * CH],
                              start=True, stop=False, skip_group_check=True)
                    for h in range(8 * q, 8 * q + 8):
                        if not last and h in beside:
                            exponents(c + 1, beside.index(h))
                        for d in range(2):
                            mm = pe.matmul(psY[:, h * HD:(h + 1) * HD], dec[n][:, d * HEADS + h, :],
                                           xd[n][:, d, h * HD:(h + 1) * HD], start=False,
                                           stop=(h == 8 * q + 7 and d == 1), skip_group_check=True)
                    return mm

                def body(c, half, n, last=False):
                    first = isinstance(c, int) and c == 0
                    pe.wait_ge(S["m_ok"], 2 * c + 2)
                    pe.wait_ge(S["xd_ok"], 3 * c + 3)
                    if not first:
                        pe.wait_ge(S["t1_ok"], c)
                    inside(c, n, 0, last)
                    if not first:
                        pe.wait_ge(S["h_ok"], c)
                        pe.wait_ge(S["t2_ok"], c)
                    offset(n, r.hf[n]).then_inc(S["off_f_ok"], 1)
                    if not last:
                        early(c + 1, half, 1 - n)
                    inside(c, n, 1, last).then_inc(S["yd_ok"], 1)
                    pe.wait_ge(S["t1_ok"], c + 1)
                    offset(n, r.hb[:, c, :]).then_inc(S["off_b_ok"], 1)

                pe.wait_ge(S["ready"], 2)
                early(0, 0, 0)
                for q in range(8):
                    exponents(0, q)
                body(0, 0, 0)
                with pe.Fori(0, NC // 2 - 1) as i:
                    for n in (1, 0):
                        body(2 * i + 2 - n, i + 1, n)
                body(NC - 1, None, 1, True)


def ssd(nc, kit, a, s):
    with ExitStack() as ctx:
        sb = lambda *args: kit.sbuf(ctx, *args)
        r = Names()
        r.dt, r.acum, r.eac, r.wst, r.cdec = (sb("ssd_" + n, [P, TT, NDH]) for n in ("dt", "acum", "eac", "wst", "cdec"))
        r.dskip = sb("ssd_dskip", [P, HEADS])
        ssd_decays(nc, kit, a, s, r)
        r.hb = sb("ssd_hb", [P, LT + 2, W_HALF])
        r.hf = [sb(f"ssd_hf{n}", [P, W_HALF]) for n in range(2)]
        ssd_states(nc, kit, a, s, r)
        ssd_outputs(nc, kit, a, s, r)


def walk_tiles(eng, body, tally=None, per=0):
    body(0, 0)
    with eng.Fori(0, LT // 2 - 1) as i:
        if tally is None:
            for n in (1, 0):
                body(2 * i + 2 - n, n)
        else:
            with tally.turn(i, 2 * per, LT // 2 - 1):
                for n in (1, 0):
                    body(2 * i + 2 - n, n)
    body(LT - 1, 1)


def starts(t):
    return isinstance(t, int) and t == 0


def ends(t):
    return isinstance(t, int) and t == LT - 1


def rows_at(t, i):
    return t[i * P:(i + 1) * P, :] if isinstance(i, int) else t[bass.ds(i * P, P), :]


def cols_at(t, i):
    t = t.rearrange("k c n -> c k n")
    return t[:, :, i * P:(i + 1) * P] if isinstance(i, int) else t[:, :, bass.ds(i * P, P)]


def mix_out(nc, kit, a, s):
    MT = 2 * KT
    with ExitStack() as ctx:
        sb = lambda *args: kit.sbuf(ctx, *args)
        w_hi, w_lo = sb("wo_hi", [P, MT, D], F32R), sb("wo_lo", [P, MT, D], F32R)
        pw = sb("pool_w_sb", [P, 4, 2, 256])
        gate, fnorm = sb("gate_row_sb", [P, D]), sb("final_norm_row", [P, D])
        dt_, zp, g, xt = (sb(n, [P, D]) for n in ("m_d", "m_zp", "m_g", "m_x"))
        piece = (dt_, zp, g, xt)
        y_hi = [sb(f"m_y_hi{n}", [P, MT, P], F32R) for n in range(2)]
        y_lo = [sb(f"m_y_lo{n}", [P, MT, P], F32R) for n in range(2)]
        rt, hn = sb("m_res", [P, D]), sb("m_hn", [P, D])
        h2t = sb("m_h2", [P, D])
        junk = sb("m_junk", [P, D], mybir.dt.bfloat16)
        st4 = sb("m_group_stat", [P, 3, GROUPS])
        st1 = sb("m_stat", [P, 8])
        bn = sb("m_bn", [P, 2, 6])
        mv, spare = sb("m_meanvar", [P, 2]), sb("m_spare", [P, 1])
        psP, psG, psH = (kit.psum(ctx, n, [P, KT, P]) for n in ("psPool", "psG", "psH"))
        psM = kit.psum(ctx, "psMix", [P, 2, CH])
        tiles = lambda t: t[:].rearrange("p (k n) -> p k n", n=P)
        k = kit
        S = k.sems("m_", ("rows_in", "scaled", "w_hi_ok", "w_lo_ok", "ssq", "root4", "gs", "yp", "hi_p", "hi_g", "lo_p", "lo_g",
                  "pool", "turn_g", "turn_h", "half", "r", "sq", "root", "x1", "mv", "root2", "hn", "ev_a", "ev_v",
                  "d_in", "zp_in", "g_in", "x_in", "x1_out", "h2_out", "sum_ok"))
        p_in = [k.sem(f"m_piece_loaded{n}") for n in range(4)]
        dve = Tally(k.sem("m_dve_chain"))

        with nc.Block() as block:
            @block.sync
            def _(sp):
                for dst, src in ((gate[:], a["gate_rows"][:, 0:D]), (fnorm[:], a["final_norm"].partition_broadcast(P)),
                                 (pw[:], a["pool_w"])):
                    sp.dma_start(dst, src).then_inc(S["rows_in"], 16)
                for q in range(MT):
                    if q >= 4:
                        sp.wait_ge(S["w_lo_ok"], q - 3)
                    sp.dma_start(piece[q % 4][:], a["w_out"][:, q, :]).then_inc(p_in[q % 4], 16)
                sp.wait_ge(S["w_lo_ok"], MT)

                def load(t):
                    if not starts(t):
                        sp.wait_ge(S["pool"], t)
                    sp.dma_start(tiles(dt_), cols_at(a["dT"], t)).then_inc(S["d_in"], 16)
                    if not starts(t):
                        sp.wait_ge(S["lo_p"], t)
                    sp.dma_start(tiles(zp), cols_at(a["zpT"], t)).then_inc(S["zp_in"], 16)
                    if not starts(t):
                        sp.wait_ge(S["turn_g"], t)
                    sp.dma_start(g[:], rows_at(a["g_tok"], t)).then_inc(S["g_in"], 16)

                load(0)
                sp.dma_start(xt[:], rows_at(a["x"], 0)).then_inc(S["x_in"], 16)
                load(1)

                def body(t, n):
                    if not ends(t) and not (isinstance(t, int) and t == LT - 2):
                        load(t + 2)
                    sp.wait_ge(S["x1"], t + 1)
                    if not ends(t):
                        sp.dma_start(xt[:], rows_at(a["x"], t + 1)).then_inc(S["x_in"], 16)
                    sp.dma_start(rows_at(a["x1"], t), rt[:]).then_inc(S["x1_out"], 16)

                def h2(t):
                    sp.wait_ge(S["ev_a"], t + 1)
                    sp.wait_ge(S["ev_v"], t + 1)
                    sp.dma_start(cols_at(a["h2T"], t), tiles(h2t)).then_inc(S["h2_out"], 16)

                body(0, 0)
                with sp.Fori(1, LT - 2) as t:
                    body(t, 0)
                    h2(t - 1)
                body(LT - 2, 0)
                h2(LT - 3)
                body(LT - 1, 1)
                h2(LT - 2)
                h2(LT - 1)
                sp.wait_ge(S["x1_out"], 16 * LT)
                sp.wait_ge(S["h2_out"], 16 * LT)

            @block.scalar
            def _(act):
                for q in range(MT):
                    v_at = V_PSCALE + q if q < KT else V_SNORM + q - KT
                    act.wait_ge(S["scaled"], q + 1)
                    act.activation(w_hi[:, q, :], piece[q % 4][:], ACT.Copy,
                                   scale=s.cols1[:, v_at:v_at + 1]).then_inc(S["w_hi_ok"], 1)

                def squares(t):
                    act.wait_ge(S["g_in"], 16 * (t + 1))
                    if not starts(t):
                        act.wait_ge(S["gs"], t)
                    for q in range(GROUPS):
                        ins = act.activation(junk[:, q * 256:(q + 1) * 256], g[:, q * 256:(q + 1) * 256], ACT.Square,
                                             accum_out=st4[:, 0, q:q + 1])
                        ins.then_inc(S["ssq"], 1)
                    act.wait_ge(S["ssq"], GROUPS * (t + 1))
                    act.activation(st4[:, 1, :], st4[:, 0, :], ACT.Sqrt, scale=1.0 / 256,
                                   bias=s.eps[:, 0:1]).then_inc(S["root4"], 1)

                def highs(t, n):
                    act.wait_ge(S["yp"], t + 1)
                    if not starts(t) and not (isinstance(t, int) and t == 1):
                        act.wait_ge(S["half"], 2 * (t - 1))
                    act.activation(y_hi[n][:, 0:KT, :], tiles(zp), ACT.Copy).then_inc(S["hi_p"], 1)
                    act.wait_ge(S["turn_g"], t + 1)
                    act.activation(y_hi[n][:, KT:MT, :], psG[:], ACT.Copy).then_inc(S["hi_g"], 1)

                def evacuate(t):
                    act.wait_ge(S["turn_h"], t + 1)
                    if not starts(t):
                        act.wait_ge(S["h2_out"], 16 * t)
                    for q in range(KT // 2):
                        ins = act.activation(tiles(h2t)[:, q, :], psH[:, q, :], ACT.Identity,
                                             scale=s.mod2[:, 1, q:q + 1], bias=s.mod2[:, 0, q:q + 1])
                    ins.then_inc(S["ev_a"], 1)

                def body(t, n):
                    if not ends(t):
                        squares(t + 1)
                        highs(t + 1, 1 - n)
                    if not starts(t):
                        evacuate(t - 1)
                    act.wait_ge(S["r"], 2 * (t + 1))
                    for q in range(2):
                        ins = act.activation(hn[:, q * CH:(q + 1) * CH], rt[:, q * CH:(q + 1) * CH], ACT.Square,
                                             accum_out=st1[:, q:q + 1])
                        ins.then_inc(S["sq"], 1)
                    act.wait_ge(S["sum_ok"], t + 1)
                    act.activation(st1[:, 3:4], st1[:, 2:3], ACT.Sqrt, scale=1.0 / D, bias=s.eps[:, 0:1]).then_inc(S["root"], 1)
                    act.wait_ge(S["mv"], t + 1)
                    act.activation(st1[:, 5:6], mv[:, 1:2], ACT.Sqrt, bias=s.eps[:, 1:2]).then_inc(S["root2"], 1)

                squares(0)
                highs(0, 0)
                walk_tiles(act, body)
                evacuate(LT - 1)

            @block.vector
            def _(v):
                def step(ins):
                    dve.mark(ins)
                    v.wait_ge(dve.sem, dve.value)

                v.wait_ge(S["rows_in"], 48)

                def gated(q):
                    b = piece[q % 4]
                    v.wait_ge(p_in[q % 4], 16 * (q // 4 + 1))
                    v.tensor_tensor(b[:], b[:], gate[:], ALU.mult).then_inc(S["scaled"], 1)

                gated(0)
                for q in range(MT):
                    b = piece[q % 4]
                    v_at = V_PSCALE + q if q < KT else V_SNORM + q - KT
                    if q < MT - 1:
                        gated(q + 1)
                    v.wait_ge(S["w_hi_ok"], q + 1)
                    v.scalar_tensor_tensor(w_lo[:, q, :], b[:], s.cols1[:, v_at:v_at + 1], w_hi[:, q, :].bitcast(F32),
                                           ALU.mult, ALU.subtract).then_inc(S["w_lo_ok"], 1)

                def normed_g(t):
                    v.wait_ge(S["root4"], t + 1)
                    step(v.reciprocal(st4[:, 2, :], st4[:, 1, :]))
                    g4 = g[:].rearrange("p (q c) -> p q c", c=256)
                    v.tensor_tensor(g4, g4, st4[:, 2, :].unsqueeze(2).to_broadcast([P, GROUPS, 256]),
                                    ALU.mult).then_inc(S["gs"], 1)

                def operands(t, n):
                    v.wait_ge(S["pool"], t + 1)
                    v.wait_ge(S["zp_in"], 16 * (t + 1))
                    v.tensor_tensor(tiles(zp), psP[:], tiles(zp), ALU.mult).then_inc(S["yp"], 1)
                    v.wait_ge(S["hi_p"], t + 1)
                    v.tensor_tensor(y_lo[n][:, 0:KT, :], tiles(zp), y_hi[n][:, 0:KT, :].bitcast(F32),
                                    ALU.subtract).then_inc(S["lo_p"], 1)
                    v.wait_ge(S["hi_g"], t + 1)
                    v.tensor_tensor(y_lo[n][:, KT:MT, :], psG[:], y_hi[n][:, KT:MT, :].bitcast(F32),
                                    ALU.subtract).then_inc(S["lo_g"], 1)

                def residual(t, q):
                    v.wait_ge(S["half"], 2 * t + q + 1)
                    if q == 0:
                        v.wait_ge(S["x_in"], 16 * (t + 1))
                        if not starts(t):
                            v.wait_ge(S["x1_out"], 16 * t)
                            v.wait_ge(S["hn"], t)
                    v.tensor_tensor(rt[:, q * CH:(q + 1) * CH], psM[:, q, :], xt[:, q * CH:(q + 1) * CH],
                                    ALU.add).then_inc(S["r"], 1)

                def evacuate(t):
                    v.wait_ge(S["turn_h"], t + 1)
                    if not starts(t):
                        v.wait_ge(S["h2_out"], 16 * t)
                    for q in range(KT // 2, KT):
                        ins = v.tensor_scalar(tiles(h2t)[:, q, :], psH[:, q, :], s.mod2[:, 1, q:q + 1],
                                              s.mod2[:, 0, q:q + 1], ALU.mult, ALU.add)
                    ins.then_inc(S["ev_v"], 1)

                def body(t, n):
                    if not ends(t):
                        normed_g(t + 1)
                    residual(t, 0)
                    if not ends(t):
                        operands(t + 1, 1 - n)
                    if not starts(t):
                        evacuate(t - 1)
                    residual(t, 1)
                    v.wait_ge(S["sq"], 2 * (t + 1))
                    v.tensor_tensor(st1[:, 2:3], st1[:, 0:1], st1[:, 1:2], ALU.add).then_inc(S["sum_ok"], 1)
                    v.wait_ge(S["root"], t + 1)
                    step(v.reciprocal(st1[:, 4:5], st1[:, 3:4]))
                    v.wait_ge(S["r"], 2 * (t + 1))
                    v.scalar_tensor_tensor(rt[:], rt[:], st1[:, 4:5], fnorm[:], ALU.mult, ALU.mult).then_inc(S["x1"], 1)
                    v.wait_ge(S["x1"], t + 1)
                    v.bn_stats(bn[:, 0, :], rt[:, 0:CH])
                    step(v.bn_stats(bn[:, 1, :], rt[:, CH:D]))
                    v.memset(spare[:], 0.0)
                    v.bn_aggr(mv[:], bn[:].rearrange("p a b -> p (a b)")).then_inc(S["mv"], 1)
                    v.wait_ge(S["root2"], t + 1)
                    step(v.reciprocal(st1[:, 6:7], st1[:, 5:6]))
                    v.tensor_scalar(hn[:], rt[:], mv[:, 0:1], st1[:, 6:7], ALU.subtract, ALU.mult).then_inc(S["hn"], 1)

                normed_g(0)
                operands(0, 0)
                body(0, 0)
                with v.Fori(0, LT // 2 - 1) as i:
                    with dve.turn(i, 8, LT // 2 - 1):
                        for n in (1, 0):
                            body(2 * i + 2 - n, n)
                body(LT - 1, 1)
                evacuate(LT - 1)

            @block.tensor
            def _(pe):
                def front(t, n):
                    pe.wait_ge(S["d_in"], 16 * (t + 1))
                    if not starts(t):
                        pe.wait_ge(S["yp"], t)
                    for o in range(KT):
                        for q in range(2):
                            mm = pe.matmul(psP[:, o, :], pw[:, o // 2, q, (o % 2) * P:(o % 2 + 1) * P],
                                           tiles(dt_)[:, 2 * (o // 2) + q, :], start=(q == 0), stop=(q == 1))
                    mm.then_inc(S["pool"], 1)
                    pe.wait_ge(S["gs"], t + 1)
                    if not starts(t):
                        pe.wait_ge(S["lo_g"], t)
                    for q in range(KT):
                        mm = pe.transpose(psG[:, q, :], g[:, q * P:(q + 1) * P], s.ident[:])
                    mm.then_inc(S["turn_g"], 1)

                def turned_norm(t):
                    pe.wait_ge(S["hn"], t + 1)
                    if not starts(t):
                        pe.wait_ge(S["ev_a"], t)
                        pe.wait_ge(S["ev_v"], t)
                    for q in range(KT):
                        mm = pe.transpose(psH[:, q, :], hn[:, q * P:(q + 1) * P], s.ident[:])
                    mm.then_inc(S["turn_h"], 1)

                def half(t, n, h):
                    if h == 0:
                        pe.wait_ge(S["lo_g"], t + 1)
                    if not starts(t):
                        pe.wait_ge(S["r"], 2 * t + h - 1)
                    for q in range(MT):
                        for j, (y, w) in enumerate(((y_hi, w_hi), (y_hi, w_lo), (y_lo, w_hi))):
                            if starts(t) and j == 0:
                                pe.wait_ge(S["w_lo_ok"], q + 1)
                            mm = pe.matmul(psM[:, h, :], y[n][:, q, :], w[:, q, h * CH:(h + 1) * CH],
                                           start=(q == 0 and j == 0), stop=(q == MT - 1 and j == 2))
                    mm.then_inc(S["half"], 1)

                def body(t, n):
                    half(t, n, 0)
                    if not ends(t):
                        front(t + 1, 1 - n)
                    if not starts(t):
                        turned_norm(t - 1)
                    half(t, n, 1)

                pe.wait_ge(S["rows_in"], 48)
                front(0, 0)
                walk_tiles(pe, body)
                turned_norm(LT - 1)


def split_h2(nc, kit, a, hT):
    hi, lo = hT
    with ExitStack() as ctx:
        h = [kit.sbuf(ctx, f"h2_raw{n}", [P, SEQ]) for n in range(2)]
        ld = [kit.sem(f"h2_loaded{n}") for n in range(2)]
        hi_ok, lo_ok = kit.sem("h2_hi_ready"), kit.sem("h2_lo_ready")
        with nc.Block() as block:
            @block.sync
            def _(sp):
                for q in range(KT):
                    if q >= 2:
                        sp.wait_ge(lo_ok, q - 1)
                    sp.dma_start(h[q % 2][:], a["h2T"][q]).then_inc(ld[q % 2], 16)

            @block.scalar
            def _(act):
                for q in range(KT):
                    act.wait_ge(ld[q % 2], 16 * (q // 2 + 1))
                    act.activation(hi[:, q, :], h[q % 2][:], ACT.Copy).then_inc(hi_ok, 1)

            @block.vector
            def _(v):
                for q in range(KT):
                    v.wait_ge(hi_ok, q + 1)
                    v.tensor_tensor(lo[:, q, :], h[q % 2][:], hi[:, q, :].bitcast(F32), ALU.subtract).then_inc(lo_ok, 1)


def projection2(nc, kit, a, s):
    with ExitStack() as ctx:
        hT = (kit.sbuf(ctx, "h2T_hi", [P, KT, SEQ], F32R), kit.sbuf(ctx, "h2T_lo", [P, KT, SEQ], F32R))
        split_h2(nc, kit, a, hT)
        kinds = [
            Kind(XR0, 4, 4, "conv", stored=a["xcT"]),
            Kind(ZR0, 4, 4, "copy", stored=a["zrT"], func=ACT.Silu),
            Kind(QK0, 8, 4, "copy", stored=a["qkT"]),
            Kind(VZ0, 8, 4, "copy", turned=a["va_tok"]),
            Kind(FL0, 1, 4, "copy", stored=a["flT"], width=NH2),
        ]
        conv = Conv(s.cols2, V2_CONVW, V2_CONVB, 4, {XR0: 0}, 3, SEQ, ACT.Identity)
        plan = [("one", b) for b in range(10)] + [("loop", 10, 3), ("one", 16), ("one", 17), ("loop", 18, 2)] + \
               [("one", b) for b in range(22, NBLK2)]
        project(nc, kit, a, s, "p2", kinds, plan, hT, a["w_in_2"], conv, False)


def lru(nc, kit, a, s):
    NT = W2 // P
    with ExitStack() as ctx:
        sb = lambda *args: kit.sbuf(ctx, *args)
        xc, rr, ii, rt, zr = (sb(f"l_{n}", [P, NT, SEQ]) for n in ("xc", "gate_a", "gate_x", "root", "zr"))
        inv = [sb(f"l_inv{n}", [P, SEQ]) for n in range(2)]
        dec = [sb(f"l_decay{n}", [P, SEQ]) for n in range(2)]
        wg = sb("l_gate_w", [P, 2, NT, P])
        sp_t = [sb(f"l_sp{n}", [P, NT]) for n in range(3)]
        lam, halfc = sb("l_neg_lambda", [P, NT]), sb("l_half_c", [P, NT])
        ones = sb("l_ones", [P, 2])
        ms = sb("l_mean_square", [P, 2, LT])
        ps = kit.psum(ctx, "l_ps", [P, 4, CH])
        psQ = kit.psum(ctx, "l_psQ", [P, LT, 2])
        k = kit
        S = k.sems("l_", ("w_zero", "w_in", "gate", "sig", "ask", "exp", "halfc", "tanh", "root", "ix", "u", "h",
                          "sq", "hz", "out", "sum", "rms"))
        x_in, z_in = [k.sem(f"l_x_loaded{n}") for n in range(NT)], k.sem("l_z_loaded")
        dve = Tally(k.sem("l_dve_chain"))
        with nc.Block() as block:
            @block.sync
            def _(sp):
                for q in range(NT):
                    sp.dma_start(xc[:, q, :], a["xcT"][q]).then_inc(x_in[q], 16)
                sp.wait_ge(S["w_zero"], 1)
                for g, w in enumerate((a["w_gate_a"], a["w_gate_x"])):
                    wb = w.rearrange("(t h) d e -> h d t e", h=2)
                    for h in range(2):
                        sp.dma_start(wg[h * 64:(h + 1) * 64, g, :, h * 64:(h + 1) * 64], wb[h]).then_inc(S["w_in"], 16)
                sp.dma_start(zr[:], a["zrT"].rearrange("k p n -> p k n")).then_inc(z_in, 16)
                for q in range(NT):
                    sp.wait_ge(S["hz"], q + 1)
                    sp.dma_start(a["hzT"][q], zr[:, q, :]).then_inc(S["out"], 16)
                sp.wait_ge(S["out"], 16 * NT)

            @block.tensor
            def _(pe):
                pe.wait_ge(S["w_in"], 64)
                for q in range(NT):
                    pe.wait_ge(x_in[q], 16)
                    for g in range(2):
                        for c in range(4):
                            m = (2 * q + g) * 4 + c
                            if m >= 4:
                                pe.wait_ge(S["sig"], m - 3)
                            pe.matmul(ps[:, c, :], wg[:, g, q, :], xc[:, q, c * CH:(c + 1) * CH], start=True,
                                      stop=True).then_inc(S["gate"], 1)
                pe.wait_ge(S["sq"], NT)
                for t in range(LT):
                    for q in range(NT):
                        mm = pe.matmul(psQ[:, t, :], rr[:, q, t * P:(t + 1) * P], ones[:], start=(q == 0),
                                       stop=(q == NT - 1))
                mm.then_inc(S["sum"], 1)

            @block.scalar
            def _(act):
                act.wait_ge(S["ask"], 1)
                act.activation(sp_t[0][:], sp_t[0][:], ACT.Exp).then_inc(S["exp"], 1)
                for q in range(NT):
                    for g, (dst, at) in enumerate(((rr, V2_BA), (ii, V2_BX))):
                        for c in range(4):
                            act.wait_ge(S["gate"], (2 * q + g) * 4 + c + 1)
                            act.activation(dst[:, q, c * CH:(c + 1) * CH], ps[:, c, :], ACT.Sigmoid,
                                           bias=s.cols2[:, at + q:at + q + 1]).then_inc(S["sig"], 1)
                act.wait_ge(S["halfc"], 1)
                act.wait_ge(S["sig"], 32)
                for q in range(NT):
                    act.activation(rr[:, q, :], rr[:, q, :], ACT.Tanh, scale=halfc[:, q:q + 1]).then_inc(S["tanh"], 1)
                for q in range(NT):
                    act.wait_ge(S["tanh"], q + 1)
                    act.activation(rt[:, q, :], rr[:, q, :], ACT.Sqrt).then_inc(S["root"], 1)
                for q in range(NT):
                    act.wait_ge(S["h"], q + 1)
                    act.activation(rr[:, q, :], xc[:, q, :], ACT.Square).then_inc(S["sq"], 1)
                act.wait_ge(S["sum"], 1)
                act.activation(ms[:, 0, :], psQ[:, :, 0], ACT.Sqrt, scale=1.0 / W2, bias=s.eps[:, 1:2]).then_inc(S["rms"], 1)

            @block.gpsimd
            def _(g):
                g.memset(wg[:], 0.0).then_inc(S["w_zero"], 1)
                for q in range(NT):
                    g.wait_ge(S["sig"], 8 * (q + 1))
                    g.tensor_tensor(ii[:, q, :], ii[:, q, :], xc[:, q, :], ALU.mult).then_inc(S["ix"], 1)

            @block.vector
            def _(v):
                def step(ins):
                    dve.mark(ins)
                    v.wait_ge(dve.sem, dve.value)

                def ask():
                    v.nop().then_inc(S["ask"], 1)
                    v.wait_ge(S["exp"], 1)

                step(v.memset(ones[:], 1.0))
                step(v.tensor_scalar(lam[:], s.cols2[:, V2_LAM:V2_LAM + NT], -1.0, None, ALU.mult))
                softplus(v, step, ask, halfc[:], lam[:], [t[:] for t in sp_t])
                v.tensor_scalar(halfc[:], halfc[:], LRU_C / 2, None, ALU.mult).then_inc(S["halfc"], 1)
                for q in range(NT):
                    iv, de = inv[q % 2], dec[q % 2]
                    v.wait_ge(S["tanh"], q + 1)
                    step(v.tensor_scalar(iv[:], rr[:, q, :], 1.0, None, ALU.add))
                    step(v.reciprocal(iv[:], iv[:]))
                    step(v.tensor_scalar(de[:], iv[:], 2.0, -1.0, ALU.mult, ALU.add))
                    v.wait_ge(S["root"], q + 1)
                    step(v.scalar_tensor_tensor(iv[:], rt[:, q, :], 2.0, iv[:], ALU.mult, ALU.mult))
                    v.wait_ge(S["ix"], q + 1)
                    step(v.tensor_tensor(ii[:, q, :], ii[:, q, :], iv[:], ALU.mult))
                    v.tensor_tensor_scan(xc[:, q, :], de[:], ii[:, q, :], 0.0, ALU.mult, ALU.add).then_inc(S["h"], 1)
                    v.wait_ge(S["h"], q + 1)
                    v.wait_ge(z_in, 16)
                    v.tensor_tensor(zr[:, q, :], zr[:, q, :], xc[:, q, :], ALU.mult).then_inc(S["hz"], 1)
                v.wait_ge(S["rms"], 1)
                v.reciprocal(s.rstd_r[:], ms[:, 0, :])


def forget_sums(nc, kit, a, s):
    with ExitStack() as ctx:
        sb = lambda *args: kit.sbuf(ctx, *args)
        x, out = sb("f_x", [P, P]), sb("f_out", [P, P])
        t = [sb(f"f_sp{n}", [P, P]) for n in range(3)]
        b = sb("f_bias", [P, 1])
        rows, one, sums = sb("f_rows", [NH2, SEQ]), sb("f_ones", [NH2, SEQ]), sb("f_sums", [NH2, SEQ])
        whole = sb("f_scaled", [NH2, SEQ])
        parts = [sb(f"f_part{n}", [NH2, SEQ], F32R) for n in range(2)]
        S = kit.sems("f_", ("fl_in", "ask", "exp", "soft", "soft_out", "rows_in", "sums", "out"))
        dve = Tally(kit.sem("f_dve_chain"))
        with nc.Block() as block:
            @block.sync
            def _(sp):
                sp.dma_start(x[:], a["flT"].rearrange("o h (s l) -> (o h s) l", l=P)).then_inc(S["fl_in"], 16)
                sp.dma_start(b[:], a["b_fgate"]).then_inc(S["fl_in"], 16)
                sp.wait_ge(S["soft"], 1)
                sp.dma_start(a["softf"], out[:]).then_inc(S["soft_out"], 16)
                sp.wait_ge(S["soft_out"], 16)
                sp.dma_start(rows[:], a["softf"].rearrange("(h s) l -> h (s l)", h=NH2)).then_inc(S["rows_in"], 16)
                sp.wait_ge(S["sums"], 2)
                for n in range(2):
                    sp.dma_start(a["forget"][:, n, :], parts[n][:].bitcast(F32)).then_inc(S["out"], 16)
                sp.wait_ge(S["out"], 32)

            @block.scalar
            def _(act):
                act.wait_ge(S["ask"], 1)
                act.activation(t[0][:], t[0][:], ACT.Exp).then_inc(S["exp"], 1)

            @block.vector
            def _(v):
                def step(ins):
                    dve.mark(ins)
                    v.wait_ge(dve.sem, dve.value)

                def ask():
                    v.nop().then_inc(S["ask"], 1)
                    v.wait_ge(S["exp"], 1)

                step(v.memset(one[:], 1.0))
                v.wait_ge(S["fl_in"], 32)
                step(v.tensor_scalar(x[:], x[:], b[:], -1.0, ALU.add, ALU.mult))
                softplus(v, step, ask, out[:], x[:], [q[:] for q in t])
                v.nop().then_inc(S["soft"], 1)
                v.wait_ge(S["rows_in"], 16)
                step(v.tensor_tensor_scan(sums[:], one[:], rows[:], 0.0, ALU.mult, ALU.add))
                step(v.tensor_scalar(whole[:], sums[:], 8.0, None, ALU.mult))
                v.tensor_copy(parts[0][:], whole[:]).then_inc(S["sums"], 1)
                v.wait_ge(S["sums"], 1)
                v.tensor_tensor(parts[1][:], whole[:], parts[0][:].bitcast(F32), ALU.subtract).then_inc(S["sums"], 1)


def attention(nc, kit, a, s, y, za):
    VD, QT = HD2 + 1, SEQ // P
    KB_ROWS, KM_ROWS = HD2 + 4, HD2 + 2
    pairs = [(qc, 2 * m, CH // 2 if m == 2 * qc + 1 else 0) for qc in range(NCH) for m in range(2 * qc + 2)]
    last_of = [max(p for p, x in enumerate(pairs) if x[0] == qc) for qc in range(NCH)]
    NPR = len(pairs)
    chunks = [(j, c) for j in range(QT) for c in range(j // 4 + 1)]
    NCK = len(chunks)
    M_FROM, M_PER = 6, 4
    M_TURN = M_FROM + NCK // M_PER
    TURNS = NCH + 1
    with ExitStack() as ctx:
        sb = lambda *args: kit.sbuf(ctx, *args)
        rk, rq = sb("t_k_raw", [P, SEQ]), sb("t_q_raw", [P, SEQ])
        KA, QA = ([sb(f"t_{m}{n}", [P, SEQ], F32R) for n in range(2)] for m in ("KA", "QA"))
        KB, QB = ([sb(f"t_{m}{n}", [KB_ROWS, SEQ], F32R) for n in range(2)] for m in ("KB", "QB"))
        KM = [sb(f"t_KM{n}", [KM_ROWS, SEQ], F32R) for n in range(2)]
        va = [sb(f"t_v{n}", [P, QT, VD + 1]) for n in range(2)]
        pt = [sb(f"t_prob{n}", [P, 2, CH]) for n in range(2)]
        ot, spare = sb("t_out_turned", [VD, CH]), sb("t_spare", [P, 1])
        causal, full = sb("t_causal", [P, 2, P]), sb("t_full", [P, P])
        ident_r, mask_q, mask_k = sb("t_ident", [P, P], F32R), sb("t_mask_q", [P, P], F32R), sb("t_mask_k", [P, 2 * P], F32R)
        mx, top, rc = sb("t_chunk_max", [P, QT, 4]), sb("t_max", [P, QT]), sb("t_sum_inverse", [P, 4])
        m_hi, m_lo = sb("t_max_hi", [QT, P], F32R), sb("t_max_lo", [QT, P], F32R)
        psM = kit.psum(ctx, "t_psM", [P, 2, CH])
        psS = [kit.psum(ctx, f"t_psS{n}", [P, 2, CH]) for n in range(2)]
        psO = kit.psum(ctx, "t_psO", [VD, CH])
        psX = kit.psum(ctx, "t_psX", [P, CH])
        turned_y = psX[:, 0:4 * VD].rearrange("p (t d) -> p t d", d=VD)
        S = kit.sems("t_", ("tables_in", "ready", "raw_in", "act_split", "dve_split", "first", "first_read", "max",
                            "x_turned", "x_read", "logits", "prob", "pv", "out_read", "spare", "za_in"))
        row_in = [kit.sem(f"t_rows_loaded{n}") for n in range(2)]
        max_in = [kit.sem(f"t_max_loaded{n}") for n in range(2)]
        dve = Tally(kit.sem("t_dve_chain"))
        NP = NH2 // 2

        def walk(eng, head):
            with eng.Fori(0, NP - 1) as i:
                for n in range(2):
                    head(2 * i + n, i, n, False)
            for n in range(2):
                head(NH2 - 2 + n, NP - 1, n, n == 1)

        with nc.Block() as block:
            @block.sync
            def _(sp):
                heads = a["qkT"].rearrange("b (h d) n -> (b h) d n", d=HD2)
                def raw(h):
                    for dst, src in ((rk, heads[h + NH2]), (rq, heads[h])):
                        for half in range(2):
                            sp.dma_start(dst[half * HD2:(half + 1) * HD2, :], src).then_inc(S["raw_in"], 16)

                raw(0)
                for dst, src in ((causal[:, 0], a["causal"]), (causal[:, 1], a["causal_turned"])):
                    sp.dma_start(dst, src).then_inc(S["tables_in"], 16)
                def head(h, i, n, last):
                    if not last:
                        sp.wait_ge(S["act_split"], 6 * h + 6)
                        sp.wait_ge(S["dve_split"], 6 * h + 6)
                        raw(h + 1)
                walk(sp, head)
                sp.dma_start(za[:], a["va_tok"].rearrange("(t p) c -> p t c", p=P)[:, :, W2:2 * W2]).then_inc(S["za_in"], 16)
                sp.wait_ge(S["za_in"], 16)

            @block.gpsimd
            def _(g):
                heads_v = a["va_tok"].rearrange("(t p) (h d) -> h p t d", p=P, d=HD2)

                def rows(h, n):
                    g.dma_start(KM[n][HD2:HD2 + 2, :], a["forget"][h]).then_inc(row_in[n], 16)
                    g.dma_start(KB[n][HD2:HD2 + 2, :], a["forget"][h]).then_inc(row_in[n], 16)
                    g.dma_start(va[n][:, :, 0:HD2], heads_v[h]).then_inc(row_in[n], 16)

                def maxima(h, n, turns):
                    if not isinstance(h, int) or h > 0:
                        g.wait_ge(S["spare"], h)
                    g.wait_ge(S["x_read"], turns)
                    g.tensor_tensor(spare[:], s.eps[:, 0:1], s.eps[:, 0:1], ALU.add).then_inc(S["spare"], 1)
                    for row, src in enumerate((m_hi, m_lo)):
                        g.dma_start(QB[n][HD2 + 2 + row:HD2 + 3 + row, :], src[:].bitcast(F32)).then_inc(max_in[n], 16)

                g.wait_ge(S["ready"], 1)
                rows(0, 0)
                maxima(0, 0, 1)

                def head(h, i, n, last):
                    if not last:
                        g.wait_ge(S["pv"], h * NPR + 2)
                        rows(h + 1, 1 - n)
                        maxima(h + 1, 1 - n, h * TURNS + 1 + NCH)
                walk(g, head)

            @block.tensor
            def _(pe):
                def first_pass(h, i, n, cs):
                    for m in cs:
                        j, c = chunks[m]
                        if m == 0:
                            pe.wait_ge(S["act_split"], 6 * h + 6)
                            pe.wait_ge(S["dve_split"], 6 * h + 6)
                            pe.wait_ge(row_in[n], 48 * (i + 1))
                        if not isinstance(h, int) or h > 0 or m >= 2:
                            pe.wait_ge(S["first_read"], h * NCK + m - 1)
                        w = min(CH, (j + 1) * P - c * CH)
                        edge = c == j // 4
                        mm = pe.matmul(psM[:, m % 2, 0:w], QB[n][0:KM_ROWS, j * P:(j + 1) * P],
                                       KM[n][:, c * CH:c * CH + w], start=True, stop=not edge, skip_group_check=True)
                        if edge:
                            mm = pe.matmul(psM[:, m % 2, w - P:w], ident_r[:], mask_q[:], start=False, stop=True,
                                           skip_group_check=True)
                        mm.then_inc(S["first"], 1)

                def logits(h, i, n, p):
                    qc, kt, off = pairs[p]
                    if p == 0:
                        pe.wait_ge(max_in[n], 32 * (i + 1))
                    if not isinstance(h, int) or h > 0 or p > 0:
                        pe.wait_ge(S["prob"], h * NPR + p)
                    for e in range(2):
                        out = psS[p % 2][:, e, off:CH]
                        ks, qs = slice((kt + e) * P, (kt + e + 1) * P), slice(qc * CH + off, (qc + 1) * CH)
                        edge = kt >= 4 * qc
                        pe.matmul(out, KA[n][:, ks], QA[n][:, qs], start=True, stop=False, skip_group_check=True)
                        mm = pe.matmul(out, KB[n][:, ks], QB[n][:, qs], start=False, stop=not edge, skip_group_check=True)
                        if edge:
                            mm = pe.matmul(psS[p % 2][:, e, off:off + (e + 1) * P], ident_r[:],
                                           mask_k[:, (1 - e) * P:2 * P], start=False, stop=True, skip_group_check=True)
                    mm.then_inc(S["logits"], 1)

                def values(h, n, p):
                    qc, kt, off = pairs[p]
                    if kt == 0:
                        pe.wait_ge(S["out_read"], h * NCH + qc + 1)
                    pe.wait_ge(S["prob"], h * NPR + p + 2)
                    for e in range(2):
                        o = max(off, (kt + e) * P - qc * CH)
                        mm = pe.matmul(psO[:, o:CH], va[n][:, kt + e, 0:VD], pt[p % 2][:, e, o:CH],
                                       start=(kt + e == 0), stop=(kt + e == 4 * qc + 3), skip_group_check=True)
                    mm.then_inc(S["pv"], 1)

                def turn_out(h, qc, k):
                    pe.wait_ge(S["out_read"], h * NCH + qc + 2)
                    pe.wait_ge(S["x_read"], h * TURNS + 1 + k)
                    for t in range(4):
                        mm = pe.transpose(turned_y[:, t, :], ot[:, t * P:(t + 1) * P], s.ident[0:VD, 0:VD])
                    mm.then_inc(S["x_turned"], 1)

                def turn_max(before):
                    pe.wait_ge(S["max"], before["heads"])
                    if before["turns"] is not None:
                        pe.wait_ge(S["x_read"], before["turns"])
                    pe.transpose(psX[0:QT, 0:P], top[:], s.ident[:]).then_inc(S["x_turned"], 1)

                def head(h, i, n, last):
                    for p in range(NPR):
                        if p < NPR - 1:
                            logits(h, i, n, p + 1)
                        elif not last:
                            logits(h + 1, i + n, 1 - n, 0)
                        m = (p - M_FROM) * M_PER
                        beside = 0 <= m < NCK and not last
                        if beside:
                            first_pass(h + 1, i + n, 1 - n, range(m, m + M_PER // 2))
                        values(h, n, p)
                        for qc in range(NCH - 1):
                            if p == last_of[qc] + 1:
                                turn_out(h, qc, qc)
                        if beside:
                            first_pass(h + 1, i + n, 1 - n, range(m + M_PER // 2, m + M_PER))
                        if p == M_TURN and not last:
                            turn_max({"heads": h + 2, "turns": h * TURNS + NCH})
                    turn_out(h, NCH - 1, NCH - 1 if last else NCH)

                for _ in range(2):
                    pe.nop().then_inc(S["pv"], 1)
                pe.wait_ge(S["ready"], 1)
                first_pass(0, 0, 0, range(NCK))
                turn_max({"heads": 1, "turns": None})
                logits(0, 0, 0, 0)
                walk(pe, head)

            @block.scalar
            def _(act):
                def split(h, n, step, turns):
                    if step == 0:
                        act.wait_ge(S["raw_in"], 64 * h + 64)
                        if turns is not None:
                            act.wait_ge(S["pv"], turns)
                    cols = slice(step % 2 * (SEQ // 2), (step % 2 + 1) * (SEQ // 2))
                    dst, src, rows = ((KA[n], rk, P), (QA[n], rq, P), (QB[n], rq, HD2))[step // 2]
                    act.activation(dst[0:rows, cols], src[0:rows, cols], ACT.Copy).then_inc(S["act_split"], 1)

                def head(h, i, n, last):
                    for p in range(NPR):
                        off = pairs[p][2]
                        act.wait_ge(S["logits"], h * NPR + p + 1)
                        act.wait_ge(S["pv"], h * NPR + p + 1)
                        act.activation(pt[p % 2][:, :, off:CH], psS[p % 2][:, :, off:CH], ACT.Exp,
                                       scale=1.0 / 8).then_inc(S["prob"], 1)
                        if p < 6 and not last:
                            split(h + 1, 1 - n, p, h * NPR + 2)

                act.nop().then_inc(S["prob"], 1)
                act.wait_ge(S["ready"], 1)
                for step in range(6):
                    split(0, 0, step, None)
                walk(act, head)

            @block.vector
            def _(v):
                def step(ins):
                    dve.mark(ins)
                    v.wait_ge(dve.sem, dve.value)

                def split(h, n, k):
                    cols = slice(k % 2 * (SEQ // 2), (k % 2 + 1) * (SEQ // 2))
                    if k < 2:
                        v.wait_ge(S["act_split"], 6 * h + k + 1)
                        ins = v.tensor_tensor(KB[n][0:HD2, cols], rk[0:HD2, cols], KA[n][0:HD2, cols].bitcast(F32),
                                              ALU.subtract)
                    elif k < 4:
                        ins = v.tensor_copy(KM[n][0:HD2, cols], rk[0:HD2, cols])
                    else:
                        v.wait_ge(S["act_split"], 6 * h + k - 1)
                        ins = v.tensor_tensor(QA[n][HD2:P, cols], rq[HD2:P, cols], QA[n][HD2:P, cols].bitcast(F32),
                                              ALU.subtract)
                    ins.then_inc(S["dve_split"], 1)

                def first_max(h, cs):
                    for m in cs:
                        j, c = chunks[m]
                        v.wait_ge(S["first"], h * NCK + m + 1)
                        w = min(CH, (j + 1) * P - c * CH)
                        v.reduce_max(mx[:, j, c:c + 1], psM[:, m % 2, 0:w], axis=AX_X).then_inc(S["first_read"], 1)

                def head_max(h):
                    v.wait_ge(S["first_read"], h * NCK + NCK)
                    v.reduce_max(top[:], mx[:], axis=AX_X).then_inc(S["max"], 1)

                def split_max(turns):
                    v.wait_ge(S["x_turned"], turns)
                    step(v.tensor_scalar(m_hi[:], psX[0:QT, 0:P], -1.0, None, ALU.mult))
                    v.scalar_tensor_tensor(m_lo[:], psX[0:QT, 0:P], -1.0, m_hi[:].bitcast(F32), ALU.mult,
                                           ALU.subtract).then_inc(S["x_read"], 1)

                def read_out(h, p):
                    v.wait_ge(S["pv"], h * NPR + p + 3)
                    v.tensor_copy(ot[:], psO[:]).then_inc(S["out_read"], 1)

                def normal(h, qc, k):
                    v.wait_ge(S["x_turned"], h * TURNS + 2 + k)
                    step(v.reciprocal(rc[:], turned_y[:, :, HD2]))
                    dst = y[:, 4 * qc:4 * qc + 4, h * HD2:(h + 1) * HD2] if isinstance(h, int) \
                        else y[:, 4 * qc:4 * qc + 4, bass.ds(h * HD2, HD2)]
                    v.tensor_tensor(dst, turned_y[:, :, 0:HD2], rc[:].unsqueeze(2).to_broadcast([P, 4, HD2]),
                                    ALU.mult).then_inc(S["x_read"], 1)

                def head(h, i, n, last):
                    for p in range(NPR):
                        if not last:
                            if p < 6:
                                split(h + 1, 1 - n, p)
                            m = (p - M_FROM) * M_PER
                            if 0 <= m < NCK:
                                first_max(h + 1, range(m, m + M_PER))
                                if m + M_PER == NCK:
                                    head_max(h + 1)
                        for qc in range(NCH):
                            if p == last_of[qc]:
                                read_out(h, p)
                            if p == last_of[qc] + 1:
                                normal(h, qc, qc)
                        if p == M_TURN and not last:
                            split_max(h * TURNS + 1 + NCH)
                    normal(h, NCH - 1, NCH - 1 if last else NCH)

                v.memset(full[:], -1e30)
                v.memset(mx[:], -3e38)
                step(v.memset(pt[0][:], 1.0))
                for n in range(2):
                    v.memset(va[n][:, :, HD2:HD2 + 1], 1.0)
                    for dst in (KB[n], QB[n]):
                        for c in range(NCH):
                            v.tensor_copy(dst[HD2:HD2 + 4, c * CH:(c + 1) * CH], pt[0][HD2:HD2 + 4, 0, :])
                v.tensor_copy(ident_r[:], s.ident[:])
                v.wait_ge(S["tables_in"], 32)
                v.tensor_copy(mask_q[:], causal[:, 0])
                step(v.tensor_copy(mask_k[:, P:2 * P], causal[:, 1]))
                v.tensor_copy(mask_k[:, 0:P], full[:]).then_inc(S["ready"], 1)
                v.nop().then_inc(S["out_read"], 1)
                for k in range(6):
                    split(0, 0, k)
                first_max(0, range(NCK))
                head_max(0)
                split_max(1)
                with v.Fori(0, NP - 1) as i:
                    with dve.turn(i, 2 * (NCH + 1), NP - 1):
                        for n in range(2):
                            head(2 * i + n, i, n, False)
                for n in range(2):
                    head(NH2 - 2 + n, NP - 1, n, n == 1)


def out2(nc, kit, a, s, y, za):
    NT = W2 // P
    with ExitStack() as ctx:
        sb = lambda *args: kit.sbuf(ctx, *args)
        w_hi, w_lo = sb("o_w_hi", [P, 2 * NT, D], F32R), sb("o_w_lo", [P, 2 * NT, D], F32R)
        gate, gain, bias = (sb(f"o_{n}", [P, D]) for n in ("gate", "gain", "bias"))
        piece = [sb(f"o_piece{n}", [P, D]) for n in range(4)]
        junk = sb("o_junk", [P, W2], mybir.dt.bfloat16)
        ms = sb("o_mean_square", [P, 3, LT])
        ga = [sb(f"o_gated{n}", [P, W2]) for n in range(2)]
        hz = [sb(f"o_hz{n}", [P, NT, P]) for n in range(2)]
        x = [sb(f"o_x{n}", [P, D]) for n in range(2)]
        yh = [sb(f"o_y_hi{n}", [P, 2 * NT, P], F32R) for n in range(2)]
        yl = [sb(f"o_y_lo{n}", [P, 2 * NT, P], F32R) for n in range(2)]
        spare = sb("o_spare", [P, 1])
        bn, mv, st = sb("o_bn", [P, 2, 6]), sb("o_mv", [P, 2]), sb("o_st", [P, 2])
        psA, psR = (kit.psum(ctx, f"o_ps{n}", [P, 2, CH]) for n in "AR")
        psG = [kit.psum(ctx, f"o_psG{n}", [P, NT, P]) for n in range(2)]
        S = kit.sems("o_", ("rows_in", "scaled", "w_hi", "w_lo", "za", "sq", "root", "ya", "turn", "hi_r",
                            "hi_a", "lo_r", "lo_a", "prod", "res", "mv", "root2", "norm", "y"))
        p_in = [kit.sem(f"o_piece_loaded{n}") for n in range(4)]
        hz_in, x_in, out = ([kit.sem(f"o_{m}{n}") for n in range(2)] for m in ("hz_loaded", "x_loaded", "stored"))
        dve = Tally(kit.sem("o_dve_chain"))
        half = LT // 2

        def walk(eng, body, tally=None, per=0):
            for n in range(2):
                body(n, 0, n)
            with eng.Fori(1, half - 1) as i:
                if tally is None:
                    for n in range(2):
                        body(2 * i + n, i, n)
                else:
                    with tally.turn(i - 1, 2 * per, half - 2):
                        for n in range(2):
                            body(2 * i + n, i, n)
            for n in range(2):
                body(LT - 2 + n, half - 1, n)

        def late(t):
            return not isinstance(t, int) or t >= 2

        with nc.Block() as block:
            @block.sync
            def _(sp):
                for dst, src in ((gate[:], a["gate_rows"][:, D:2 * D]), (gain[:], a["ln_gain"].partition_broadcast(P)),
                                 (bias[:], a["ln_bias"].partition_broadcast(P))):
                    sp.dma_start(dst, src).then_inc(S["rows_in"], 16)
                for q in range(2 * NT):
                    if q >= 4:
                        sp.wait_ge(S["w_lo"], q - 3)
                    sp.dma_start(piece[q % 4][:], a["w_out_2"][:, q, :]).then_inc(p_in[q % 4], 16)

                def load(t, n):
                    sp.dma_start(hz[n][:], cols_at(a["hzT"], t)).then_inc(hz_in[n], 16)
                    sp.dma_start(x[n][:], rows_at(a["x1"], t)).then_inc(x_in[n], 16)

                load(0, 0)
                load(1, 1)

                def body(t, i, n):
                    sp.wait_ge(S["y"], t + 1)
                    sp.dma_start(rows_at(a["out"], t), x[n][:]).then_inc(out[n], 16)
                    if not isinstance(t, int) or t < LT - 2:
                        sp.wait_ge(out[n], 16 * (i + 1))
                        load(t + 2, n)
                walk(sp, body)
                for n in range(2):
                    sp.wait_ge(out[n], 16 * half)

            @block.gpsimd
            def _(g):
                def body(t, i, n):
                    g.wait_ge(S["norm"], t + 1)
                    g.tensor_tensor(x[n][:], x[n][:], bias[:], ALU.add).then_inc(S["y"], 1)
                g.wait_ge(S["rows_in"], 48)
                walk(g, body)

            @block.scalar
            def _(act):
                for q in range(2 * NT):
                    v_at = V2_NLRU + q
                    act.wait_ge(S["scaled"], q + 1)
                    act.activation(w_hi[:, q, :], piece[q % 4][:], ACT.Copy,
                                   scale=s.cols2[:, v_at:v_at + 1]).then_inc(S["w_hi"], 1)
                for t in range(LT):
                    ins = act.activation(junk[:], y[:, t, :], ACT.Square, accum_out=ms[:, 0, t:t + 1])
                    ins.then_inc(S["sq"], 1)
                    act.wait_ge(S["sq"], t + 1)
                for q in range(4):
                    act.activation(za[:, 4 * q:4 * q + 4, :], za[:, 4 * q:4 * q + 4, :], ACT.Silu).then_inc(S["za"], 1)
                act.activation(ms[:, 1, :], ms[:, 0, :], ACT.Sqrt, scale=1.0 / W2, bias=s.eps[:, 1:2]).then_inc(S["root"], 1)

                def highs(t, i, n):
                    act.wait_ge(hz_in[n], 16 * (i + 1))
                    if late(t):
                        act.wait_ge(S["prod"], 2 * (t - 1))
                    act.activation(yh[n][:, 0:NT, :], hz[n][:], ACT.Copy).then_inc(S["hi_r"], 1)
                    act.wait_ge(S["turn"], t + 1)
                    act.activation(yh[n][:, NT:2 * NT, :], psG[n][:], ACT.Copy).then_inc(S["hi_a"], 1)

                def body(t, i, n):
                    if not ends(t):
                        highs(t + 1, i + n, 1 - n)
                    act.wait_ge(S["mv"], t + 1)
                    act.activation(st[:, 0:1], mv[:, 1:2], ACT.Sqrt, bias=s.eps[:, 1:2]).then_inc(S["root2"], 1)
                highs(0, 0, 0)
                walk(act, body)

            @block.vector
            def _(v):
                def step(ins):
                    dve.mark(ins)
                    v.wait_ge(dve.sem, dve.value)

                v.wait_ge(S["rows_in"], 48)

                def scaled(q):
                    b = piece[q % 4]
                    v.wait_ge(p_in[q % 4], 16 * (q // 4 + 1))
                    v.tensor_tensor(b[:], b[:], gate[:], ALU.mult).then_inc(S["scaled"], 1)

                scaled(0)
                for q in range(2 * NT):
                    b, v_at = piece[q % 4], V2_NLRU + q
                    if q < 2 * NT - 1:
                        scaled(q + 1)
                    v.wait_ge(S["w_hi"], q + 1)
                    v.scalar_tensor_tensor(w_lo[:, q, :], b[:], s.cols2[:, v_at:v_at + 1], w_hi[:, q, :].bitcast(F32),
                                           ALU.mult, ALU.subtract).then_inc(S["w_lo"], 1)
                v.wait_ge(S["za"], 4)
                v.wait_ge(S["root"], 1)
                step(v.reciprocal(ms[:, 2, :], ms[:, 1, :]))

                def gated(t, n):
                    if late(t):
                        v.wait_ge(S["turn"], t - 1)
                    v.scalar_tensor_tensor(ga[n][:], y[:, t, :], ms[:, 2, t:t + 1] if isinstance(t, int) else ms[:, 2, bass.ds(t, 1)],
                                           za[:, t, :], ALU.mult, ALU.mult).then_inc(S["ya"], 1)

                def lows(t, i, n):
                    for m, (hi_ok, lo_ok, src) in enumerate(((S["hi_r"], S["lo_r"], hz[n]), (S["hi_a"], S["lo_a"], psG[n]))):
                        v.wait_ge(hi_ok, t + 1)
                        v.tensor_tensor(yl[n][:, m * NT:(m + 1) * NT, :], src[:],
                                        yh[n][:, m * NT:(m + 1) * NT, :].bitcast(F32), ALU.subtract).then_inc(lo_ok, 1)

                def body(t, i, n):
                    if not isinstance(t, int) or t < LT - 2:
                        gated(t + 2, n)
                    if not ends(t):
                        lows(t + 1, i + n, 1 - n)
                    v.wait_ge(x_in[n], 16 * (i + 1))
                    v.wait_ge(S["prod"], 2 * (t + 1))
                    step(v.scalar_tensor_tensor(x[n][:], x[n][:], ALPHA, psA[:].rearrange("p h c -> p (h c)"),
                                                ALU.mult, ALU.add))
                    r1 = s.rstd_r[:, t:t + 1] if isinstance(t, int) else s.rstd_r[:, bass.ds(t, 1)]
                    v.scalar_tensor_tensor(x[n][:], psR[:].rearrange("p h c -> p (h c)"), r1, x[n][:], ALU.mult,
                                           ALU.add).then_inc(S["res"], 1)
                    v.wait_ge(S["res"], t + 1)
                    v.bn_stats(bn[:, 0, :], x[n][:, 0:CH])
                    step(v.bn_stats(bn[:, 1, :], x[n][:, CH:D]))
                    v.memset(spare[:], 0.0)
                    v.bn_aggr(mv[:], bn[:].rearrange("p a b -> p (a b)")).then_inc(S["mv"], 1)
                    v.wait_ge(S["root2"], t + 1)
                    step(v.reciprocal(st[:, 1:2], st[:, 0:1]))
                    step(v.tensor_scalar(x[n][:], x[n][:], mv[:, 0:1], st[:, 1:2], ALU.subtract, ALU.mult))
                    v.tensor_tensor(x[n][:], x[n][:], gain[:], ALU.mult).then_inc(S["norm"], 1)

                gated(0, 0)
                gated(1, 1)
                lows(0, 0, 0)
                for n in range(2):
                    body(n, 0, n)
                with v.Fori(1, half - 1) as i:
                    with dve.turn(i - 1, 8, half - 2):
                        for n in range(2):
                            body(2 * i + n, i, n)
                for n in range(2):
                    body(LT - 2 + n, half - 1, n)

            @block.tensor
            def _(pe):
                def turn(t, n):
                    pe.wait_ge(S["ya"], t + 1)
                    if late(t):
                        pe.wait_ge(S["lo_a"], t - 1)
                    for q in range(NT):
                        mm = pe.transpose(psG[n][:, q, :], ga[n][:, q * P:(q + 1) * P], s.ident[:])
                    mm.then_inc(S["turn"], 1)

                def body(t, i, n):
                    if not ends(t):
                        turn(t + 1, 1 - n)
                    pe.wait_ge(S["lo_r"], t + 1)
                    pe.wait_ge(S["lo_a"], t + 1)
                    if not starts(t):
                        pe.wait_ge(S["res"], t)
                    for m, acc in enumerate((psR, psA)):
                        for h in range(2):
                            for q in range(m * NT, (m + 1) * NT):
                                for j, (yy, w) in enumerate(((yh, w_hi), (yh, w_lo), (yl, w_hi))):
                                    if starts(t) and j == 0:
                                        pe.wait_ge(S["w_lo"], q + 1)
                                    mm = pe.matmul(acc[:, h, :], yy[n][:, q, :], w[:, q, h * CH:(h + 1) * CH],
                                                   start=(q == m * NT and j == 0), stop=(q == (m + 1) * NT - 1 and j == 2))
                        mm.then_inc(S["prod"], 1)

                turn(0, 0)
                walk(pe, body)


def packed(inputs):
    i = {k: np.asarray(v) for k, v in inputs.items()}
    tiles = lambda v: np.ascontiguousarray(v.reshape(-1, P).T)

    def rows(w):
        return w.reshape(-1, P, w.shape[1]).transpose(1, 0, 2)

    def blocks(w, width):
        return np.ascontiguousarray(rows(w).reshape(P, -1, w.shape[1] // width, width).transpose(2, 0, 1, 3))

    w1, w2 = i["w_in"][0], i["w_in_2"][0]
    pad = lambda w: np.concatenate([w, np.zeros((w.shape[0], P - w.shape[1]), w.dtype)], 1)
    w_in = np.concatenate([w1[:, 3072:5120], pad(w1[:, 5120:]), w1[:, 2048:3072], w1[:, 1024:2048], w1[:, 0:1024]], 1)
    w_in_2 = np.concatenate([w2[:, :3072], pad(w2[:, 3072:])], 1)
    ada1, ada2 = i["w_ada"][0], i["w_ada_2"][0]
    wada = np.concatenate([ada1[:, :2 * D], ada2[:, :2 * D], ada1[:, 2 * D:], ada2[:, 2 * D:]], 1)
    c3 = np.stack([i["c"][0], i["c_ctx"], i["c_2"][0]], 1)
    cols1 = np.concatenate([tiles(v) for v in (i["b_ada"][0], i["norm_w"][0], i["conv_b"][0], i["conv_w"][0],
                                               i["pool_scale"][0], i["ssd_norm_w"][0])], 1)
    cols2 = np.concatenate([tiles(v) for v in (i["b_ada_2"][0], i["conv_w_2"][0], i["conv_b_2"][0],
                                               i["b_gate_a_2"][0], i["b_gate_x_2"][0], i["lru_lambda_2"][0],
                                               i["norm_lru_2"][0], i["norm_attn_2"][0])], 1)
    f = np.float32
    r = np.arange(P)
    def inv_count(n, w):
        t = np.arange(n)
        return 1.0 / (np.minimum(t + w - w // 2, n) - np.maximum(t - w // 2, 0))
    inv = np.stack([np.outer(inv_count(GRID_R, w), inv_count(GRID_C, w)).reshape(-1) for w in WINDOWS]).astype(f)
    upper = (r[:, None] <= r[None, :]).astype(f)
    return {
        "x": i["x"][0], "ctx": i["ctx"][0], "cols1": cols1, "cols2": cols2, "ident": np.eye(P, dtype=f),
        "c3": np.ascontiguousarray(c3.reshape(KT, P, 3).transpose(1, 0, 2)),
        "wada": blocks(wada, 256), "gate_bias": np.concatenate([i["b_ada"][0, 2 * D:], i["b_ada_2"][0, 2 * D:]]).reshape(8, 256),
        "w_in": blocks(w_in, P), "w_in_2": blocks(w_in_2, P), "inv_count": inv,
        "sel_last": np.outer(r == P - 1, np.ones(P)).astype(f), "sel_first": np.outer(r == 0, np.ones(P)).astype(f),
        "keep_fwd": np.tile((np.arange(TOK) % P != 0).astype(f), (HEADS, 1)),
        "keep_bwd": np.tile((np.arange(TOK) % P != P - 1).astype(f), (HEADS, 1)),
        "upper": upper, "lower": np.ascontiguousarray(upper.T),
        "causal": ((upper.T - 1) * 1e30).astype(f),
        "seg_r": np.concatenate([np.zeros((2, NDH * P)), 
                                 np.tile(-1.0 * (np.arange(NDH * P) // P % 4 == np.arange(4)[:, None]), (2, 1))]).astype(f),
        "seg_l": np.ones((10, 8, P), f),
        "causal_turned": np.ascontiguousarray(((upper - 1) * 1e30).astype(f)),
        "dt_bias": i["dt_bias"][0].reshape(1, NDH), "a_log": i["a_log"][0].reshape(1, NDH),
        "d_skip": i["d_skip"][0].reshape(1, HEADS),
        "pool_w": np.ascontiguousarray(i["pool_w"][0].reshape(4, 2, P, 256).transpose(2, 0, 1, 3)),
        "w_out": np.ascontiguousarray(rows(i["w_out"][0])), "final_norm": i["final_norm_w"].reshape(1, D),
        "b_fgate": np.repeat(i["b_fgate_2"][0], P // NH2).reshape(P, 1),
        "w_gate_a": i["w_gate_a_2"][0], "w_gate_x": i["w_gate_x_2"][0],
        "w_out_2": np.ascontiguousarray(rows(i["w_out_2"][0])),
        "ln_gain": i["ln_gain_2"][0].reshape(1, D), "ln_bias": i["ln_bias_2"][0].reshape(1, D),
    }


SCRATCH = {"gate_rows": [P, 2 * D],
           "xs_tok": [TOK, W_HALF], "b_tok": [TOK, GROUPS * NS], "z_tok": [SEQ, W_HALF], "dt_tok": [TOK, NDH],
           "bT": [4, P, SEQ], "cT": [4, P, SEQ], "zpT": [8, P, SEQ], "dT": [8, P, SEQ],
           "acum_rows": [2, TT, NDH, P], "g_tok": [SEQ, W_HALF],
           "x1": [SEQ, D], "h2T": [KT, P, SEQ],
           "xcT": [4, P, SEQ], "zrT": [4, P, SEQ], "qkT": [8, P, SEQ], "va_tok": [SEQ, 2 * W2], "flT": [1, NH2, SEQ],
           "softf": [P, P], "forget": [NH2, 2, SEQ], "hzT": [4, P, SEQ]}


def tables(nc, kit, a, s):
    ok = kit.sem("tables_loaded")
    with nc.Block() as block:
        @block.sync
        def _(sp):
            for dst, src in ((s.cols1, a["cols1"]), (s.cols2, a["cols2"]), (s.ident, a["ident"])):
                sp.dma_start(dst[:], src).then_inc(ok, 16)
            sp.wait_ge(ok, 48)

        @block.vector
        def _(v):
            v.memset(s.eps[:, 0:1], EPS)
            v.memset(s.eps[:, 1:2], LN_EPS)


def program(nc, a):
    kit, s = Kit(nc), Names()
    with ExitStack() as keep:
        s.cols1, s.cols2 = kit.sbuf(keep, "cols1", [P, P]), kit.sbuf(keep, "cols2", [P, 64])
        s.ident = kit.sbuf(keep, "ident", [P, P])
        s.eps = kit.sbuf(keep, "eps", [P, 2])
        s.mod2 = kit.sbuf(keep, "mod2", [P, 2, KT])
        s.rstd_r = kit.sbuf(keep, "rstd_r", [P, LT])
        tables(nc, kit, a, s)
        with ExitStack() as proj:
            hmT = (kit.sbuf(proj, "hmT_hi", [P, KT, TOK], F32R), kit.sbuf(proj, "hmT_lo", [P, KT, TOK], F32R))
            modulation(nc, kit, a, s, hmT)
            projection(nc, kit, a, s, hmT)
        kit.end_phase()
        ssd(nc, kit, a, s)
        mix_out(nc, kit, a, s)
        kit.end_phase()
        projection2(nc, kit, a, s)
        lru(nc, kit, a, s)
        with ExitStack() as att:
            y, za = (kit.sbuf(att, n, [P, LT, W2]) for n in ("att_y", "att_za"))
            forget_sums(nc, kit, a, s)
            attention(nc, kit, a, s, y, za)
            out2(nc, kit, a, s, y, za)


def kernel(**inputs):
    import concourse.bacc as bacc
    from concourse.bass_utils import run_bass_kernel_spmd

    arrays = packed(inputs)
    nc = bacc.Bacc("TRN2", target_bir_lowering=False, num_devices=1)
    a = {name: nc.dram_tensor(f"in_{name}", v.shape, mybir.dt.from_np(v.dtype), kind="ExternalInput").ap()
         for name, v in arrays.items()}
    for name, shape in SCRATCH.items():
        a[name] = nc.dram_tensor(f"scratch_{name}", shape, F32, kind="Internal").ap()
    a["out"] = nc.dram_tensor("out", [SEQ, D], F32, kind="ExternalOutput").ap()
    program(nc, a)
    r = run_bass_kernel_spmd(nc, [{f"in_{k}": v for k, v in arrays.items()}], core_ids=[0])
    return r.results[0]["out"].reshape(1, SEQ, D)
```
